# Optimizing a Trainium2 kernel written in Bass

```python
import math
import jax
import jax.numpy as jnp
from jax import lax
import numpy as np

D_MODEL = 1024
BATCH = 1
SEQ = 512
DEPTH = 2

RMS_EPS = 1e-6
L2_EPS = 1e-6
CHUNK = 64
CONV_K = 4

GDN_HEADS = 4
GDN_DK = 128
GDN_DV = 128
HGRN_HEADS = 4
HGRN_DK = 128
HGRN_DV = 128
RET_HEADS = 4
RET_DK = D_MODEL // RET_HEADS
RET_DV = 2 * RET_DK
ROPE_BASE = 10000.0
N_GROUPS = 4
EXPERTS_PER_GROUP = 4
N_EXPERTS = N_GROUPS * EXPERTS_PER_GROUP
D_EXPERT = 256
TOP_K_INNER = 2

N_EVEN = (DEPTH + 1) // 2
N_ODD = DEPTH // 2

GDN_QK_W = GDN_HEADS * GDN_DK
GDN_V_W = GDN_HEADS * GDN_DV
GDN_CONV_W = 2 * GDN_QK_W + GDN_V_W
HGRN_K_W = HGRN_HEADS * HGRN_DK
HGRN_V_W = HGRN_HEADS * HGRN_DV
EVEN_SPLITS = (GDN_CONV_W, GDN_V_W, GDN_HEADS, GDN_HEADS, HGRN_K_W, HGRN_K_W, HGRN_V_W, HGRN_V_W)
EVEN_IN = sum(EVEN_SPLITS)
EVEN_MIX_W = GDN_V_W + HGRN_V_W
RET_QK_W = RET_HEADS * RET_DK
RET_V_W = RET_HEADS * RET_DV
ODD_SPLITS = (RET_QK_W, RET_QK_W, RET_V_W, RET_V_W)
ODD_IN = sum(ODD_SPLITS)
ODD_MIX_W = RET_V_W

kernel_name = 'hybrid_gdn_hgrn2_retnet_hmoe'

def rms_norm(x, w):
    xf = x.astype(jnp.float32)
    xf = xf * lax.rsqrt(jnp.mean(xf * xf, axis=-1, keepdims=True) + RMS_EPS)
    return (xf * w.astype(jnp.float32)).astype(x.dtype)

def l2_normalize(x):
    xf = x.astype(jnp.float32)
    return (xf * lax.rsqrt(jnp.sum(xf * xf, axis=-1, keepdims=True) + L2_EPS)).astype(x.dtype)

def split_heads(x, n_heads):
    b, t, c = x.shape
    return x.reshape(b, t, n_heads, c // n_heads).transpose(0, 2, 1, 3)

def merge_heads(x):
    b, h, t, d = x.shape
    return x.transpose(0, 2, 1, 3).reshape(b, t, h * d)

def split_cols(p, sizes):
    idx = [int(i) for i in np.cumsum(sizes)[:-1]]
    return jnp.split(p, idx, axis=-1)

def to_chunks(x):
    b, h, t = x.shape[:3]
    x = x.reshape((b, h, t // CHUNK, CHUNK) + x.shape[3:])
    return jnp.moveaxis(x, 2, 0)

def from_chunks(y):
    n, b, h, c, d = y.shape
    return jnp.moveaxis(y, 0, 2).reshape(b, h, n * c, d)

def causal_short_conv(x, w):
    t = x.shape[1]
    xp = jnp.pad(x, ((0, 0), (CONV_K - 1, 0), (0, 0)))
    return sum(xp[:, j:j + t] * w[j] for j in range(CONV_K))

def rotary(x):
    t, d = x.shape[2], x.shape[3]
    inv = 1.0 / (ROPE_BASE ** jnp.linspace(0.0, 1.0, d // 2, dtype=jnp.float32))
    ang = jnp.arange(t, dtype=jnp.float32)[:, None] * inv[None, :]
    cos = jnp.cos(ang).astype(x.dtype)
    sin = jnp.sin(ang).astype(x.dtype)
    x1, x2 = x[..., 0::2], x[..., 1::2]
    return jnp.stack([x1 * cos - x2 * sin, x1 * sin + x2 * cos], axis=-1).reshape(x.shape)

def gated_delta_rule(q, k, v, beta, g):
    f32 = jnp.float32
    dk, dv = q.shape[-1], v.shape[-1]
    qc = to_chunks(q.astype(f32) * dk ** -0.5)
    kc = to_chunks(k.astype(f32))
    vc = to_chunks(v.astype(f32))
    bc = to_chunks(beta.astype(f32))[..., None]
    gc = jnp.cumsum(to_chunks(g.astype(f32)), axis=-1)
    causal = jnp.tril(jnp.ones((CHUNK, CHUNK), bool))
    decay = jnp.exp(jnp.where(causal, gc[..., :, None] - gc[..., None, :], -jnp.inf))
    a = jnp.tril(jnp.einsum('nbhid,nbhjd->nbhij', kc * bc, kc) * decay, -1)
    rhs = jnp.concatenate([vc * bc, kc * bc * jnp.exp(gc)[..., None]], axis=-1)
    sol = lax.linalg.triangular_solve(a, rhs, left_side=True, lower=True, unit_diagonal=True)
    u, w = sol[..., :dv], sol[..., dv:]

    def step(state, inp):
        q_i, k_i, u_i, w_i, g_i, d_i = inp
        v_new = u_i - jnp.einsum('bhck,bhkv->bhcv', w_i, state)
        attn = jnp.einsum('bhik,bhjk->bhij', q_i, k_i) * d_i
        o = (jnp.einsum('bhck,bhkv->bhcv', q_i * jnp.exp(g_i)[..., None], state)
             + jnp.einsum('bhij,bhjv->bhiv', attn, v_new))
        g_last = g_i[..., -1:]
        k_dec = k_i * jnp.exp(g_last - g_i)[..., None]
        state = state * jnp.exp(g_last)[..., None] + jnp.einsum('bhck,bhcv->bhkv', k_dec, v_new)
        return state, o

    s0 = jnp.zeros(qc.shape[1:3] + (dk, dv), f32)
    _, o = lax.scan(step, s0, (qc, kc, u, w, gc, decay))
    return from_chunks(o).astype(v.dtype)

def hgrn2_recurrence(q, k, i, log_f):
    f32 = jnp.float32
    dk, dv = q.shape[-1], i.shape[-1]
    qc = to_chunks(q.astype(f32) * dk ** -0.5)
    kc = to_chunks(k.astype(f32))
    ic = to_chunks(i.astype(f32))
    bc = jnp.cumsum(to_chunks(log_f.astype(f32)), axis=-2)
    causal = jnp.tril(jnp.ones((CHUNK, CHUNK), bool))[:, :, None]

    def step(state, inp):
        q_i, k_i, i_i, b_i = inp
        dmat = jnp.exp(jnp.where(causal, b_i[:, :, :, None, :] - b_i[:, :, None, :, :], -jnp.inf))
        attn = jnp.einsum('bhtk,bhsk,bhtsk->bhts', q_i, k_i, dmat)
        o = (jnp.einsum('bhtk,bhkv->bhtv', q_i * jnp.exp(b_i), state)
             + jnp.einsum('bhts,bhsv->bhtv', attn, i_i))
        b_last = b_i[:, :, -1:, :]
        state = (state * jnp.exp(b_last[:, :, 0, :])[..., None]
                 + jnp.einsum('bhsk,bhsv->bhkv', k_i * jnp.exp(b_last - b_i), i_i))
        return state, o

    s0 = jnp.zeros(qc.shape[1:3] + (dk, dv), f32)
    _, o = lax.scan(step, s0, (qc, kc, ic, bc))
    return from_chunks(o).astype(i.dtype)

def multiscale_retention(q, k, v):
    f32 = jnp.float32
    n_heads, dk, dv = q.shape[1], q.shape[-1], v.shape[-1]
    log_gamma = jnp.log(1.0 - 2.0 ** (-5.0 - jnp.arange(n_heads, dtype=f32)))
    pos = jnp.arange(CHUNK, dtype=f32)
    rel = pos[:, None] - pos[None, :]
    intra = jnp.where(rel >= 0, jnp.exp(jnp.maximum(rel, 0.0) * log_gamma[:, None, None]), 0.0)
    q_decay = jnp.exp((pos + 1.0) * log_gamma[:, None])[:, :, None]
    k_decay = jnp.exp((CHUNK - 1.0 - pos) * log_gamma[:, None])[:, :, None]
    chunk_decay = jnp.exp(CHUNK * log_gamma)[:, None, None]
    qc = to_chunks(q.astype(f32))
    kc = to_chunks(k.astype(f32) * dk ** -0.5)
    vc = to_chunks(v.astype(f32))

    def step(state, inp):
        q_i, k_i, v_i = inp
        attn = jnp.einsum('bhik,bhjk->bhij', q_i, k_i) * intra
        o = (jnp.einsum('bhck,bhkv->bhcv', q_i, state) * q_decay
             + jnp.einsum('bhij,bhjv->bhiv', attn, v_i))
        state = state * chunk_decay + jnp.einsum('bhck,bhcv->bhkv', k_i * k_decay, v_i)
        return state, o

    s0 = jnp.zeros(qc.shape[1:3] + (dk, dv), f32)
    _, o = lax.scan(step, s0, (qc, kc, vc))
    return from_chunks(o).astype(v.dtype)

def even_mixer(h, w_in, conv_w, a_log, dt_bias, gdn_norm_w, lower_bound, hgrn_norm_w, w_out):
    f32 = jnp.float32
    g_qkv, g_z, g_b, g_a, h_q, h_f, h_i, h_g = split_cols(h @ w_in, EVEN_SPLITS)
    qkv = jax.nn.silu(causal_short_conv(g_qkv, conv_w))
    q, k, v = split_cols(qkv, (GDN_QK_W, GDN_QK_W, GDN_V_W))
    q = l2_normalize(split_heads(q, GDN_HEADS))
    k = l2_normalize(split_heads(k, GDN_HEADS))
    v = split_heads(v, GDN_HEADS)
    beta = jax.nn.sigmoid(g_b.astype(f32)).transpose(0, 2, 1)
    g = (-jnp.exp(a_log.astype(f32)) * jax.nn.softplus(g_a.astype(f32) + dt_bias.astype(f32))).transpose(0, 2, 1)
    o_a = gated_delta_rule(q, k, v, beta, g)
    o_a = rms_norm(o_a, gdn_norm_w) * jax.nn.silu(split_heads(g_z, GDN_HEADS))
    f_gate = lower_bound + (1.0 - lower_bound) * jax.nn.sigmoid(h_f.astype(f32))
    o_b = hgrn2_recurrence(split_heads(jax.nn.silu(h_q), HGRN_HEADS),
                           split_heads((1.0 - f_gate).astype(h.dtype), HGRN_HEADS),
                           split_heads(h_i, HGRN_HEADS),
                           split_heads(jnp.log(f_gate), HGRN_HEADS))
    o_b = rms_norm(o_b, hgrn_norm_w) * jax.nn.silu(split_heads(h_g, HGRN_HEADS))
    return jnp.concatenate([merge_heads(o_a), merge_heads(o_b)], axis=-1) @ w_out

def retention_mixer(h, w_in, norm_w, w_out):
    q, k, v, g = split_cols(h @ w_in, ODD_SPLITS)
    q = rotary(split_heads(q, RET_HEADS))
    k = rotary(split_heads(k, RET_HEADS))
    o = multiscale_retention(q, k, split_heads(v, RET_HEADS))
    o = rms_norm(o, norm_w) * jax.nn.silu(split_heads(g, RET_HEADS))
    return merge_heads(o) @ w_out

def hierarchical_moe(h, wc, bc, wf, bf, w_gate_up, w_down):
    b, t, d = h.shape
    xt = h.reshape(b * t, d)
    n = xt.shape[0]
    coarse_prob = jax.nn.softmax((xt @ wc + bc).astype(jnp.float32), axis=-1)
    g_prob, g_idx = lax.top_k(coarse_prob, 1)
    fine_logits = (xt @ wf + bf).astype(jnp.float32).reshape(n, N_GROUPS, EXPERTS_PER_GROUP)
    fine_sel = jnp.take_along_axis(fine_logits, g_idx[:, :, None], axis=1)[:, 0]
    e_logit, e_idx = lax.top_k(fine_sel, TOP_K_INNER)
    e_w = jax.nn.softmax(e_logit, axis=-1) * g_prob
    expert_id = g_idx * EXPERTS_PER_GROUP + e_idx
    gates = jnp.sum(jax.nn.one_hot(expert_id, N_EXPERTS, dtype=jnp.float32) * e_w[..., None], axis=1)
    gu = jnp.einsum('nd,edf->nef', xt, w_gate_up)
    gate, up = jnp.split(gu, 2, axis=-1)
    act = jax.nn.silu(gate) * up * gates.astype(h.dtype)[..., None]
    return jnp.einsum('nef,efd->nd', act, w_down).reshape(b, t, d)

def setup_inputs(seed: int = 0) -> dict:
    key = jax.random.key(seed)
    ks = jax.random.split(key, 24)
    f32 = jnp.float32

    def normal(k, shape, scale):
        return scale * jax.random.normal(k, shape, f32)

    def gain(k, shape):
        return 1.0 + 0.02 * jax.random.normal(k, shape, f32)

    dt = jnp.exp(jax.random.uniform(ks[6], (N_EVEN, GDN_HEADS), f32, math.log(1e-3), math.log(1e-1)))
    return {
        'x': normal(ks[0], (BATCH, SEQ, D_MODEL), 1.0),
        'norm_mix_w': gain(ks[1], (DEPTH, D_MODEL)),
        'norm_ffn_w': gain(ks[2], (DEPTH, D_MODEL)),
        'even_w_in': normal(ks[3], (N_EVEN, D_MODEL, EVEN_IN), D_MODEL ** -0.5),
        'gdn_conv_w': normal(ks[4], (N_EVEN, CONV_K, GDN_CONV_W), CONV_K ** -0.5),
        'gdn_a_log': jnp.log(jax.random.uniform(ks[5], (N_EVEN, GDN_HEADS), f32, 1.0, 16.0)),
        'gdn_dt_bias': dt + jnp.log(-jnp.expm1(-dt)),
        'gdn_norm_w': gain(ks[7], (N_EVEN, GDN_DV)),
        'hgrn_lb_logits': normal(ks[8], (DEPTH + 1, HGRN_K_W), 0.1),
        'hgrn_norm_w': gain(ks[9], (N_EVEN, HGRN_DV)),
        'even_w_out': normal(ks[10], (N_EVEN, EVEN_MIX_W, D_MODEL), EVEN_MIX_W ** -0.5),
        'odd_w_in': normal(ks[11], (N_ODD, D_MODEL, ODD_IN), D_MODEL ** -0.5),
        'ret_norm_w': gain(ks[12], (N_ODD, RET_DV)),
        'odd_w_out': normal(ks[13], (N_ODD, ODD_MIX_W, D_MODEL), ODD_MIX_W ** -0.5),
        'router_c_w': normal(ks[14], (DEPTH, D_MODEL, N_GROUPS), D_MODEL ** -0.5),
        'router_c_b': normal(ks[15], (DEPTH, N_GROUPS), 0.01),
        'router_f_w': normal(ks[16], (DEPTH, D_MODEL, N_EXPERTS), D_MODEL ** -0.5),
        'router_f_b': normal(ks[17], (DEPTH, N_EXPERTS), 0.01),
        'moe_w_gate_up': normal(ks[18], (DEPTH, N_EXPERTS, D_MODEL, 2 * D_EXPERT), D_MODEL ** -0.5),
        'moe_w_down': normal(ks[19], (DEPTH, N_EXPERTS, D_EXPERT, D_MODEL), D_EXPERT ** -0.5),
        'final_norm_w': gain(ks[20], (D_MODEL,)),
    }

def reference(x, norm_mix_w, norm_ffn_w, even_w_in, gdn_conv_w, gdn_a_log, gdn_dt_bias, gdn_norm_w,
              hgrn_lb_logits, hgrn_norm_w, even_w_out, odd_w_in, ret_norm_w, odd_w_out,
              router_c_w, router_c_b, router_f_w, router_f_b, moe_w_gate_up, moe_w_down, final_norm_w):
    lower_bounds = jnp.cumsum(jax.nn.softmax(hgrn_lb_logits.astype(jnp.float32), axis=0), axis=0)
    for layer in range(DEPTH):
        j = layer // 2
        h = rms_norm(x, norm_mix_w[layer])
        if layer % 2 == 0:
            mix = even_mixer(h, even_w_in[j], gdn_conv_w[j], gdn_a_log[j], gdn_dt_bias[j], gdn_norm_w[j],
                             lower_bounds[layer], hgrn_norm_w[j], even_w_out[j])
        else:
            mix = retention_mixer(h, odd_w_in[j], ret_norm_w[j], odd_w_out[j])
        x = x + mix
        h = rms_norm(x, norm_ffn_w[layer])
        x = x + hierarchical_moe(h, router_c_w[layer], router_c_b[layer], router_f_w[layer], router_f_b[layer],
                                 moe_w_gate_up[layer], moe_w_down[layer])
    return rms_norm(x, final_norm_w)


_drawn_inputs = setup_inputs


def setup_inputs(seed=0):
    import zlib

    import numpy as np

    out = dict(_drawn_inputs(seed))
    spreads = {}
    factors = {'hgrn_lb_logits': 8.0,
     'ret_norm_w': 4.38,
     'router_c_b': 4.778,
     'router_f_b': 4.415,
     'final_norm_w': 2.957}
    for name, (base, spread) in spreads.items():
        noise = np.random.default_rng([zlib.crc32(name.encode()), seed]).standard_normal(out[name].shape)
        drawn = base * np.exp(spread * noise) if base else spread * noise
        out[name] = jnp.asarray(drawn.astype(out[name].dtype))
    for name, factor in factors.items():
        out[name] = (out[name] * factor).astype(out[name].dtype)
    return out
```

```python
from contextlib import ExitStack

import concourse.bass as bass
from concourse import mybir
import numpy as np

F32 = mybir.dt.float32
F32R = mybir.dt.float32r
I32 = mybir.dt.int32
I8 = mybir.dt.int8
U32 = mybir.dt.uint32
ALU = mybir.AluOpType
ACT = mybir.ActivationFunctionType
AX = mybir.AxisListType

P = 128
SEQ = 512
DM = 1024
NT = SEQ // P
KD = DM // P
NH = 4
DK = 128
CH = 64
NC = SEQ // CH
RDV = 512
RDK = 256
NE = 16
NG = 4
EPG = 4
FE = 256
EPS = 1e-6
NRAW = 6
NSPL = 4
SLOT_TILES = NE + 7
EMPTY = 4096.0
LEVELS = (32, 16, 8, 4, 2, 1)

EVEN_COL = {"q": 0, "k": 512, "v": 1024, "z": 1536, "hq": 2056, "hf": 2568, "hi": 3080, "hg": 3592}
BLOCKS = [("even_in", n, EVEN_COL[n]) for n in ("q", "k", "v", "hf", "hq", "hi", "z", "hg")]
BLOCKS += [("even_out", 0, 0), ("even_out", 0, 512)]
for pair in range(2):
    BLOCKS += [("odd_in", ("rq", pair), 512 * pair), ("odd_in", ("rk", pair), 1024 + 512 * pair),
               ("odd_in", ("rv", 2 * pair), 2048 + 1024 * pair), ("odd_in", ("rv", 2 * pair + 1), 2560 + 1024 * pair),
               ("odd_in", ("rg", 2 * pair), 4096 + 1024 * pair), ("odd_in", ("rg", 2 * pair + 1), 4608 + 1024 * pair)]
BLOCKS += [("odd_out", kh, c) for kh in range(2) for c in (0, 512)]
MOE_AT = (10, 26)
MOE_PIECE = (4 * 10, 4 * 26 + 6 * NE)
NPIECE = 4 * len(BLOCKS) + 12 * NE + 4


def first_piece(db):
    return 4 * db + (6 * NE if db >= MOE_AT[0] else 0)


def rot_index(db):
    return [b for b, (_, w, _) in enumerate(BLOCKS) if isinstance(w, tuple) and w[0] in ("rq", "rk")].index(db)


def evac_engine(db):
    return "dve" if BLOCKS[db][0].endswith("out") else "act"


def evac_count(db, t):
    return 4 * sum(evac_engine(b) == evac_engine(db) for b in range(db)) + t + 1


def lo_by_dve(i):
    return any(m + 4 <= i < m + 6 * NE + 4 for m in MOE_PIECE)


def lo_count(i):
    return sum(lo_by_dve(j) == lo_by_dve(i) for j in range(i + 1)) + 4 * lo_by_dve(i)


def schedule():
    s = [("consts",), ("norm", 0), ("ba",)]

    def block(db, side=((), (), (), ())):
        for kp in range(4):
            s.append(("piece", db, kp))
            s.extend(side[kp])
        s.append(("evac", db))

    block(0)
    block(1)
    block(2, ([("tok", "q", T) for T in range(NT)], [("gates",)], [("tok", "k", T) for T in range(NT)], ()))
    s.extend(("tok", "v", T) for T in range(NT))
    s.append(("l2",))
    for pr in range(2):
        s.append(("gdn_chunks", pr))
    scan = [[("scan", c)] for c in range(NC)]
    block(3, ((), scan[0], scan[1], scan[2]))
    block(4, ((), scan[3], scan[4], scan[5]))
    block(5, ((), scan[6], scan[7], [("onorm", 0)]))
    block(6, ((), [("hdiag",)], [("hlevel", 0)], [("hlevel", 1)]))
    block(7, ([("hlevel", 2)], [("hlevel", 3)], [("hlevel", 4)], [("hlevel", 5)]))
    evac7 = s.pop()
    s.append(("hstate",))
    s.extend(("hscan", c) for c in range(NC))
    s.append(("onorm", 1))
    s.append(evac7)
    s.append(("yT", 0, 0))
    block(8)
    block(9)
    s.append(("norm", 1))
    s.append(("moe", 0))
    s.append(("norm", 2))
    for pair in range(2):
        b = 10 + 6 * pair
        h0, h1 = 2 * pair, 2 * pair + 1
        block(b)
        block(b + 1)
        block(b + 2)
        block(b + 3, ((), [("score", h0)], [("ro", h0)], ()))
        block(b + 4, ((), [("score", h1)], (), ()))
        s.append(("ro", h1))
        block(b + 5)
    for kh in range(2):
        s.append(("yT", 1, kh))
        block(22 + 2 * kh)
        block(23 + 2 * kh)
    s.append(("norm", 3))
    s.append(("moe", 1))
    s.append(("norm", 4))
    return s


def side_tiles(step):
    k = step[0]
    if k == "consts":
        return [("vec", "dve")]
    if k == "norm" and step[1] < 4:
        who = "act" if step[1] in (1, 3) else "dve"
        return [(("hT", step[1], T, g), who) for T in range(NT) for g in range(2)]
    if k == "yT":
        return [(("yT", step[1], step[2], T, g), "dve") for T in range(NT) for g in range(2)]
    if k == "ba":
        return [("ba", "dve")]
    if k == "tok":
        return [(("tok", step[1], step[2]), "act")]
    if k == "gates":
        return [("gc", "dve")]
    if k == "l2":
        return [((n, T), "act" if n == "qb" else "dve") for T in range(NT) for n in ("qb", "kb")]
    if k == "gdn_chunks":
        Ts = (2 * step[1], 2 * step[1] + 1)
        out = []
        for T in Ts:
            out += [(("Gb", T), "act"), (("KK", T), "dve"), (("KQ", T), "dve"), (("DT", T), "act")]
        for T in Ts:
            out += [(("P2", T), "act"), (("P2T", T), "act")]
        for r in (1, 2):
            for T in Ts:
                out += [(("X", r, T), "dve"), (("XT", r, T), "dve"), (("PT", r, T), "act")]
                if r == 1:
                    out += [(("P", r, T), "act")]
        for T in Ts:
            out += [(("X", 3, T), "dve"), (("XT", 3, T), "dve")]
        for T in Ts:
            out += [(("B", T), "act"), (("BT", T), "act")]
        for T in Ts:
            out += [(("B2", T), "act")]
        for T in Ts:
            out += [(("N2", T), "dve")]
        for T in Ts:
            out += [(("IT", T), "act")]
        for T in Ts:
            out += [(("u", T), "act"), (("wT", T), "act")]
        return out
    if k == "scan":
        c = step[1]
        return [(("sv", c), "dve"), (("so", c), "act"), (("ss", c), "dve")]
    if k == "hdiag":
        return [(("dg", T), "dve") for T in range(NT)]
    if k == "hlevel":
        return [(("lv", step[1], T), "dve") for T in range(NT)]
    if k == "hstate":
        return [(("kd", T), "act") for T in range(NT)]
    if k == "hscan":
        return [(("ho", step[1]), "act"), (("hs", step[1]), "dve")]
    if k == "score":
        return [(("sc", step[1], J), "dve") for J in range(NT)]
    if k == "ro":
        return [(("ro", step[1], T), "act") for T in range(NT)]
    return []


SCHEDULE = schedule()
SIDE = [t for st in SCHEDULE for t in side_tiles(st)]
SIDE_AT = {name: n for n, (name, _) in enumerate(SIDE)}
SIDE_READ = {}
for _n, (_name, _who) in enumerate(SIDE):
    SIDE_READ[_name] = sum(w == _who for _, w in SIDE[:_n + 1])


def build(nc, a, out):
    ctx = ExitStack()
    with ctx:
        def sb(name, shape, dt=F32):
            return ctx.enter_context(nc.sbuf_tensor(name, shape, dt))

        def sem(name):
            return ctx.enter_context(nc.semaphore(name))

        hs_dram = [nc.dram_tensor(f"hs{l}", (SEQ, DM), F32, kind="Internal").ap() for l in range(2)]
        y2_dram = [nc.dram_tensor(f"y2{l}", (2 * SEQ, DM), F32, kind="Internal").ap() for l in range(2)]
        slot_dram = [nc.dram_tensor(f"slots{l}", (SLOT_TILES * P, 1), F32, kind="Internal").ap() for l in range(2)]

        raw = sb("raw", [P, NRAW, 2, 512])
        wh = sb("wh", [P, NSPL, 2, 512], F32R)
        wl = sb("wl", [P, NSPL, 2, 512], F32R)
        X = sb("x", [P, NT, DM])
        HTH = sb("hT_hi", [P, KD, SEQ], F32R)
        HTL = sb("hT_lo", [P, KD, SEQ], F32R)
        ident = sb("ident", [P, P])
        U = sb("cum_upper", [P, P])
        m16 = sb("mask16", [P, P])
        moff = sb("mask_off", [P, P])
        lvmask = sb("level_masks", [P, len(LEVELS), P], I8)
        resetm = sb("reset", [P, SEQ])
        vec = sb("vec", [P, 60])
        small = sb("small", [P, 420])
        wba_h = sb("wba_hi", [P, KD, 8], F32R)
        wba_l = sb("wba_lo", [P, KD, 8], F32R)
        S = sb("state", [P, 512])
        Stmp = sb("state_decayed", [P, 512])
        vnew = sb("vnew", [P, 512])
        gnw = sb("gdn_w", [P, P])
        hnw = sb("hgrn_w", [P, P])
        ar = sb("arena", [P, 22528])
        idx = sb("slot_rows", [P, 2, SLOT_TILES], I32)
        cur = sb("cur_rows", [P, 4], U32)
        eid = sb("overflow_expert", [1, 8], I32)
        ps = ctx.enter_context(nc.psum_tensor("ps", [P, 8, 512], F32))

        def reg(off, n):
            return ar[:, off:off + n]

        def v3(ap, k):
            return ap.rearrange("p (k n) -> p k n", k=k)

        ss = small[:, 0:4]
        ms = small[:, 4:8]
        rs = small[:, 8:12]
        mhalf = small[:, 12:44]
        ba = v3(small[:, 44:76], 4)
        beta = small[:, 76:92]
        gg = small[:, 92:108]
        gc = small[:, 108:124]
        egc = small[:, 124:140]
        bege = small[:, 140:156]
        kde = small[:, 156:172]
        egl = v3(small[:, 172:204], 8)
        dtb = small[:, 204:208]
        alog = small[:, 208:212]
        ssn = small[:, 212:244]
        rn = small[:, 244:276]
        lbt = small[:, 276:300]
        c1 = small[:, 300:304]
        c2 = small[:, 304:308]
        zsp = small[:, 308:324]
        esp = small[:, 324:340]
        spt = small[:, 340:356]
        oss = small[:, 356:372]
        ors = small[:, 372:388]
        lbs = small[:, 388:404]

        QF, KF, VF = (v3(reg(2048 * n, 2048), 4) for n in range(3))
        KT, VT = (v3(reg(2048 * n, 2048), 4) for n in (3, 4))
        AT0 = v3(reg(4096, 2048), 4)
        Y0 = v3(reg(10240, 4096), 4)
        craw = v3(reg(14336, 1024), 2)
        sqt = v3(reg(15360, 1024), 2)
        HQ, HB, HK = (v3(reg(14336 + 2048 * n, 2048), 4) for n in range(3))
        HI = v3(reg(20480, 2048), 4)
        zt = v3(reg(6144, 1024), 2)
        PA = [v3(reg(14336 + 1024 * n, 1024), 2) for n in range(8)] + \
             [v3(reg(10240 + 1024 * n, 1024), 2) for n in range(4)]
        LE = reg(0, 2048)
        LP = reg(2048, 2048)
        HAT = v3(reg(4096, 2048), 4)
        KDT = v3(reg(8192, 2048), 4)
        onsq = v3(reg(7168, 1024), 2)
        raw_vec = reg(21000, 128)
        wba_raw = v3(reg(21200, 64), 8)
        lv_raw = v3(reg(21500, len(LEVELS) * P), len(LEVELS))
        empty = ar[0:SLOT_TILES, 21300:21428]
        Y1 = v3(reg(0, 8192), 4)
        RQ = reg(8192, 2048).rearrange("p (h c t) -> p h c t", h=2, c=2)
        RK = reg(10240, 2048).rearrange("p (h c t) -> p h c t", h=2, c=2)
        RV = reg(12288, 4096).rearrange("p (h j n) -> p h j n", h=2, j=4)
        RAT = v3(reg(16384, 2048), 4)
        cos_t = reg(18432, 512)
        sin_t = reg(18944, 512)
        DH = reg(19456, 512)
        rtmp = v3(reg(19968, 1024), 2)
        gt = v3(reg(20992, 1024), 2)
        rprod = S[:, :]
        rnw = Stmp[:, :]
        rjunk = vnew[:, :]

        def htok(n):
            return v3(reg({0: 10240, 1: 4096, 2: 0, 3: 4096, 4: 4096}[n], 2048), 2)

        def wb(n):
            return reg({0: 12288, 1: 6144, 2: 2048, 3: 6144, 4: 6144}[n], 1024)

        hTf = v3(reg(0, 4096), 8)
        xg = v3(reg(7168, 2048), 2)
        ysb = v3(reg(9216, 2048), 2)
        sg = v3(reg(11264, 512), 2)
        aact = v3(reg(11776, 512), 2)
        YP = reg(12288, 4096).rearrange("p (b j d) -> p b j d", b=2, j=2)
        ovWg = v3(reg(16384, 4096), 8)
        ovWd = v3(reg(20480, 2048), 2)

        SEM = {}

        def s_(name):
            if name not in SEM:
                SEM[name] = sem(name)
            return SEM[name]

        raw_loaded = [sem(f"raw_loaded{n}") for n in range(NRAW)]
        hi_done, lo_pool, lo_dve = sem("hi_done"), sem("lo_pool"), sem("lo_dve")
        piece_used, dense_ready = sem("piece_used"), sem("dense_ready")
        dense_read = {"act": sem("dense_read_act"), "dve": sem("dense_read_dve")}
        tile_ready = sem("tile_ready")
        tile_read = {"act": sem("tile_read_act"), "dve": sem("tile_read_dve")}

        def piece_src(i):
            for l in range(2):
                if MOE_PIECE[l] <= i < MOE_PIECE[l] + 6 * NE:
                    e, j = divmod(i - MOE_PIECE[l], 6)
                    return moe_src(l, e, j)
            if i >= MOE_PIECE[1] + 6 * NE:
                i = 0
            db = i // 4 if i < MOE_PIECE[0] else (i - 6 * NE) // 4
            kp = (i - first_piece(db)) % 4
            kind, which, c = BLOCKS[db]
            if kind.endswith("in"):
                w = a["even_w_in"][0] if kind == "even_in" else a["odd_w_in"][0]
                return w.rearrange("(p k) c -> p k c", k=KD)[:, 2 * kp:2 * kp + 2, c:c + 512]
            w = a["even_w_out"][0] if kind == "even_out" else a["odd_w_out"][0][DM * which:DM * which + DM]
            return w.rearrange("(k p) c -> p k c", p=P)[:, 2 * kp:2 * kp + 2, c:c + 512]

        def moe_src(l, e, j):
            if j < 4:
                w = a["moe_w_gate_up"][l].rearrange("e (p k) c -> p e k c", k=KD)
                return w[:, bass.ds(e, 1), 2 * j:2 * j + 2, :].squeeze(1) if not isinstance(e, int) else w[:, e, 2 * j:2 * j + 2, :]
            w = a["moe_w_down"][l].rearrange("e (k p) c -> p e k c", p=P)
            c = 512 * (j - 4)
            return w[:, bass.ds(e, 1), :, c:c + 512].squeeze(1) if not isinstance(e, int) else w[:, e, :, c:c + 512]

        def wait_lo(eng, i):
            eng.wait_ge(lo_dve if lo_by_dve(i) else lo_pool, lo_count(i))

        def wait_used(eng, i):
            db = i // 4 if i < MOE_PIECE[0] else (i - 6 * NE) // 4
            kp = i - first_piece(db)
            assert 0 <= kp < 4
            if kp == 3:
                eng.wait_ge(dense_ready, 4 * db + 4)
            else:
                eng.wait_ge(piece_used, 3 * db + kp + 1)

        def wait_spl_free(eng, i):
            if i >= NSPL and not (MOE_PIECE[0] + 6 * NE <= i < MOE_PIECE[0] + 6 * NE + 4):
                wait_used(eng, i - NSPL)

        def tile(name):
            return ps[:, 4 + SIDE_AT[name] % 4, :]

        def tile_is_ready(eng, name):
            eng.wait_ge(tile_ready, SIDE_AT[name] + 1)

        def tile_is_read(eng, name):
            eng.wait_ge(tile_read[SIDE[SIDE_AT[name]][1]], SIDE_READ[name])

        class Line:

            def __init__(self, eng, who):
                self.eng, self.who = eng, who
                self.own = s_(f"{who}_line")
                self.n = {}
                self.reads = 0

            def __call__(self, ins, on=None):
                sm = on if on is not None else self.own
                ins.then_inc(sm, 1)
                self.n[sm.name] = self.n.get(sm.name, 0) + 1
                self.eng.wait_ge(sm, self.n[sm.name])

            def read(self, ins, name):
                assert SIDE[SIDE_AT[name]][1] == self.who, name
                assert SIDE_READ[name] == self.reads + 1, (name, SIDE_READ[name], self.reads)
                self.reads += 1
                self(ins, tile_read[self.who])

        def bc_h(ap, n=P):
            return ap.unsqueeze(2).broadcast_to([ap.shape[0], 4, n])

        def bc_m(ap, n=4):
            return ap.unsqueeze(1).broadcast_to([ap.shape[0], n, ap.shape[1]])

        def cols(T, w=P):
            return slice(T * w, T * w + w)

        def mm3(dst, lh, ll, rh, rl, first, last):
            nc.tensor.matmul(dst, lh, rh, start=first, stop=False)
            nc.tensor.matmul(dst, lh, rl, start=False, stop=False)
            return nc.tensor.matmul(dst, ll, rh, start=False, stop=last)

        NORM_W = [a["norm_mix_w"][0], a["norm_ffn_w"][0], a["norm_mix_w"][1], a["norm_ffn_w"][1], a["final_norm_w"]]
        x_ready = [(s_("x_loaded"), 16), (dense_read["dve"], evac_count(9, 3)), (s_("moe_added0"), 4),
                   (dense_read["dve"], evac_count(25, 3)), (s_("moe_added1"), 4)]

        RO = 12288
        Lst = reg(RO, 128)
        ones = reg(RO + 128, 128)
        lg = v3(reg(RO + 256, 80), 4)
        rb = reg(RO + 336, 20)
        g0 = reg(RO + 356, 4)
        r_a = v3(reg(RO + 384, 16), 4)
        r_b = v3(reg(RO + 400, 16), 4)
        gm = v3(reg(RO + 416, 16), 4)
        r_c = reg(RO + 432, 64).rearrange("p (T g e) -> p T g e", T=4, g=4)
        fs = v3(reg(RO + 496, 16), 4)
        m1 = v3(reg(RO + 512, 16), 4)
        m2 = v3(reg(RO + 528, 16), 4)
        mx = reg(RO + 544, 4)
        mx2 = reg(RO + 548, 4)
        gp = reg(RO + 552, 4)
        ed = reg(RO + 556, 4)
        oh = [v3(reg(RO + 560 + 64 * n, 64), 4) for n in range(2)]
        anyh = v3(reg(RO + 688, 64), 4)
        slotv = v3(reg(RO + 752, 64), 4)
        tmp64 = v3(reg(RO + 816, 64), 4)
        ncnt = reg(RO + 880, 16)
        ovc = reg(RO + 896, 16)
        ovi = reg(RO + 912, 16)
        ovt = reg(RO + 928, 16)
        slotf = reg(RO + 944, 8)
        slots_u = reg(RO + 952, 8).bitcast(U32)
        tokv = reg(RO + 960, 8)
        first4 = reg(RO + 968, 4)
        iota8 = reg(RO + 972, 8)
        offs16 = reg(RO + 980, 16)
        eidf = reg(RO + 996, 8)
        cmp7 = reg(RO + 1004, 112)
        rw = v3(reg(RO + 1120, 160), 8)
        slotrow = ar[0:SLOT_TILES, RO + 1280:RO + 1408]
        w12 = small[:, 404:412]
        onesrow = reg(RO + 1408, 16)
        zero16 = reg(RO + 1424, 16)

        def overflow_flag(eng, l):
            eng.wait_ge(s_("slots_known"), l + 1)
            return eng.value_load(eid[0:1, 7:8], min_val=0, max_val=7)

        def overflow_sp(sp, l):
            n = overflow_flag(sp, l)
            with sp.If(n > 0):
                with sp.Fori(0, 7) as j:
                    sp.wait_ge(s_(f"ov_stored{l}"), j + 1)
                    settle(sp)
                    e = sp.value_load(eid[0:1, bass.ds(j, 1)], min_val=0, max_val=NE - 1)
                    wg = a["moe_w_gate_up"][l].rearrange("e (p k) c -> p e (k c)", k=KD)[:, bass.ds(e, 1), :].squeeze(1)
                    wd = a["moe_w_down"][l].rearrange("e (k p) c -> p e k c", p=P)[:, bass.ds(e, 1), :, :].squeeze(1)
                    sp.dma_start(ovWg.rearrange("p k c -> p (k c)"), wg).then_inc(s_(f"ov_w{l}"), 16)
                    sp.dma_start(ovWd, wd).then_inc(s_(f"ov_w{l}"), 16)

        def settle(eng):
            eng.wait_ge(hi_done, 1)

        gate_cell = sb("gate_cell", [P, 1])
        block = ctx.enter_context(nc.Block())

        @block.sync
        def _(sp):
            sp.dma_start(X[:, :, :], a["x"][0].rearrange("(T p) d -> p T d", p=P)).then_inc(s_("x_loaded"), 16)

            def load(i):
                if i >= NRAW:
                    wait_lo(sp, i - NRAW)
                sp.dma_start(raw[:, i % NRAW, :, :], piece_src(i)).then_inc(raw_loaded[i % NRAW], 16)

            def moe_loads(l):
                m = MOE_PIECE[l]
                for i in range(m, m + 12):
                    load(i)
                with sp.Fori(1, NE // 2) as it:
                    for j in range(12):
                        sp.wait_ge(lo_dve, it * 12 + (lo_count(m + 12 + j - NRAW) - 12))
                        sp.dma_start(raw[:, (m + j) % NRAW, :, :], moe_src(l, it * 2 + j // 6, j % 6))\
                            .then_inc(raw_loaded[(m + j) % NRAW], 16)

            for i in range(MOE_PIECE[0]):
                load(i)
            moe_loads(0)
            for i in range(MOE_PIECE[0] + 6 * NE, MOE_PIECE[1]):
                load(i)
                if i == MOE_PIECE[0] + 6 * NE + 3:
                    overflow_sp(sp, 0)
            moe_loads(1)
            for i in range(MOE_PIECE[1] + 6 * NE, NPIECE):
                load(i)
            overflow_sp(sp, 1)
            for T in range(NT):
                sp.wait_ge(s_("h_ready"), 4 * 4 + T + 1)
                sp.dma_start(out[0].rearrange("(T p) d -> T p d", p=P)[T], htok(4)[:, T % 2, :]).then_inc(s_(f"out_stored{T % 2}"), 16)
            sp.wait_ge(s_("out_stored0"), 32)
            sp.wait_ge(s_("out_stored1"), 32)

        @block.gpsimd
        def _(pool):
            L = Line(pool, "pool")

            def lo(i):
                if i >= NPIECE or lo_by_dve(i):
                    return
                pool.wait_ge(hi_done, i + 1)
                wait_spl_free(pool, i)
                pool.tensor_tensor(wl[:, i % NSPL, :, :], raw[:, i % NRAW, :, :], wh[:, i % NSPL, :, :].bitcast(F32),
                                   ALU.subtract).then_inc(lo_pool, 1)

            def rsqrt(dst, src, n, ready, count, on):
                pool.wait_ge(ready, count)
                pool.tensor_tensor(dst, src, mhalf[:, 0:n], ALU.pow).then_inc(on, 1)

            def carry():
                pool.tensor_tensor(gate_cell[:, :], mhalf[:, 0:1], mhalf[:, 0:1], ALU.add)

            def moe(l):
                last_row = pool.to_reg(SEQ - 1)
                last_pair_row = pool.to_reg(2 * SEQ - 1)
                pool.wait_ge(s_("slots_known"), l + 1)
                pool.wait_ge(s_("slots_cleared"), 32)
                for n in range(8):
                    pool.indirect_dma_start(out=slot_dram[l], out_offset=bass.IndirectOffsetOnAxis(ap=slots_u[:, n:n + 1], axis=0),
                                            in_=tokv[:, n:n + 1], in_offset=None).then_inc(s_(f"slots_stored{l}"), 16)
                pool.wait_ge(s_(f"slots_stored{l}"), 128)
                pool.dma_start(slotrow, slot_dram[l].rearrange("(e p) o -> e (p o)", p=P)).then_inc(s_(f"slotrow_loaded{l}"), 16)
                pool.wait_ge(s_("rows_known"), l + 1)
                for q in range(2):
                    pool.wait_ge(s_(f"h_stored{q}"), 32 * (l + 1))
                pool.wait_ge(s_("xg_cleared"), l + 1)

                def gather(col, par):
                    L(pool.tensor_copy(cur[:, par:par + 1], idx[:, 0, col].bitcast(U32)))
                    pool.indirect_dma_start(out=xg[:, par, :], out_offset=None, in_=hs_dram[l],
                                            in_offset=bass.IndirectOffsetOnAxis(ap=cur[:, par:par + 1], axis=0),
                                            bounds_check=last_row, oob_is_err=False).then_inc(s_(f"xg_loaded{par}"), 16)

                gather(slice(0, 1), 0)
                gather(slice(1, 2), 1)
                G = s_("pool_moe")
                base = l * 64
                with pool.Fori(0, NE // 2) as it:
                    for par in range(2):
                        k = base + par * 4
                        pool.wait_ge(s_("xT_ready"), it * 4 + (34 * l + 2 * par + 2))
                        pool.tensor_copy(cur[:, par:par + 1], idx[:, 0, bass.ds(it * 2 + (2 + par), 1)].bitcast(U32)).then_inc(G, 1)
                        pool.wait_ge(G, it * 4 + (32 * l + 2 * par + 1))
                        carry()
                        pool.indirect_dma_start(out=xg[:, par, :], out_offset=None, in_=hs_dram[l],
                                                in_offset=bass.IndirectOffsetOnAxis(ap=cur[:, par:par + 1], axis=0),
                                                bounds_check=last_row, oob_is_err=False).then_inc(s_(f"xg_loaded{par}"), 16)
                        pool.tensor_copy(cur[:, 2 + par:3 + par], idx[:, 1, bass.ds(it * 2 + par, 1)].bitcast(U32)).then_inc(G, 1)
                        pool.wait_ge(G, it * 4 + (32 * l + 2 * par + 2))
                        pool.wait_ge(s_("y_read"), it * 4 + (32 * l + 2 * par + 4))
                        carry()
                        pool.indirect_dma_start(out=y2_dram[l], out_offset=bass.IndirectOffsetOnAxis(ap=cur[:, 2 + par:3 + par], axis=0),
                                                in_=ysb[:, par, :], in_offset=None,
                                                bounds_check=last_pair_row, oob_is_err=False).then_inc(s_("y_stored"), 16)
                        pool.wait_ge(s_("y_stored"), it * 32 + (256 * l + 16 * par + 16))
                        pool.nop().then_inc(s_("ysb_free"), 1)
                for q in range(2):
                    pool.wait_ge(s_(f"xg_loaded{q}"), 144 * (l + 1))
                pool.nop().then_inc(s_(f"ov_stored{l}"), 1)
                n = overflow_flag(pool, l)
                with pool.If(n > 0):
                    with pool.Fori(0, 7) as j:
                        pool.tensor_copy(cur[:, 0:1], idx[:, 0, bass.ds(j + NE, 1)].bitcast(U32)).then_inc(s_(f"ov_cur{l}"), 1)
                        pool.wait_ge(s_(f"ov_cur{l}"), j * 2 + 1)
                        pool.wait_ge(s_(f"ov_stored{l}"), j + 1)
                        carry()
                        pool.indirect_dma_start(out=xg[:, 0, :], out_offset=None, in_=hs_dram[l],
                                                in_offset=bass.IndirectOffsetOnAxis(ap=cur[:, 0:1], axis=0),
                                                bounds_check=last_row, oob_is_err=False).then_inc(s_(f"ov_x{l}"), 16)
                        pool.tensor_copy(cur[:, 2:3], idx[:, 1, bass.ds(j + NE, 1)].bitcast(U32)).then_inc(s_(f"ov_cur{l}"), 1)
                        pool.wait_ge(s_(f"ov_cur{l}"), j * 2 + 2)
                        pool.wait_ge(s_(f"ov_y{l}"), j * 2 + 2)
                        carry()
                        pool.indirect_dma_start(out=y2_dram[l], out_offset=bass.IndirectOffsetOnAxis(ap=cur[:, 2:3], axis=0),
                                                in_=ysb[:, 0, :], in_offset=None,
                                                bounds_check=last_pair_row, oob_is_err=False).then_inc(s_(f"ov_ydma{l}"), 16)
                        pool.wait_ge(s_(f"ov_ydma{l}"), j * 16 + 16)
                        pool.nop().then_inc(s_(f"ov_stored{l}"), 1)
                pool.nop().then_inc(s_("y_all_stored"), 1)

            pool.memset(mhalf, -0.5).then_inc(L.own, 1)
            L.n[L.own.name] = 1
            pool.wait_ge(L.own, 1)
            for _ in range(2):
                pool.nop().then_inc(s_("ysb_free"), 1)
            for i in range(3):
                lo(i)
            for step in SCHEDULE:
                if step[0] == "piece":
                    lo(first_piece(step[1]) + step[2] + 3)
                elif step[0] == "norm":
                    n = step[1]
                    rsqrt(rs, ms, 4, s_("norm_ms"), n + 1, s_("norm_r"))
                elif step[0] == "l2":
                    rsqrt(rn, ssn, 32, s_("l2_ms"), 1, s_("l2_r"))
                elif step[0] == "onorm":
                    rsqrt(ors, oss, 16, s_("o_ms"), step[1] + 1, s_("o_r"))
                elif step[0] == "evac" and BLOCKS[step[1]][1] and isinstance(BLOCKS[step[1]][1], tuple) and BLOCKS[step[1]][1][0] == "rg":
                    h = BLOCKS[step[1]][1][1]
                    rsqrt(ors[:, 0:4], oss[:, 0:4], 4, s_("ro_ms"), h + 1, s_("ro_r"))
                elif step[0] == "moe":
                    lo(MOE_PIECE[step[1]] + 3)
                    moe(step[1])

        @block.scalar
        def _(act):
            A = Line(act, "act")
            dense_reads = [0]

            def hi(i):
                if i >= NPIECE:
                    return
                act.wait_ge(raw_loaded[i % NRAW], 16 * (i // NRAW + 1))
                wait_spl_free(act, i)
                act.activation(wh[:, i % NSPL, :, :], raw[:, i % NRAW, :, :], ACT.Copy).then_inc(hi_done, 1)

            def dense_tile(db, t):
                act.wait_ge(dense_ready, 4 * db + t + 1)
                return ps[:, t, :]

            def consts():
                ld = s_("consts_loaded")
                dm = [(ident[:, :], a["c_ident"]), (U[:, :], a["c_U"]), (m16[:, :], a["c_m16"]), (moff[:, :], a["c_moff"]),
                      (lv_raw, a["c_lv"]), (resetm[:, :], a["c_reset"]),
                      (raw_vec[0:48, :], a["gdn_conv_w"][0].rearrange("j (g p) -> (j g) p", p=P)),
                      (raw_vec[48:60, :], a["hgrn_lb_logits"].rearrange("r (h p) -> (r h) p", p=P)),
                      (dtb, a["gdn_dt_bias"].broadcast_to([P, 4])), (alog, a["gdn_a_log"].broadcast_to([P, 4])),
                      (gnw[:, :], a["gdn_norm_w"].broadcast_to([P, P])), (hnw[:, :], a["hgrn_norm_w"].broadcast_to([P, P])),
                      (wba_raw, a["even_w_in"][0].rearrange("(p k) c -> p k c", k=KD)[:, :, 2048:2056])]
                for dst, src in dm:
                    act.dma_start(dst, src).then_inc(ld, 16)
                act.wait_ge(s_("empty_made"), 1)
                for l in range(2):
                    act.dma_start(slot_dram[l].rearrange("(e p) o -> e (p o)", p=P), empty).then_inc(s_("slots_cleared"), 16)
                act.wait_ge(ld, 16 * len(dm))
                A(act.activation(wba_h[:, :, :], wba_raw, ACT.Copy), s_("wba_hi"))
                act.wait_ge(s_("lb_args"), 1)
                A(act.activation(lbt[:, 0:12], lbt[:, 0:12], ACT.Exp), s_("lb_exp"))

            def norm(n):
                sm, val = x_ready[n]
                act.wait_ge(sm, val)
                act.dma_start(wb(n), NORM_W[n].rearrange("(a n) -> a n", a=1).broadcast_to([P, DM])).then_inc(s_("wb_loaded"), 16)
                for T in range(NT):
                    A(act.activation(htok(n)[:, 1, :], X[:, T, :], ACT.Square, accum_out=ss[:, T:T + 1]), s_("norm_ss"))
                if n == 4:
                    return
                for T in range(NT):
                    if n in (1, 3):
                        act.wait_ge(s_("h_ready"), 4 * n + T + 1)
                        act.dma_start(hs_dram[n // 2].rearrange("(T p) d -> T p d", p=P)[T], htok(n)[:, T % 2, :])\
                            .then_inc(s_(f"h_stored{T % 2}"), 16)
                    for g in range(2):
                        name = ("hT", n, T, g)
                        tile_is_ready(act, name)
                        src = v3(tile(name), 4)
                        if n in (1, 3):
                            A.read(act.activation(hTf[:, 4 * g:4 * g + 4, cols(T)], src, ACT.Copy), name)
                        else:
                            A(act.activation(HTH[:, 4 * g:4 * g + 4, cols(T)], src, ACT.Copy), s_("hT_hi_made"))

            def yT(l, kh):
                act.wait_ge(dense_ready, 4 * {(0, 0): 8, (1, 0): 22, (1, 1): 24}[l, kh])
                for T in range(NT):
                    for g in range(2):
                        name = ("yT", l, kh, T, g)
                        tile_is_ready(act, name)
                        A(act.activation(HTH[:, 4 * g:4 * g + 4, cols(T)], v3(tile(name), 4), ACT.Copy), s_("hT_hi_made"))

            def gates_act():
                act.wait_ge(s_("z_ready"), 1)
                A(act.activation(esp, esp, ACT.Exp, scale=-1.0), s_("gate_exp"))
                A(act.activation(alog, alog, ACT.Exp), s_("gate_exp"))
                A(act.activation(beta, beta, ACT.Tanh, scale=0.5), s_("gate_exp"))
                act.wait_ge(s_("sp_ready"), 1)
                A(act.activation(spt, spt, ACT.Ln), s_("gate_exp"))
                tile_is_read(act, "gc")
                A(act.activation(egc, gc, ACT.Exp), s_("egc_ready"))

            def tok(nm, T):
                name = ("tok", nm, T)
                tile_is_ready(act, name)
                dst = {"q": Y0[:, T, 0:512], "k": KT[:, T, :], "v": VT[:, T, :]}[nm]
                if nm == "v":
                    A.read(act.activation(dst, tile(name), ACT.Copy), name)
                    return
                A(act.activation(dst, tile(name), ACT.Copy))
                n = (nm == "k") * 4 + T
                if n >= 2:
                    act.wait_ge(s_("sq_reduced"), n - 1)
                A.read(act.activation(sqt[:, n % 2, :], tile(name), ACT.Square), name)

            def l2():
                for T in range(NT):
                    tile_is_ready(act, ("qb", T))
                    A.read(act.activation(QF[:, :, cols(T)], v3(tile(("qb", T)), 4), ACT.Copy), ("qb", T))

            def gdn_chunks(pr):
                Ts = (2 * pr, 2 * pr + 1)
                for T in Ts:
                    q = T % 2
                    act.wait_ge(s_("g_args"), T + 1)
                    A.read(act.activation(PA[2][:, q, :], tile(("Gb", T)), ACT.Exp), ("Gb", T))
                    A(act.activation(PA[0][:, q, :], PA[0][:, q, :], ACT.Exp, scale=-1.0))
                    A(act.activation(PA[1][:, q, :], PA[1][:, q, :], ACT.Exp))
                    A(act.activation(kde[:, 4 * T:4 * T + 4], kde[:, 4 * T:4 * T + 4], ACT.Exp), s_("decays"))
                    tile_is_ready(act, ("DT", T))
                    A.read(act.activation(PA[4][:, q, :], tile(("DT", T)), ACT.Copy), ("DT", T))

                def copy(name, dst, after=None):
                    tile_is_ready(act, name)
                    if after is not None:
                        tile_is_ready(act, after)
                    A.read(act.activation(dst, tile(name), ACT.Copy), name)

                for T in Ts:
                    copy(("P2", T), PA[5][:, T % 2, :])
                    copy(("P2T", T), PA[6][:, T % 2, :])
                for r in (1, 2):
                    for T in Ts:
                        last = ("P", r, T) if r == 1 else ("PT", r, T)
                        copy(("PT", r, T), PA[6][:, T % 2, :], last)
                        if r == 1:
                            copy(("P", r, T), PA[5][:, T % 2, :])
                for T in Ts:
                    copy(("B", T), PA[5][:, T % 2, :])
                    copy(("BT", T), PA[6][:, T % 2, :])
                for T in Ts:
                    copy(("B2", T), PA[4][:, T % 2, :])
                for T in Ts:
                    copy(("IT", T), PA[8][:, T % 2, :])
                for T in Ts:
                    copy(("u", T), VT[:, T, :])
                    tile_is_ready(act, ("wT", T))
                    A.read(act.activation(KF[:, :, cols(T)], v3(tile(("wT", T)), 4), ACT.Copy), ("wT", T))

            def scan_out(nm, c, c0):
                T, r = c // 2, slice(64 * (c % 2), 64 * (c % 2) + 64)
                tile_is_ready(act, (nm, c))
                A.read(act.activation(Y0[r, T, c0:c0 + 512], tile((nm, c))[r, :], ACT.Copy, scale=DK ** -0.5), (nm, c))

            def onorm(w):
                act.wait_ge(s_("scan_done"), 1)
                for T in range(NT):
                    n = 8 + 4 * w + T
                    act.wait_ge(s_("sq_reduced"), n - 1)
                    A(act.activation(onsq[:, T % 2, :], Y0[:, T, 512 * w:512 * w + 512], ACT.Square), s_("o_sq"))

            def hgrn(step):
                if step[0] == "hdiag":
                    pass
                elif step[0] == "hlevel":
                    n = step[1]
                    act.wait_ge(s_("lv_args"), n + 1)
                    A(act.activation(LE, LE, ACT.Exp), s_("lv_exp"))
                elif step[0] == "hstate":
                    act.wait_ge(s_("lv_args"), len(LEVELS) + 1)
                    A(act.activation(LE, LE, ACT.Exp), s_("lv_exp"))
                    act.wait_ge(s_("hk_decayed"), 1)
                    A(act.activation(LE, HB.rearrange("p h t -> p (h t)"), ACT.Exp), s_("lv_exp"))
                    for T in range(NT):
                        tile_is_ready(act, ("kd", T))
                        A.read(act.activation(KDT[:, T, :], tile(("kd", T)), ACT.Copy), ("kd", T))

            def evac(db):
                kind, which, _c = BLOCKS[db]
                rd = dense_read["act"]
                if which in ("q", "k", "v"):
                    dst = {"q": QF, "k": KF, "v": VF}[which]
                    for t in range(5):
                        if t < 4:
                            n = 4 * db + t
                            src = dense_tile(db, t)
                            if n >= 2:
                                act.wait_ge(s_("conv_done"), n - 1)
                            A(act.activation(craw[:, t % 2, :], src, ACT.Copy), rd)
                        if t > 0:
                            act.wait_ge(s_("conv_done"), 4 * db + t)
                            A(act.activation(dst[:, t - 1, :], dst[:, t - 1, :], ACT.Silu), s_("conv_silu"))
                elif which == "hf":
                    for t in range(4):
                        src = dense_tile(db, t)
                        A(act.activation(HK[:, t, :], src, ACT.Tanh, scale=0.5), rd)
                    for t in range(4):
                        act.wait_ge(s_("f_ready"), t + 1)
                        A(act.activation(HQ[:, t, :], HB[:, t, :], ACT.Ln), s_("lf_ready"))
                elif which == "hq":
                    for t in range(4):
                        src = dense_tile(db, t)
                        act.wait_ge(s_("b_ready"), 4)
                        A(act.activation(HQ[:, t, :], src, ACT.Silu), rd)
                elif which == "hi":
                    for t in range(4):
                        src = dense_tile(db, t)
                        A(act.activation(HI[:, t, :], src, ACT.Copy), rd)
                elif which in ("z", "hg"):
                    for t in range(4):
                        src = dense_tile(db, t)
                        n = 4 * (which == "hg") + t
                        if n == 0:
                            act.wait_ge(s_("scan_done"), 1)
                        if n >= 2:
                            act.wait_ge(s_("z_used"), n - 1)
                        A(act.activation(zt[:, t % 2, :], src, ACT.Silu), rd)
                elif kind == "odd_in":
                    nm, h = which
                    if nm in ("rq", "rk"):
                        for t in range(4):
                            src = dense_tile(db, t)
                            n = rot_index(db) * 2 + t // 2
                            if n >= 1 and t % 2 == 0:
                                act.wait_ge(s_("rot_done"), n)
                            A(act.activation(rtmp[:, t % 2, :], src, ACT.Copy), rd)
                    elif nm == "rv":
                        for t in range(4):
                            src = dense_tile(db, t)
                            A(act.activation(RV[:, h % 2, t, :], src, ACT.Copy), rd)
                    else:
                        for t in range(4):
                            src = dense_tile(db, t)
                            n = 4 * h + t
                            if n >= 2:
                                act.wait_ge(s_("g_used"), n - 1)
                            A(act.activation(gt[:, t % 2, :], src, ACT.Silu), rd)

            def ro(h):
                for T in range(NT):
                    name = ("ro", h, T)
                    tile_is_ready(act, name)
                    A(act.activation(Y1[:, T, h * RDV:(h + 1) * RDV], tile(name), ACT.Copy))
                    if T == 0 and h > 0:
                        act.wait_ge(s_("ro_r"), h)
                    A.read(act.activation(rjunk, tile(name), ACT.Square, accum_out=oss[:, T:T + 1]), name)

            def moe(l):
                m = MOE_PIECE[l]
                act.wait_ge(s_("r_cexp"), l + 1)
                A(act.activation(r_a, r_a, ACT.Exp), s_("r_exp"))
                act.wait_ge(s_("r_eexp"), l + 1)
                A(act.activation(ed, ed, ACT.Exp), s_("r_exp"))
                xT_hi(l, 0, 0, 0, True)
                xT_hi(l, 0, 1, 0, True)
                with act.Fori(0, NE // 2) as it:
                    for par in range(2):
                        E = it * 2 + (16 * l + par)

                        def hi_in(j, ready_sem, ready_val):
                            n = m + 6 * par + j
                            act.wait_ge(raw_loaded[n % NRAW], it * 32 + 16 * (n // NRAW + 1))
                            act.wait_ge(ready_sem, ready_val)
                            act.activation(wh[:, n % NSPL, :, :], raw[:, n % NRAW, :, :], ACT.Copy).then_inc(hi_done, 1)

                        used = s_("gu_used")
                        hi_in(4, used, it * 6 + (48 * l + 3 * par + 1))
                        hi_in(5, used, it * 6 + (48 * l + 3 * par + 2))
                        hi_in(6, used, it * 6 + (48 * l + 3 * par + 3))
                        act.wait_ge(s_("gu_ready"), E + 1)
                        act.activation(sg[:, par, :], ps[:, par, 0:FE], ACT.Silu).then_inc(s_("silu_done"), 1)
                        act.wait_ge(s_("aT_ready"), E + 1)
                        act.activation(HTH[:, 4 + par, 0:256], ps[:, 6, 0:256], ACT.Copy).then_inc(s_("aT_hi"), 1)
                        hi_in(7, s_("gu_ready"), E + 1)
                        for g in range(2):
                            xT_hi(l, it * 2 + (par + 1), g, 1 - par, False)
                        act.wait_ge(s_("ysb_free"), E + 1)
                        for hf in range(2):
                            act.wait_ge(s_("y_ready"), E * 2 + (hf + 1))
                            act.activation(ysb[:, par, 512 * hf:512 * hf + 512], ps[:, 2 + hf, :], ACT.Copy).then_inc(s_("y_read"), 1)
                            hi_in(8 + hf, s_("y_ready"), E * 2 + (hf + 1))
                n = overflow_flag(act, l)
                with act.If(n > 0):
                    with act.Fori(0, 7) as j:
                        for g in range(2):
                            act.wait_ge(s_(f"ov_xT{l}"), j * 2 + (g + 1))
                            act.activation(hTf[:, 4 * g:4 * g + 4, 0:P], v3(ps[:, 4 + g, :], 4), ACT.Copy).then_inc(s_(f"ov_xTr{l}"), 1)
                        act.wait_ge(s_(f"ov_gu{l}"), j + 1)
                        act.activation(sg[:, 0, :], ps[:, 0, 0:FE], ACT.Silu).then_inc(s_(f"ov_silu{l}"), 1)
                        act.wait_ge(s_(f"ov_aT{l}"), j + 1)
                        act.activation(hTf[:, 0:2, P:2 * P], ps[:, 6, 0:256].rearrange("p (k n) -> p k n", k=2), ACT.Copy).then_inc(s_(f"ov_aTr{l}"), 1)
                        for hf in range(2):
                            act.wait_ge(s_(f"ov_yp{l}"), j * 2 + (hf + 1))
                            act.activation(ysb[:, 0, 512 * hf:512 * hf + 512], ps[:, 2 + hf, :], ACT.Copy).then_inc(s_(f"ov_y{l}"), 1)
                act.wait_ge(s_("y_all_stored"), l + 1)
                src = y2_dram[l].rearrange("(T p j) d -> T p j d", p=P, j=2)
                for T in range(NT):
                    if T >= 2:
                        act.wait_ge(s_(f"moe_added{l}"), T - 1)
                    act.dma_start(YP[:, T % 2, :, :], src[T]).then_inc(s_(f"yp_loaded{T % 2}"), 16)

            def xT_hi(l, e, g, par, static):
                act.wait_ge(s_("xT_ready"), e * 2 + (34 * l + g + 1))
                act.activation(HTH[:, 2 * par + g, :], ps[:, 4 + g, :], ACT.Copy).then_inc(s_("xT_hi"), 1)

            for _ in range(2):
                act.nop().then_inc(s_("y_read"), 1)
            for i in range(3):
                hi(i)
            for step in SCHEDULE:
                k = step[0]
                if k == "consts":
                    consts()
                elif k == "norm":
                    if step[1] == 2:
                        act.wait_ge(s_("moe_added0"), 4)
                        for n, (dst, src) in enumerate(((cos_t, a["c_cos"]), (sin_t, a["c_sin"]), (rnw, a["ret_norm_w"].broadcast_to([P, RDV])))):
                            act.dma_start(dst, src).then_inc(s_("ret_consts"), 16)
                    if step[1] in (1, 3):
                        l = step[1] // 2
                        act.wait_ge(*x_ready[step[1]])
                        for dst, src in ((Lst, a["c_Lst"]), (reg(RO + 972, 24), a["c_iota"]),
                                         (rb[:, 0:4], a["router_c_b"][l].rearrange("(a n) -> a n", a=1).broadcast_to([P, 4])),
                                         (rb[:, 4:20], a["router_f_b"][l].rearrange("(a n) -> a n", a=1).broadcast_to([P, 16])),
                                         (rw[:, :, 0:4], a["router_c_w"][l].rearrange("(p k) c -> p k c", k=KD)),
                                         (rw[:, :, 4:20], a["router_f_w"][l].rearrange("(p k) c -> p k c", k=KD)),
                                         (tokv, a["c_tok"]), (first4, a["c_first"])):
                            act.dma_start(dst, src).then_inc(s_("router_loaded"), 16)
                    norm(step[1])
                elif k == "piece":
                    hi_i = first_piece(step[1]) + step[2] + 3
                    if not lo_by_dve(hi_i):
                        hi(hi_i)
                elif k == "ba":
                    pass
                elif k == "gates":
                    gates_act()
                elif k == "tok":
                    tok(step[1], step[2])
                elif k == "l2":
                    l2()
                elif k == "gdn_chunks":
                    gdn_chunks(step[1])
                elif k == "scan":
                    scan_out("so", step[1], 0)
                elif k == "hscan":
                    scan_out("ho", step[1], 512)
                elif k == "onorm":
                    onorm(step[1])
                elif k in ("hdiag", "hlevel", "hstate"):
                    hgrn(step)
                elif k == "evac":
                    if evac_engine(step[1]) == "act":
                        evac(step[1])
                elif k == "yT":
                    yT(step[1], step[2])
                elif k == "score":
                    h = step[1]
                    if h > 0:
                        act.wait_ge(tile_read["dve"], SIDE_READ[("sc", h - 1, NT - 1)])
                    act.dma_start(DH, a["c_decay"][h]).then_inc(s_("dh_loaded"), 16)
                elif k == "ro":
                    ro(step[1])
                elif k == "moe":
                    hi(MOE_PIECE[step[1]] + 3)
                    moe(step[1])

        @block.vector
        def _(dve):
            D = Line(dve, "dve")
            tt, ts, stt = dve.tensor_tensor, dve.tensor_scalar, dve.scalar_tensor_tensor

            def consts():
                D(dve.memset(empty, EMPTY), s_("empty_made"))
                D(dve.memset(S[:, :], 0.0))
                tile_is_ready(dve, "vec")
                D.read(dve.tensor_copy(vec[:, :], tile("vec")[:, 0:60]), "vec")
                D(dve.tensor_copy(lvmask[:, :, :], lv_raw))
                lb3 = vec[:, 48:60]
                D(tt(lbs[:, 0:4], lb3[:, 0:4], lb3[:, 4:8], ALU.max))
                D(tt(lbs[:, 0:4], lbs[:, 0:4], lb3[:, 8:12], ALU.max))
                D(tt(v3(lbt[:, 0:12], 3), v3(lb3, 3), bc_m(lbs[:, 0:4], 3), ALU.subtract), s_("lb_args"))
                dve.wait_ge(s_("lb_exp"), 1)
                D(tt(lbs[:, 4:8], lbt[:, 0:4], lbt[:, 4:8], ALU.add))
                D(tt(lbs[:, 4:8], lbs[:, 4:8], lbt[:, 8:12], ALU.add))
                D(dve.reciprocal(lbs[:, 4:8], lbs[:, 4:8]))
                D(tt(lbs[:, 8:12], lbt[:, 0:4], lbs[:, 4:8], ALU.mult))
                D(ts(c1, lbs[:, 8:12], -0.5, 0.5, ALU.mult, ALU.add))
                D(tt(c2, lbs[:, 8:12], c1, ALU.add))
                dve.wait_ge(s_("wba_hi"), 1)
                D(tt(wba_l[:, :, :], wba_raw, wba_h[:, :, :].bitcast(F32), ALU.subtract), s_("wba_lo"))

            def norm(n):
                dve.wait_ge(s_("norm_ss"), 4 * n + 4)
                D(ts(ms, ss, 1.0 / DM, EPS, ALU.mult, ALU.add), s_("norm_ms"))
                dve.wait_ge(s_("norm_r"), n + 1)
                dve.wait_ge(s_("wb_loaded"), 16 * (n + 1))
                for T in range(NT):
                    if T >= 2:
                        if n < 4:
                            tile_is_ready(dve, ("hT", n, T - 2, 1))
                        if n in (1, 3):
                            dve.wait_ge(s_(f"h_stored{T % 2}"), 32 * (n // 2) + 16)
                        if n == 4:
                            dve.wait_ge(s_(f"out_stored{T % 2}"), 16)
                    D(stt(htok(n)[:, T % 2, :], X[:, T, :], rs[:, T:T + 1], wb(n), ALU.mult, ALU.mult), s_("h_ready"))
                    if n in (0, 2) and T >= 1:
                        lo_tiles(("hT", n, T - 1), T - 1)
                if n in (0, 2):
                    lo_tiles(("hT", n, 3), 3)

            his = [0]

            def lo_tiles(name, T):
                for g in range(2):
                    his[0] += 1
                    dve.wait_ge(s_("hT_hi_made"), his[0])
                    nm = name + (g,)
                    D.read(tt(HTL[:, 4 * g:4 * g + 4, cols(T)], v3(tile(nm), 4), HTH[:, 4 * g:4 * g + 4, cols(T)].bitcast(F32),
                              ALU.subtract), nm)

            def gate_inputs():
                tile_is_ready(dve, "ba")
                D.read(dve.tensor_copy(ba, v3(tile("ba")[:, 0:32], 4)), "ba")
                D(tt(v3(zsp, 4), ba[:, :, 4:8], bc_m(dtb), ALU.add))
                D(ts(spt, zsp, -1.0, None, ALU.mult))
                D(tt(esp, zsp, spt, ALU.max))
                D(dve.tensor_copy(v3(beta, 4), ba[:, :, 0:4]), s_("z_ready"))

            def gates():
                dve.wait_ge(s_("gate_exp"), 3)
                D(ts(spt, esp, 1.0, None, ALU.add), s_("sp_ready"))
                D(ts(beta, beta, 0.5, 0.5, ALU.mult, ALU.add))
                dve.wait_ge(s_("gate_exp"), 4)
                D(stt(spt, zsp, 0.0, spt, ALU.max, ALU.add))
                D(stt(v3(gg, 4), v3(spt, 4), -1.0, bc_m(alog), ALU.mult, ALU.mult), s_("g_ready"))
                tile_is_ready(dve, "gc")
                D.read(dve.tensor_copy(gc, tile("gc")[:, 0:16]), "gc")
                dve.wait_ge(s_("egc_ready"), 1)
                D(tt(bege, beta, egc, ALU.mult))

            def tok(nm, T):
                if nm == "v":
                    return
                tile_is_read(dve, ("tok", nm, T))
                n = 4 * (nm == "k") + T
                D(dve.tensor_reduce(ssn[:, 4 * n:4 * n + 4], v3(sqt[:, n % 2, :], 4), AX.X, ALU.add), s_("sq_reduced"))

            def l2():
                D(ts(ssn, ssn, EPS, None, ALU.add), s_("l2_ms"))
                dve.wait_ge(s_("l2_r"), 1)
                for T in range(NT):
                    D(tt(v3(Y0[:, T, 0:512], 4), v3(Y0[:, T, 0:512], 4), bc_h(rn[:, 4 * T:4 * T + 4]), ALU.mult), s_("qk_normed"))
                    D(tt(v3(KT[:, T, :], 4), v3(KT[:, T, :], 4), bc_h(rn[:, 16 + 4 * T:20 + 4 * T]), ALU.mult), s_("qk_normed"))
                for T in range(NT):
                    tile_is_ready(dve, ("kb", T))
                    D.read(dve.tensor_copy(KF[:, :, cols(T)], v3(tile(("kb", T)), 4)), ("kb", T))

            def gdn_chunks(pr):
                Ts = (2 * pr, 2 * pr + 1)
                for T in Ts:
                    q = T % 2
                    h4 = slice(4 * T, 4 * T + 4)
                    gb = tile(("Gb", T))
                    tile_is_ready(dve, ("Gb", T))
                    for h in range(NH):
                        D(ts(PA[0][:, q, cols(h)], gb[:, cols(h)], gc[:, 4 * T + h:4 * T + h + 1], 0.0, ALU.subtract, ALU.max))
                        D(ts(PA[1][:, q, cols(h)], gb[:, cols(h)], gc[:, 4 * T + h:4 * T + h + 1], 0.0, ALU.subtract, ALU.min))
                    D(tt(kde[0:64, h4], v3(gb, 4)[0:64, :, 63], gc[0:64, h4], ALU.subtract))
                    D(tt(kde[64:128, h4], v3(gb, 4)[64:128, :, 127], gc[64:128, h4], ALU.subtract), s_("g_args"))
                    dve.wait_ge(s_("decays"), T + 1)
                    D(tt(v3(PA[0][:, q, :], 4), v3(PA[0][:, q, :], 4), bc_h(beta[:, h4]), ALU.mult))
                    D(tt(v3(PA[3][:, q, :], 4), v3(PA[0][:, q, :], 4), bc_m(moff[:, :]), ALU.mult))
                    D(tt(v3(PA[0][:, q, :], 4), v3(PA[0][:, q, :], 4), bc_m(m16[:, :]), ALU.mult))
                    D(tt(v3(PA[1][:, q, :], 4), v3(PA[1][:, q, :], 4), bc_m(U[:, :]), ALU.mult))
                    tile_is_ready(dve, ("KK", T))
                    D(tt(PA[3][:, q, :], tile(("KK", T)), PA[3][:, q, :], ALU.mult))
                    D.read(tt(PA[0][:, q, :], tile(("KK", T)), PA[0][:, q, :], ALU.mult), ("KK", T))
                    tile_is_ready(dve, ("KQ", T))
                    D.read(tt(AT0[:, T, :], tile(("KQ", T)), PA[1][:, q, :], ALU.mult), ("KQ", T))
                    for c in range(2):
                        D(dve.tensor_copy(egl[:, 2 * T + c, :], v3(PA[2][:, q, :], 4)[:, :, 64 * c + 63]))
                    D(tt(QF[:, :, cols(T)], QF[:, :, cols(T)], v3(PA[2][:, q, :], 4), ALU.mult))
                    D(tt(v3(PA[7][:, q, :], 4), bc_m(ident[:, :]), v3(PA[0][:, q, :], 4), ALU.subtract))
                    tile_is_read(dve, ("DT", T))
                    D(tt(v3(PA[8][:, q, :], 4), bc_m(ident[:, :]), v3(PA[4][:, q, :], 4), ALU.subtract), s_("x1_ready"))
                    D(tt(v3(PA[9][:, q, :], 4), v3(VT[:, T, :], 4), bc_h(beta[:, h4]), ALU.mult))
                    D(tt(v3(PA[10][:, q, :], 4), v3(KT[:, T, :], 4), bc_h(bege[:, h4]), ALU.mult))
                    D(tt(v3(KT[:, T, :], 4), v3(KT[:, T, :], 4), bc_h(kde[:, h4]), ALU.mult), s_("vk_ready"))
                for r in (1, 2, 3):
                    for T in Ts:
                        q = T % 2
                        tile_is_ready(dve, ("XT", r, T))
                        D.read(tt(PA[7][:, q, :], PA[7][:, q, :], tile(("X", r, T)), ALU.add), ("X", r, T))
                        D.read(tt(PA[8][:, q, :], PA[8][:, q, :], tile(("XT", r, T)), ALU.add), ("XT", r, T))
                for T in Ts:
                    tile_is_read(dve, ("BT", T))
                    D(tt(v3(PA[0][:, T % 2, :], 4), bc_m(ident[:, :]), v3(PA[6][:, T % 2, :], 4), ALU.subtract), s_("n1_ready"))
                for T in Ts:
                    tile_is_ready(dve, ("N2", T))
                    D.read(tt(PA[1][:, T % 2, :], PA[0][:, T % 2, :], tile(("N2", T)), ALU.add), ("N2", T))

            def scan(c):
                T, r = c // 2, slice(64 * (c % 2), 64 * (c % 2) + 64)
                tile_is_read(dve, ("u", T))
                tile_is_ready(dve, ("sv", c))
                D.read(tt(vnew[r, :], VT[r, T, :], tile(("sv", c))[r, :], ALU.subtract), ("sv", c))
                D(tt(v3(Stmp[:, :], 4), v3(S[:, :], 4), bc_h(egl[:, c, :]), ALU.mult))
                tile_is_ready(dve, ("ss", c))
                D.read(tt(S[:, :], Stmp[:, :], tile(("ss", c)), ALU.add), ("ss", c))
                if c == NC - 1:
                    D(dve.memset(S[:, :], 0.0), s_("scan_done"))

            def onorm(w):
                for T in range(NT):
                    dve.wait_ge(s_("o_sq"), 4 * w + T + 1)
                    D(dve.tensor_reduce(oss[:, 4 * T:4 * T + 4], v3(onsq[:, T % 2, :], 4), AX.X, ALU.add), s_("sq_reduced"))
                D(ts(oss, oss, 1.0 / DK, EPS, ALU.mult, ALU.add), s_("o_ms"))
                dve.wait_ge(s_("o_r"), w + 1)
                for T in range(NT):
                    y = v3(Y0[:, T, 512 * w:512 * w + 512], 4)
                    D(tt(y, y, bc_h(ors[:, 4 * T:4 * T + 4]), ALU.mult))

            HBf = HB.rearrange("p h t -> p (h t)")
            HQf = HQ.rearrange("p h t -> p (h t)")
            HKf = HK.rearrange("p h t -> p (h t)")

            def halves(ap, s):
                return ap.rearrange("p (b s) -> p b s", s=2 * s)

            def hgrn(step):
                if step[0] == "hdiag":
                    for T in range(NT):
                        tile_is_ready(dve, ("dg", T))
                        D.read(tt(v3(HAT[:, T, :], 4), v3(tile(("dg", T)), 4), bc_m(ident[:, :]), ALU.mult), ("dg", T))
                elif step[0] == "hlevel":
                    n = step[1]
                    s = LEVELS[n]
                    nb = 2048 // (2 * s)
                    b, e, p_ = halves(HBf, s), halves(LE, s), halves(LP, s)
                    ref = b[:, :, s - 1:s].broadcast_to([P, nb, s])
                    D(tt(e[:, :, 0:s], ref, b[:, :, 0:s], ALU.subtract))
                    D(tt(e[:, :, s:2 * s], b[:, :, s:2 * s], ref, ALU.subtract), s_("lv_args"))
                    dve.wait_ge(s_("lv_exp"), n + 1)
                    D(tt(p_[:, :, 0:s], halves(HKf, s)[:, :, 0:s], e[:, :, 0:s], ALU.mult))
                    D(tt(p_[:, :, s:2 * s], halves(HQf, s)[:, :, s:2 * s], e[:, :, s:2 * s], ALU.mult), s_("lp_ready"))
                    for T in range(NT):
                        tile_is_ready(dve, ("lv", n, T))
                        D.read(dve.copy_predicated(v3(HAT[:, T, :], 4), bc_m(lvmask[:, n, :]), v3(tile(("lv", n, T)), 4)), ("lv", n, T))
                elif step[0] == "hstate":
                    b = halves(HBf, CH // 2)
                    D(tt(halves(LE, CH // 2), b[:, :, CH - 1:CH].broadcast_to([P, 2048 // CH, CH]), b, ALU.subtract), s_("lv_args"))
                    dve.wait_ge(s_("lv_exp"), len(LEVELS) + 1)
                    D(tt(HKf, HKf, LE, ALU.mult), s_("hk_decayed"))
                    dve.wait_ge(s_("lv_exp"), len(LEVELS) + 2)
                    D(tt(HQf, HQf, LE, ALU.mult), s_("hq_decayed"))

            def hscan(c):
                D(tt(v3(Stmp[:, :], 4), v3(S[:, :], 4), bc_h(v3(LE, 4)[:, :, CH * c + CH - 1]), ALU.mult))
                tile_is_ready(dve, ("hs", c))
                D.read(tt(S[:, :], Stmp[:, :], tile(("hs", c)), ALU.add), ("hs", c))

            def dense_read_by_act(db, t):
                dve.wait_ge(dense_read["act"], evac_count(db, t))

            def evac(db):
                kind, which, c0 = BLOCKS[db]
                if which in ("q", "k", "v") :
                    dst = {"q": QF, "k": KF, "v": VF}[which]
                    for t in range(4):
                        g = 4 * db + t
                        w = [vec[:, 12 * j + g:12 * j + g + 1] for j in range(4)]
                        c, o = craw[:, t % 2, :], dst[:, t, :]
                        dense_read_by_act(db, t)
                        D(ts(o, c, w[3], None, ALU.mult))
                        for j in (2, 1):
                            d = 3 - j
                            D(stt(o[:, d:SEQ], c[:, 0:SEQ - d], w[j], o[:, d:SEQ], ALU.mult, ALU.add))
                        D(stt(o[:, 3:SEQ], c[:, 0:SEQ - 3], w[0], o[:, 3:SEQ], ALU.mult, ALU.add), s_("conv_done"))
                elif which == "hf":
                    for t in range(4):
                        dense_read_by_act(db, t)
                        D(ts(HB[:, t, :], HK[:, t, :], c1[:, t:t + 1], c2[:, t:t + 1], ALU.mult, ALU.add), s_("f_ready"))
                        D(ts(HK[:, t, :], HB[:, t, :], -1.0, 1.0, ALU.mult, ALU.add))
                    for t in range(4):
                        dve.wait_ge(s_("lf_ready"), t + 1)
                        D(dve.tensor_tensor_scan(HB[:, t, :], resetm[:, :], HQ[:, t, :], 0.0, ALU.mult, ALU.add), s_("b_ready"))
                elif which in ("z", "hg"):
                    wgt = gnw if which == "z" else hnw
                    w = int(which == "hg")
                    for t in range(4):
                        dense_read_by_act(db, t)
                        z = zt[:, t % 2, :]
                        y = Y0[:, t, 512 * w:512 * w + 512]
                        D(tt(v3(z, 4), v3(z, 4), bc_m(wgt[:, :]), ALU.mult))
                        D(tt(y, y, z, ALU.mult), s_("z_used"))
                elif kind == "odd_in" and which[0] in ("rq", "rk"):
                    dst = RQ if which[0] == "rq" else RK
                    dve.wait_ge(s_("ret_consts"), 48)
                    for hh in range(2):
                        dense_read_by_act(db, 2 * hh + 1)
                        D(tt(dst[:, hh, 0, :], rtmp[:, 0, :], cos_t, ALU.mult))
                        D(tt(rprod, rtmp[:, 1, :], sin_t, ALU.mult))
                        D(tt(dst[:, hh, 0, :], dst[:, hh, 0, :], rprod, ALU.subtract))
                        D(tt(dst[:, hh, 1, :], rtmp[:, 0, :], sin_t, ALU.mult))
                        D(tt(rprod, rtmp[:, 1, :], cos_t, ALU.mult), s_("rot_done"))
                        D(tt(dst[:, hh, 1, :], dst[:, hh, 1, :], rprod, ALU.add), s_("rot_ready"))
                elif kind == "odd_in" and which[0] == "rg":
                    h = which[1]
                    dve.wait_ge(s_("ro_r"), h + 1)
                    for t in range(4):
                        dense_read_by_act(db, t)
                        y = Y1[:, t, h * RDV:(h + 1) * RDV]
                        D(stt(y, y, ors[:, t:t + 1], gt[:, t % 2, :], ALU.mult, ALU.mult))
                        D(tt(y, y, rnw, ALU.mult), s_("g_used"))
                elif kind.endswith("out"):
                    for t in range(4):
                        dve.wait_ge(dense_ready, 4 * db + t + 1)
                        x = X[:, t, c0:c0 + 512]
                        D(tt(x, x, ps[:, t, :], ALU.add), dense_read["dve"])

            def score(h):
                dve.wait_ge(s_("dh_loaded"), 16 * (h + 1))
                if h > 0:
                    tile_is_ready(dve, ("ro", h - 1, NT - 1))
                for J in range(NT):
                    n = SEQ - P * J
                    tile_is_ready(dve, ("sc", h, J))
                    D.read(tt(RAT[:, J, 0:n], tile(("sc", h, J))[:, 0:n], DH[:, 0:n], ALU.mult), ("sc", h, J))

            def ro(h):
                tile_is_read(dve, ("ro", h, NT - 1))
                D(ts(oss[:, 0:4], oss[:, 0:4], 1.0 / RDV, EPS, ALU.mult, ALU.add), s_("ro_ms"))

            def pick_first(dst, eq):
                D(tt(eq, eq, bc_m(first4), ALU.mult))
                D(dve.tensor_reduce(mx2, eq, AX.X, ALU.max))
                D(tt(dst, eq, bc_h(mx2, 4), ALU.is_equal))

            def route(l):
                D(dve.memset(ar[:, 7168:9216], 0.0), s_("xg_cleared"))
                dve.wait_ge(s_("router_loaded"), 128 * (l + 1))
                D(dve.memset(ones, 1.0))
                D(dve.memset(onesrow, 1.0))
                dve.wait_ge(s_("r_logits"), l + 1)
                D(tt(lg, v3(ps[:, 7, 0:80], 4), bc_m(rb), ALU.add), s_("r_bank"))
                c, f = lg[:, :, 0:4], lg[:, :, 4:20]
                D(dve.tensor_reduce(mx, c, AX.X, ALU.max))
                D(tt(r_b, c, bc_h(mx, 4), ALU.is_equal))
                D(tt(r_a, c, bc_h(mx, 4), ALU.subtract), s_("r_cexp"))
                pick_first(gm, r_b)
                D(tt(r_c, f.rearrange("p T (g e) -> p T g e", g=4), gm.unsqueeze(3).broadcast_to([P, 4, 4, 4]), ALU.mult))
                D(dve.tensor_reduce(fs, r_c.rearrange("p T g e -> p T e g"), AX.X, ALU.add))
                D(dve.tensor_reduce(mx, fs, AX.X, ALU.max))
                D(tt(r_b, fs, bc_h(mx, 4), ALU.is_equal))
                pick_first(m1, r_b)
                D(stt(fs, m1, -1e30, fs, ALU.mult, ALU.add))
                D(dve.tensor_reduce(ed, fs, AX.X, ALU.max))
                D(tt(r_b, fs, bc_h(ed, 4), ALU.is_equal))
                pick_first(m2, r_b)
                D(tt(ed, ed, mx, ALU.subtract), s_("r_eexp"))
                for n, m in enumerate((m1, m2)):
                    D(tt(oh[n].rearrange("p T (g e) -> p T g e", g=4), gm.unsqueeze(3).broadcast_to([P, 4, 4, 4]),
                         m.unsqueeze(2).broadcast_to([P, 4, 4, 4]), ALU.mult))
                D(tt(anyh, oh[0], oh[1], ALU.add), s_("r_any"))
                dve.wait_ge(s_("r_exp"), 2 * l + 2)
                D(dve.tensor_reduce(gp, r_a, AX.X, ALU.add))
                D(ts(mx, ed, 1.0, None, ALU.add))
                D(tt(gp, gp, mx, ALU.mult))
                w = v3(w12, 4)
                D(dve.reciprocal(w[:, :, 0], gp))
                D(tt(w[:, :, 1], w[:, :, 0], ed, ALU.mult))
                dve.wait_ge(s_("r_pos"), l + 1)
                D(dve.tensor_copy(slotv, v3(ps[:, 7, 0:64], 4)))
                D(dve.tensor_copy(ncnt, ps[:, 7, 64:80]), s_("r_bank"))
                D(ts(ovc, ncnt, 128.0, None, ALU.is_gt))
                D(stt(ovc, ncnt, 256.0, ovc, ALU.is_gt, ALU.add))
                D(stt(ovc, ncnt, 384.0, ovc, ALU.is_gt, ALU.add))
                D(dve.tensor_tensor_scan(ovi, onesrow, ovc, 0.0, ALU.mult, ALU.add))
                D(tt(ovt, ovi, ovc, ALU.subtract))
                D(ts(ovt, ovt, 128.0, 128.0 * NE - 128.0, ALU.mult, ALU.add))
                D(tt(ovt, ovt, offs16, ALU.subtract))
                D(ts(tmp64, slotv, 128.0, None, ALU.is_ge))
                D(tt(tmp64, tmp64, bc_m(ovt), ALU.mult))
                D(tt(slotv, slotv, tmp64, ALU.add))
                D(tt(slotv, slotv, bc_m(offs16), ALU.add))
                for n in range(2):
                    D(tt(tmp64, oh[n], slotv, ALU.mult))
                    D(dve.tensor_reduce(v3(slotf, 4)[:, :, n], tmp64, AX.X, ALU.add))
                D(dve.tensor_copy(slots_u, slotf))
                D(tt(v3(cmp7, 7), bc_m(ovi, 7), iota8[:, 0:7].unsqueeze(2).broadcast_to([P, 7, 16]), ALU.is_le))
                D(dve.tensor_reduce(eidf[:, 0:7], v3(cmp7, 7), AX.X, ALU.add))
                D(ts(eidf[:, 0:7], eidf[:, 0:7], float(NE - 1), None, ALU.min))
                D(dve.tensor_copy(eidf[:, 7:8], ovi[:, 15:16]))
                D(dve.tensor_copy(eid[:, :], eidf[0:1, :]), s_("slots_known"))
                dve.wait_ge(s_("r_rows"), l + 1)
                D(dve.tensor_copy(idx[:, 1, :], ps[:, 7, 0:SLOT_TILES]), s_("r_bank"))
                D(ts(idx[:, 0, :], idx[:, 1, :], 1, None, ALU.logical_shift_right), s_("rows_known"))

            def xT_lo(l, e, g, par):
                dve.wait_ge(s_("xT_hi"), e * 2 + (34 * l + g + 1))
                tt(HTL[:, 2 * par + g, :], ps[:, 4 + g, :], HTH[:, 2 * par + g, :].bitcast(F32), ALU.subtract).then_inc(s_("xT_lo"), 1)

            def moe(l):
                m = MOE_PIECE[l]
                route(l)
                xT_lo(l, 0, 0, 0)
                xT_lo(l, 0, 1, 0)
                with dve.Fori(0, NE // 2) as it:
                    for par in range(2):
                        E = it * 2 + (16 * l + par)

                        def lo_in(j):
                            n = m + 6 * par + j
                            dve.wait_ge(hi_done, it * 12 + (n + 1))
                            tt(wl[:, n % NSPL, :, :], raw[:, n % NRAW, :, :], wh[:, n % NSPL, :, :].bitcast(F32),
                               ALU.subtract).then_inc(lo_dve, 1)

                        for j in (4, 5, 6):
                            lo_in(j)
                        dve.wait_ge(s_("silu_done"), E + 1)
                        tt(aact[:, par, :], sg[:, par, :], ps[:, par, FE:2 * FE], ALU.mult).then_inc(s_("act_done"), 1)
                        dve.wait_ge(s_("aT_hi"), E + 1)
                        tt(HTL[:, 4 + par, 0:256], ps[:, 6, 0:256], HTH[:, 4 + par, 0:256].bitcast(F32), ALU.subtract)\
                            .then_inc(s_("aT_lo"), 1)
                        lo_in(7)
                        for g in range(2):
                            xT_lo(l, it * 2 + (par + 1), g, 1 - par)
                        lo_in(8)
                        lo_in(9)
                n = overflow_flag(dve, l)
                with dve.If(n > 0):
                    with dve.Fori(0, 7) as j:
                        dve.wait_ge(s_(f"ov_silu{l}"), j + 1)
                        tt(aact[:, 0, :], sg[:, 0, :], ps[:, 0, FE:2 * FE], ALU.mult).then_inc(s_(f"ov_act{l}"), 1)
                for T in range(NT):
                    dve.wait_ge(s_(f"yp_loaded{T % 2}"), 32 * l + 16 * (T // 2 + 1))
                    D(stt(X[:, T, :], YP[:, T % 2, 0, :], w12[:, 2 * T:2 * T + 1], X[:, T, :], ALU.mult, ALU.add))
                    D(stt(X[:, T, :], YP[:, T % 2, 1, :], w12[:, 2 * T + 1:2 * T + 2], X[:, T, :], ALU.mult, ALU.add), s_(f"moe_added{l}"))

            for sm, n in ((s_("act_done"), 2), (s_("xT_lo"), 2), (s_("aT_lo"), 1), (lo_dve, 4)):
                for _ in range(n):
                    dve.nop().then_inc(sm, 1)
            for step in SCHEDULE:
                k = step[0]
                if k == "consts":
                    consts()
                elif k == "norm":
                    norm(step[1])
                elif k == "ba":
                    gate_inputs()
                elif k == "gates":
                    gates()
                elif k == "tok":
                    tok(step[1], step[2])
                elif k == "l2":
                    l2()
                elif k == "gdn_chunks":
                    gdn_chunks(step[1])
                elif k == "scan":
                    scan(step[1])
                elif k == "onorm":
                    onorm(step[1])
                elif k in ("hdiag", "hlevel", "hstate"):
                    hgrn(step)
                elif k == "hscan":
                    hscan(step[1])
                elif k == "evac":
                    evac(step[1])
                elif k == "yT":
                    for T in range(NT):
                        lo_tiles(("yT", step[1], step[2], T), T)
                elif k == "score":
                    score(step[1])
                elif k == "ro":
                    ro(step[1])
                elif k == "moe":
                    moe(step[1])

        @block.tensor
        def _(pe):
            mm = nc.tensor.matmul
            tr = nc.tensor.transpose

            def open_tile(name):
                n = SIDE_AT[name]
                if n >= 4:
                    tile_is_read(pe, SIDE[n - 4][0])
                return tile(name)

            def done(ins):
                ins.then_inc(tile_ready, 1)

            def four(name, f):
                t = open_tile(name)
                for h in range(NH):
                    ins = f(t[:, cols(h)], h)
                done(ins)

            def norm(n):
                for T in range(NT):
                    pe.wait_ge(s_("h_ready"), 4 * n + T + 1)
                    for g in range(2):
                        t = open_tile(("hT", n, T, g))
                        for j in range(4):
                            k = 4 * g + j
                            ins = tr(t[:, cols(j)], htok(n)[:, T % 2, k:DM:KD], ident[:, :])
                        done(ins)

            def yT(l, kh):
                for T in range(NT):
                    if l == 0:
                        pe.wait_ge(s_("z_used"), 4 + T + 1)
                    else:
                        pe.wait_ge(s_("g_used"), 4 * (2 * kh + 1) + T + 1)
                    for g in range(2):
                        t = open_tile(("yT", l, kh, T, g))
                        for j in range(4):
                            c = (4 * g + j) * P
                            src = Y0[:, T, c:c + P] if l == 0 else Y1[:, T, kh * DM + c:kh * DM + c + P]
                            ins = tr(t[:, cols(j)], src, ident[:, :])
                        done(ins)

            def ba_product():
                tile_is_read(pe, ("hT", 0, NT - 1, 1))
                pe.wait_ge(s_("wba_lo"), 1)
                t = open_tile("ba")
                for T in range(NT):
                    for k in range(KD):
                        ins = mm3(t[:, 8 * T:8 * T + 8], HTH[:, k, cols(T)], HTL[:, k, cols(T)], wba_h[:, k, :], wba_l[:, k, :],
                                  k == 0, k == KD - 1)
                done(ins)

            def hT_ready(db):
                last = {0: ("hT", 0), 8: ("yT", 0, 0), 10: ("hT", 2), 22: ("yT", 1, 0), 24: ("yT", 1, 1)}.get(db)
                if last:
                    tile_is_read(pe, last + (NT - 1, 1))

            def piece(db, kp):
                i = first_piece(db) + kp
                sl = i % NSPL
                kind, which, _c = BLOCKS[db]
                if kp == 0:
                    hT_ready(db)
                pe.wait_ge(hi_done, i + 1)
                wait_lo(pe, i)
                feature = which in ("q", "k", "v", "hf", "hq") or (kind == "odd_in" and which[0] in ("rq", "rk"))
                for t in range(NT):
                    if kp == 0 and db > 0:
                        pe.wait_ge(dense_read[evac_engine(db - 1)], evac_count(db - 1, t))
                    for k2 in range(2):
                        k = 2 * kp + k2
                        first, last = kp == 0 and k2 == 0, kp == 3 and k2 == 1
                        if feature:
                            c = cols(t) if kind == "even_in" else slice(256 * (t // 2) + t % 2, 256 * (t // 2 + 1), 2)
                            ins = mm3(ps[:, t, :], wh[:, sl, k2, c], wl[:, sl, k2, c], HTH[:, k, :], HTL[:, k, :], first, last)
                        else:
                            ins = mm3(ps[:, t, :], HTH[:, k, cols(t)], HTL[:, k, cols(t)], wh[:, sl, k2, :], wl[:, sl, k2, :], first, last)
                    if kp == 3:
                        ins.then_inc(dense_ready, 1)
                if kp < 3:
                    ins.then_inc(piece_used, 1)

            def tok(nm, T):
                src, n = {"q": (QF, 4), "k": (KF, 8), "v": (VF, 12)}[nm]
                pe.wait_ge(s_("conv_silu"), n)
                four(("tok", nm, T), lambda o, h: tr(o, src[:, h, cols(T)], ident[:, :]))

            def gates():
                pe.wait_ge(s_("g_ready"), 1)
                done(mm(open_tile("gc")[:, 0:16], U[:, :], gg, start=True, stop=True))

            def l2():
                for T in range(NT):
                    pe.wait_ge(s_("qk_normed"), 2 * T + 2)
                    four(("qb", T), lambda o, h: tr(o, Y0[:, T, cols(h)], ident[:, :]))
                    four(("kb", T), lambda o, h: tr(o, KT[:, T, cols(h)], ident[:, :]))

            def gdn_chunks(pr):
                Ts = (2 * pr, 2 * pr + 1)

                def prod(name, T, lh, rh):
                    q = T % 2
                    four(name, lambda o, h: mm(o, PA[lh][:, q, cols(h)], PA[rh][:, q, cols(h)], start=True, stop=True))

                for T in Ts:
                    tile_is_read(pe, ("qb", T))
                    tile_is_read(pe, ("kb", T))
                    four(("Gb", T), lambda o, h: mm(o, gg[:, 4 * T + h:4 * T + h + 1].broadcast_to([P, P]), U[:, :], start=True, stop=True))
                    four(("KK", T), lambda o, h: mm(o, KF[:, h, cols(T)], KF[:, h, cols(T)], start=True, stop=True))
                    four(("KQ", T), lambda o, h: mm(o, KF[:, h, cols(T)], QF[:, h, cols(T)], start=True, stop=True))
                    tile_is_read(pe, ("KK", T))
                    four(("DT", T), lambda o, h: tr(o, PA[0][:, T % 2, cols(h)], ident[:, :]))
                for T in Ts:
                    tile_is_read(pe, ("DT", T))
                    prod(("P2", T), T, 4, 0)
                    prod(("P2T", T), T, 0, 4)
                for r in (1, 2, 3):
                    for T in Ts:
                        if r == 1:
                            pe.wait_ge(s_("x1_ready"), T + 1)
                            tile_is_read(pe, ("P2T", T))
                        else:
                            tile_is_read(pe, ("XT", r - 1, T))
                            tile_is_read(pe, ("P", 1, T) if r == 2 else ("PT", 2, T))
                        prod(("X", r, T), T, 6, 7)
                        prod(("XT", r, T), T, 7, 6)
                        if r < 3:
                            prod(("PT", r, T), T, 5, 6)
                        if r == 1:
                            prod(("P", r, T), T, 6, 5)
                for T in Ts:
                    tile_is_read(pe, ("XT", 3, T))
                    prod(("B", T), T, 8, 3)
                    prod(("BT", T), T, 3, 8)
                for T in Ts:
                    tile_is_read(pe, ("BT", T))
                    prod(("B2", T), T, 6, 5)
                for T in Ts:
                    tile_is_read(pe, ("B2", T))
                    pe.wait_ge(s_("n1_ready"), T + 1)
                    prod(("N2", T), T, 4, 0)
                for T in Ts:
                    tile_is_read(pe, ("N2", T))
                    prod(("IT", T), T, 7, 1)
                for T in Ts:
                    tile_is_read(pe, ("IT", T))
                    pe.wait_ge(s_("vk_ready"), T + 1)
                    prod(("u", T), T, 8, 9)
                    prod(("wT", T), T, 10, 8)

            def scan(c):
                T, p0 = c // 2, 64 * (c % 2)
                r, tc = slice(p0, p0 + 64), slice(P * T + p0, P * T + p0 + 64)
                tile_is_read(pe, ("wT", T))
                pe.wait_ge(s_("vk_ready"), NT)
                if c > 0:
                    tile_is_read(pe, ("ss", c - 1))
                t = open_tile(("sv", c))
                for h in range(NH):
                    ins = mm(t[r, cols(h)], KF[:, h, tc], S[:, cols(h)], start=True, stop=True)
                done(ins)
                t = open_tile(("so", c))
                tile_is_read(pe, ("sv", c))
                for h in range(NH):
                    mm(t[r, cols(h)], QF[:, h, tc], S[:, cols(h)], start=True, stop=False)
                    ins = mm(t[r, cols(h)], AT0[r, T, P * h + p0:P * h + p0 + 64], vnew[r, cols(h)], start=False, stop=True)
                done(ins)
                t = open_tile(("ss", c))
                for h in range(NH):
                    ins = mm(t[:, cols(h)], KT[r, T, cols(h)], vnew[r, cols(h)], start=True, stop=True)
                done(ins)

            def hgrn(step):
                if step[0] == "hdiag":
                    pe.wait_ge(dense_read["act"], evac_count(4, 3))
                    pe.wait_ge(s_("b_ready"), 4)
                    for T in range(NT):
                        four(("dg", T), lambda o, h: mm(o, HK[:, h, cols(T)], HQ[:, h, cols(T)], start=True, stop=True))
                elif step[0] == "hlevel":
                    pe.wait_ge(s_("lp_ready"), step[1] + 1)
                    lp = v3(LP, 4)
                    for T in range(NT):
                        four(("lv", step[1], T), lambda o, h: mm(o, lp[:, h, cols(T)], lp[:, h, cols(T)], start=True, stop=True))
                elif step[0] == "hstate":
                    pe.wait_ge(s_("hk_decayed"), 1)
                    for T in range(NT):
                        four(("kd", T), lambda o, h: tr(o, HK[:, h, cols(T)], ident[:, :]))

            def hscan(c):
                T, p0 = c // 2, 64 * (c % 2)
                r, tc = slice(p0, p0 + 64), slice(P * T + p0, P * T + p0 + 64)
                pe.wait_ge(s_("hq_decayed"), 1)
                pe.wait_ge(s_("scan_done"), 1)
                tile_is_read(pe, ("kd", T))
                if c > 0:
                    tile_is_read(pe, ("hs", c - 1))
                t = open_tile(("ho", c))
                for h in range(NH):
                    mm(t[r, cols(h)], HQ[:, h, tc], S[:, cols(h)], start=True, stop=False)
                    ins = mm(t[r, cols(h)], HAT[r, T, P * h + p0:P * h + p0 + 64], HI[r, T, cols(h)], start=False, stop=True)
                done(ins)
                t = open_tile(("hs", c))
                for h in range(NH):
                    ins = mm(t[:, cols(h)], KDT[r, T, cols(h)], HI[r, T, cols(h)], start=True, stop=True)
                done(ins)

            def score(h):
                pe.wait_ge(s_("rot_ready"), 4 * (h // 2) + 3 + h % 2)
                for J in range(NT):
                    t = open_tile(("sc", h, J))
                    n = SEQ - P * J
                    mm(t[:, 0:n], RK[:, h % 2, 0, cols(J)], RQ[:, h % 2, 0, P * J:SEQ], start=True, stop=False)
                    done(mm(t[:, 0:n], RK[:, h % 2, 1, cols(J)], RQ[:, h % 2, 1, P * J:SEQ], start=False, stop=True))

            def ro(h):
                tile_is_read(pe, ("sc", h, NT - 1))
                pe.wait_ge(dense_read["act"], evac_count([b for b, x in enumerate(BLOCKS) if x[1] == ("rv", h)][0], 3))
                for T in range(NT):
                    t = open_tile(("ro", h, T))
                    for J in range(T + 1):
                        ins = mm(t, RAT[:, J, P * (T - J):P * (T - J) + P], RV[:, h % 2, J, :], start=J == 0, stop=J == T)
                    done(ins)

            def xT(l, e, par):
                pe.wait_ge(s_(f"xg_loaded{par}"), e * 8 + (144 * l + (16 if par == 0 else 8)))
                for g in range(2):
                    pe.wait_ge(s_("xT_lo"), e * 2 + (34 * l + g + 1))
                    for j in range(4):
                        ins = tr(ps[:, 4 + g, cols(j)], xg[:, par, 4 * g + j:DM:KD], ident[:, :])
                    ins.then_inc(s_("xT_ready"), 1)

            def moe(l):
                m = MOE_PIECE[l]
                for t in range(4):
                    tile_is_read(pe, SIDE[SIDE_AT[("hT", 2 * l + 1, NT - 1, 1)] - t][0])
                pe.wait_ge(s_("router_loaded"), 128 * (l + 1))
                for T in range(NT):
                    for k in range(KD):
                        ins = mm(ps[:, 7, 20 * T:20 * T + 20], hTf[:, k, cols(T)], rw[:, k, :], start=k == 0, stop=k == KD - 1)
                ins.then_inc(s_("r_logits"), 1)
                pe.wait_ge(s_("r_any"), l + 1)
                for T in range(NT):
                    ins = mm(ps[:, 7, 16 * T:16 * T + 16], Lst, anyh[:, T, :], start=True, stop=T == 0)
                    for q in range(T):
                        ins = mm(ps[:, 7, 16 * T:16 * T + 16], ones, anyh[:, q, :], start=False, stop=q == T - 1)
                for T in range(NT):
                    ins = mm(ps[:, 7, 64:80], ones, anyh[:, T, :], start=T == 0, stop=T == NT - 1)
                ins.then_inc(s_("r_pos"), 1)
                pe.wait_ge(s_(f"slotrow_loaded{l}"), 16)
                pe.wait_ge(s_("r_bank"), 3 * l + 2)
                tr(ps[:, 7, 0:SLOT_TILES], slotrow, ident[0:SLOT_TILES, 0:SLOT_TILES]).then_inc(s_("r_rows"), 1)
                xT(l, 0, 0)
                with pe.Fori(0, NE // 2) as it:
                    for par in range(2):
                        E = it * 2 + (16 * l + par)

                        def parts(j):
                            n = m + 6 * par + j
                            pe.wait_ge(hi_done, it * 12 + (n + 1))
                            if j < 4 and par == 0:
                                pe.wait_ge(lo_pool, lo_count(m + j))
                                pe.wait_ge(lo_dve, it * 12 + (lo_count(m + 12 + j) - 12))
                            else:
                                pe.wait_ge(lo_dve, it * 12 + lo_count(n))
                            return n % NSPL

                        pe.wait_ge(s_("act_done"), E + 1)
                        pe.wait_ge(s_("xT_lo"), E * 2 + (2 * l + 4))
                        for j in range(4):
                            sl = parts(j)
                            for k2 in range(2):
                                k = 2 * j + k2
                                a_ = 2 * par + k // 4
                                ins = mm3(ps[:, par, :], HTH[:, a_, cols(k % 4)], HTL[:, a_, cols(k % 4)], wh[:, sl, k2, :], wl[:, sl, k2, :],
                                          k == 0, k == KD - 1)
                            ins.then_inc(s_("gu_used") if j < 3 else s_("gu_ready"), 1)
                        pe.wait_ge(s_("act_done"), E + 3)
                        pe.wait_ge(s_("aT_lo"), E + 1)
                        for k in range(2):
                            ins = tr(ps[:, 6, cols(k)], aact[:, par, cols(k)], ident[:, :])
                        ins.then_inc(s_("aT_ready"), 1)
                        xT(l, it * 2 + (par + 1), 1 - par)
                        pe.wait_ge(s_("aT_lo"), E + 2)
                        for hf in range(2):
                            sl = parts(4 + hf)
                            pe.wait_ge(s_("y_read"), E * 2 + (hf + 1))
                            for k in range(2):
                                ins = mm3(ps[:, 2 + hf, :], HTH[:, 4 + par, cols(k)], HTL[:, 4 + par, cols(k)], wh[:, sl, k, :], wl[:, sl, k, :],
                                          k == 0, k == 1)
                            ins.then_inc(s_("y_ready"), 1)
                pe.wait_ge(s_("y_read"), 32 * (l + 1) + 2)
                n = overflow_flag(pe, l)
                with pe.If(n > 0):
                    pe.wait_ge(s_("xT_lo"), 34 * (l + 1) + 2)
                    with pe.Fori(0, 7) as j:
                        pe.wait_ge(s_(f"ov_x{l}"), j * 16 + 16)
                        pe.wait_ge(s_(f"ov_w{l}"), j * 32 + 32)
                        for g in range(2):
                            for q in range(4):
                                ins = tr(ps[:, 4 + g, cols(q)], xg[:, 0, 4 * g + q:DM:KD], ident[:, :])
                            ins.then_inc(s_(f"ov_xT{l}"), 1)
                        pe.wait_ge(s_(f"ov_xTr{l}"), j * 2 + 2)
                        for k in range(KD):
                            ins = mm(ps[:, 0, :], hTf[:, k, 0:P], ovWg[:, k, :], start=k == 0, stop=k == KD - 1)
                        ins.then_inc(s_(f"ov_gu{l}"), 1)
                        pe.wait_ge(s_(f"ov_act{l}"), j + 1)
                        for k in range(2):
                            ins = tr(ps[:, 6, cols(k)], aact[:, 0, cols(k)], ident[:, :])
                        ins.then_inc(s_(f"ov_aT{l}"), 1)
                        pe.wait_ge(s_(f"ov_aTr{l}"), j + 1)
                        for hf in range(2):
                            for k in range(2):
                                ins = mm(ps[:, 2 + hf, :], hTf[:, k, P:2 * P], ovWd[:, k, 512 * hf:512 * hf + 512], start=k == 0, stop=k == 1)
                            ins.then_inc(s_(f"ov_yp{l}"), 1)

            pe.wait_ge(s_("consts_loaded"), 16 * 13)
            for step in SCHEDULE:
                k = step[0]
                if k == "consts":
                    done(tr(open_tile("vec")[:, 0:60], raw_vec[0:60, :], ident[0:60, 0:60]))
                elif k == "norm" and step[1] < 4:
                    norm(step[1])
                elif k == "ba":
                    ba_product()
                elif k == "piece":
                    piece(step[1], step[2])
                elif k == "tok":
                    tok(step[1], step[2])
                elif k == "gates":
                    gates()
                elif k == "l2":
                    l2()
                elif k == "gdn_chunks":
                    gdn_chunks(step[1])
                elif k == "scan":
                    scan(step[1])
                elif k in ("hdiag", "hlevel", "hstate"):
                    hgrn(step)
                elif k == "hscan":
                    hscan(step[1])
                elif k == "yT":
                    yT(step[1], step[2])
                elif k == "score":
                    score(step[1])
                elif k == "ro":
                    ro(step[1])
                elif k == "moe":
                    moe(step[1])


def shape_constants():
    i = np.arange(P)
    same = i[:, None] // CH == i[None, :] // CH
    c = {"c_ident": np.eye(P), "c_U": same & (i[:, None] <= i[None, :])}
    b16 = i[:, None] // 16 == i[None, :] // 16
    c["c_m16"] = b16 & (i[:, None] > i[None, :])
    c["c_moff"] = same & ~b16 & (i[:, None] > i[None, :])
    c["c_Lst"] = i[:, None] < i[None, :]
    c["c_reset"] = np.broadcast_to(np.arange(SEQ) % CH != 0, (P, SEQ))
    T, j = np.arange(NT), np.arange(2)
    c["c_tok"] = (2 * (P * T[None, :, None] + i[:, None, None]) + j[None, None, :]).reshape(P, 8)
    c["c_first"] = np.broadcast_to(np.array([4, 3, 2, 1]), (P, 4))
    c["c_iota"] = np.broadcast_to(np.concatenate([np.arange(8), P * np.arange(NE)]), (P, 24))
    f = np.float32
    inv = f(1.0) / (f(10000.0) ** np.linspace(0.0, 1.0, RDK // 2, dtype=f))
    ang = (np.arange(SEQ, dtype=f)[None, :] * inv.astype(f)[:, None]).astype(f).astype(np.float64)
    c["c_cos"], c["c_sin"] = np.cos(ang), np.sin(ang)
    lg = np.log(1.0 - 2.0 ** (-5.0 - np.arange(NH)))
    rel = np.arange(SEQ)[None, :] - i[:, None]
    c["c_decay"] = np.where(rel >= 0, np.exp(np.maximum(rel, 0) * lg[:, None, None]), 0.0) * RDK ** -0.5
    c = {k: np.ascontiguousarray(v, dtype=np.float32) for k, v in c.items()}
    lv = [(i[:, None] // (2 * s) == i[None, :] // (2 * s)) & (i[:, None] % (2 * s) < s) & (i[None, :] % (2 * s) >= s) for s in LEVELS]
    c["c_lv"] = np.ascontiguousarray(np.stack(lv, 1), dtype=np.float32)
    return c


_INS = ['x', 'norm_mix_w', 'norm_ffn_w', 'even_w_in', 'gdn_conv_w', 'gdn_a_log', 'gdn_dt_bias', 'gdn_norm_w', 'hgrn_lb_logits',
        'hgrn_norm_w', 'even_w_out', 'odd_w_in', 'ret_norm_w', 'odd_w_out', 'router_c_w', 'router_c_b', 'router_f_w',
        'router_f_b', 'moe_w_gate_up', 'moe_w_down', 'final_norm_w']


def kernel(**inputs):
    import concourse.bacc as _bacc
    from concourse.bass_utils import run_bass_kernel_spmd as _run

    nc = _bacc.Bacc("TRN2", target_bir_lowering=False, num_devices=1)
    arrays, aps = {}, {}
    for name, v in [(n, inputs[n]) for n in _INS] + sorted(shape_constants().items()):
        v = np.ascontiguousarray(v)
        arrays[f"in_{name}_dram"] = v
        aps[name] = nc.dram_tensor(f"in_{name}_dram", v.shape, mybir.dt.from_np(v.dtype), kind="ExternalInput").ap()
    out = nc.dram_tensor("out_0_dram", (1, SEQ, DM), F32, kind="ExternalOutput").ap()
    build(nc, aps, out)
    r = _run(nc, [arrays], core_ids=[0])
    return r.results[0]["out_0_dram"]
```

```python
from contextlib import ExitStack

import concourse.bass as bass
from concourse import mybir
import numpy as np

F32 = mybir.dt.float32
F32R = mybir.dt.float32r
I32 = mybir.dt.int32
I8 = mybir.dt.int8
U32 = mybir.dt.uint32
ALU = mybir.AluOpType
ACT = mybir.ActivationFunctionType
AX = mybir.AxisListType

P = 128
SEQ = 512
DM = 1024
NT = SEQ // P
KD = DM // P
NH = 4
DK = 128
CH = 64
NC = SEQ // CH
RDV = 512
RDK = 256
NE = 16
NG = 4
EPG = 4
FE = 256
EPS = 1e-6
NRAW = 6
NSPL = 4
SLOT_TILES = NE + 7
EMPTY = 4096.0
LEVELS = (32, 16, 8, 4, 2, 1)

EVEN_COL = {"q": 0, "k": 512, "v": 1024, "z": 1536, "hq": 2056, "hf": 2568, "hi": 3080, "hg": 3592}
BLOCKS = [("even_in", n, EVEN_COL[n]) for n in ("q", "k", "v", "hf", "hq", "hi", "z", "hg")]
BLOCKS += [("even_out", 0, 0), ("even_out", 0, 512)]
for pair in range(2):
    BLOCKS += [("odd_in", ("rq", pair), 512 * pair), ("odd_in", ("rk", pair), 1024 + 512 * pair),
               ("odd_in", ("rv", 2 * pair), 2048 + 1024 * pair), ("odd_in", ("rv", 2 * pair + 1), 2560 + 1024 * pair),
               ("odd_in", ("rg", 2 * pair), 4096 + 1024 * pair), ("odd_in", ("rg", 2 * pair + 1), 4608 + 1024 * pair)]
BLOCKS += [("odd_out", kh, c) for kh in range(2) for c in (0, 512)]
MOE_AT = (10, 26)
MOE_PIECE = (4 * 10, 4 * 26 + 6 * NE)
NPIECE = 4 * len(BLOCKS) + 12 * NE


def first_piece(db):
    return 4 * db + (6 * NE if db >= MOE_AT[0] else 0)


def rot_index(db):
    return [b for b, (_, w, _) in enumerate(BLOCKS) if isinstance(w, tuple) and w[0] in ("rq", "rk")].index(db)


def evac_engine(db):
    return "dve" if BLOCKS[db][0].endswith("out") else "act"


def evac_count(db, t):
    return 4 * sum(evac_engine(b) == evac_engine(db) for b in range(db)) + t + 1


def lo_by_dve(i):
    return any(m + 4 <= i < m + 6 * NE for m in MOE_PIECE)


def lo_count(i):
    return sum(lo_by_dve(j) == lo_by_dve(i) for j in range(i + 1)) + 4 * lo_by_dve(i)


def schedule():
    s = [("norm", 0), ("consts",), ("ba",)]

    def block(db, side=((), (), (), ())):
        for kp in range(4):
            s.append(("piece", db, kp))
            s.extend(side[kp])
        s.append(("evac", db))

    block(0)
    s.append(("ba_tok",))
    block(1)
    block(2, ([("tok", "q", T) for T in range(NT)], [("gates",)], [("tok", "k", T) for T in range(NT)], ()))
    s.extend(("tok", "v", T) for T in range(NT))
    s.append(("l2",))
    for pr in range(2):
        s.append(("gdn_chunks", pr))
    scan = [[("scan", c)] for c in range(NC)]
    block(3, ((), scan[0], scan[1], scan[2]))
    block(4, ((), scan[3], scan[4], scan[5]))
    block(5, ((), scan[6], scan[7], [("onorm", 0)]))
    block(6, ((), [("hdiag",)], [("hlevel", 0)], [("hlevel", 1)]))
    block(7, ([("hlevel", 2)], [("hlevel", 3)], [("hlevel", 4)], [("hlevel", 5)]))
    evac7 = s.pop()
    s.append(("hstate",))
    s.extend(("hscan", c) for c in range(NC))
    s.append(("onorm", 1))
    s.append(evac7)
    s.append(("yT", 0, 0))
    block(8)
    block(9)
    s.append(("norm", 1))
    s.append(("moe", 0))
    s.append(("norm", 2))
    for pair in range(2):
        b = 10 + 6 * pair
        h0, h1 = 2 * pair, 2 * pair + 1
        block(b)
        block(b + 1)
        block(b + 2)
        block(b + 3, ((), [("score", h0)], [("ro", h0)], ()))
        block(b + 4, ((), [("score", h1)], (), ()))
        s.append(("ro", h1))
        block(b + 5)
    for kh in range(2):
        s.append(("yT", 1, kh))
        block(22 + 2 * kh)
        block(23 + 2 * kh)
    s.append(("norm", 3))
    s.append(("moe", 1))
    s.append(("norm", 4))
    return s


def side_tiles(step):
    k = step[0]
    if k == "consts":
        return [("vec", "dve")]
    if k == "norm" and step[1] < 4:
        who = "act" if step[1] in (1, 3) else "dve"
        return [(("hT", step[1], T, g), who) for T in range(NT) for g in range(2)]
    if k == "yT":
        return [(("yT", step[1], step[2], T, g), "dve") for T in range(NT) for g in range(2)]
    if k == "ba":
        return [("ba", "dve")]
    if k == "ba_tok":
        return [("ba_tok", "dve")]
    if k == "tok":
        return [(("tok", step[1], step[2]), "act")]
    if k == "gates":
        return [("gc", "dve")]
    if k == "l2":
        return [((n, T), "act" if n == "qb" else "dve") for T in range(NT) for n in ("qb", "kb")]
    if k == "gdn_chunks":
        Ts = (2 * step[1], 2 * step[1] + 1)
        out = []
        for T in Ts:
            out += [(("Gb", T), "act"), (("KK", T), "dve"), (("KQ", T), "dve"), (("DT", T), "act")]
        for T in Ts:
            out += [(("P2", T), "act"), (("P2T", T), "act")]
        for r in (1, 2):
            for T in Ts:
                out += [(("X", r, T), "dve"), (("XT", r, T), "dve"), (("PT", r, T), "act")]
                if r == 1:
                    out += [(("P", r, T), "act")]
        for T in Ts:
            out += [(("X", 3, T), "dve"), (("XT", 3, T), "dve")]
        for T in Ts:
            out += [(("B", T), "act"), (("BT", T), "act")]
        for T in Ts:
            out += [(("B2", T), "act")]
        for T in Ts:
            out += [(("N2", T), "dve")]
        for T in Ts:
            out += [(("IT", T), "act")]
        for T in Ts:
            out += [(("u", T), "act"), (("wT", T), "act")]
        return out
    if k == "scan":
        c = step[1]
        return [(("sv", c), "dve"), (("so", c), "act"), (("ss", c), "dve")]
    if k == "hdiag":
        return [(("dg", T), "dve") for T in range(NT)]
    if k == "hlevel":
        return [(("lv", step[1], T), "dve") for T in range(NT)]
    if k == "hstate":
        return [(("kd", T), "act") for T in range(NT)]
    if k == "hscan":
        return [(("ho", step[1]), "act"), (("hs", step[1]), "dve")]
    if k == "score":
        return [(("sc", step[1], J), "dve") for J in range(NT)]
    if k == "ro":
        return [(("ro", step[1], T), "act") for T in range(NT)]
    return []


SCHEDULE = schedule()
SIDE = [t for st in SCHEDULE for t in side_tiles(st)]
SIDE_AT = {name: n for n, (name, _) in enumerate(SIDE)}
SIDE_READ = {}
for _n, (_name, _who) in enumerate(SIDE):
    SIDE_READ[_name] = sum(w == _who for _, w in SIDE[:_n + 1])


def build(nc, a, out):
    ctx = ExitStack()
    with ctx:
        def sb(name, shape, dt=F32):
            return ctx.enter_context(nc.sbuf_tensor(name, shape, dt))

        def sem(name):
            return ctx.enter_context(nc.semaphore(name))

        hs_dram = [nc.dram_tensor(f"hs{l}", (SEQ, DM), F32, kind="Internal").ap() for l in range(2)]
        y2_dram = [nc.dram_tensor(f"y2{l}", (2 * SEQ, DM), F32, kind="Internal").ap() for l in range(2)]

        raw = sb("raw", [P, NRAW, 2, 512])
        wh = sb("wh", [P, NSPL, 2, 512], F32R)
        wl = sb("wl", [P, NSPL, 2, 512], F32R)
        X = sb("x", [P, NT, DM])
        HTH = sb("hT_hi", [P, KD, SEQ], F32R)
        HTL = sb("hT_lo", [P, KD, SEQ], F32R)
        ident = sb("ident", [P, P])
        U = sb("cum_upper", [P, P])
        m16 = sb("mask16", [P, P])
        moff = sb("mask_off", [P, P])
        lvmask = sb("level_masks", [P, len(LEVELS), P], I8)
        resetm = sb("reset", [P, SEQ])
        vec = sb("vec", [P, 60])
        small = sb("small", [P, 420])
        wba_h = sb("wba_hi", [P, KD, 8], F32R)
        wba_l = sb("wba_lo", [P, KD, 8], F32R)
        S = sb("state", [P, 512])
        Stmp = sb("state_decayed", [P, 512])
        vnew = sb("vnew", [P, 512])
        gnw = sb("gdn_w", [P, P])
        hnw = sb("hgrn_w", [P, P])
        ar = sb("arena", [P, 22528])
        idx = sb("slot_rows", [P, 2, SLOT_TILES], I32)
        cur = sb("cur_rows", [P, 4], U32)
        eid = sb("overflow_expert", [1, 8], I32)
        ps = ctx.enter_context(nc.psum_tensor("ps", [P, 8, 512], F32))

        def reg(off, n):
            return ar[:, off:off + n]

        def v3(ap, k):
            return ap.rearrange("p (k n) -> p k n", k=k)

        ss = small[:, 0:4]
        ms = small[:, 4:8]
        rs = small[:, 8:12]
        mhalf = small[:, 12:44]
        ba = v3(small[:, 44:76], 4)
        beta = small[:, 76:92]
        gg = small[:, 92:108]
        gc = small[:, 108:124]
        egc = small[:, 124:140]
        bege = small[:, 140:156]
        kde = small[:, 156:172]
        egl = v3(small[:, 172:204], 8)
        dtb = small[:, 204:208]
        alog = small[:, 208:212]
        ssn = small[:, 212:244]
        rn = small[:, 244:276]
        lbt = small[:, 276:300]
        c1 = small[:, 300:304]
        c2 = small[:, 304:308]
        zsp = small[:, 308:324]
        esp = small[:, 324:340]
        spt = small[:, 340:356]
        oss = small[:, 356:372]
        ors = small[:, 372:388]
        lbs = small[:, 388:404]

        QF, KF, VF = (v3(reg(2048 * n, 2048), 4) for n in range(3))
        KT, VT = (v3(reg(2048 * n, 2048), 4) for n in (3, 4))
        AT0 = v3(reg(4096, 2048), 4)
        Y0 = v3(reg(10240, 4096), 4)
        craw = v3(reg(14336, 1024), 2)
        sqt = v3(reg(15360, 1024), 2)
        HQ, HB, HK = (v3(reg(14336 + 2048 * n, 2048), 4) for n in range(3))
        HI = v3(reg(20480, 2048), 4)
        zt = v3(reg(6144, 1024), 2)
        PA = [v3(reg(14336 + 1024 * n, 1024), 2) for n in range(8)] + \
             [v3(reg(10240 + 1024 * n, 1024), 2) for n in range(4)]
        LE = reg(0, 2048)
        LP = reg(2048, 2048)
        HAT = v3(reg(4096, 2048), 4)
        KDT = v3(reg(8192, 2048), 4)
        onsq = v3(reg(7168, 1024), 2)
        raw_vec = reg(21000, 128)
        wba_raw = v3(reg(21200, 64), 8)
        lv_raw = v3(reg(21500, len(LEVELS) * P), len(LEVELS))
        baT = ar[0:8, 20480:20992]
        Y1 = v3(reg(0, 8192), 4)
        RQ = reg(8192, 2048).rearrange("p (h c t) -> p h c t", h=2, c=2)
        RK = reg(10240, 2048).rearrange("p (h c t) -> p h c t", h=2, c=2)
        RV = reg(12288, 4096).rearrange("p (h j n) -> p h j n", h=2, j=4)
        RAT = v3(reg(16384, 2048), 4)
        cos_t = reg(18432, 512)
        sin_t = reg(18944, 512)
        DH = reg(19456, 512)
        rtmp = v3(reg(19968, 1024), 2)
        gt = v3(reg(20992, 1024), 2)
        rprod = S[:, :]
        rnw = Stmp[:, :]
        rjunk = vnew[:, :]

        def htok(n):
            return v3(reg({0: 10240, 1: 4096, 2: 0, 3: 4096, 4: 4096}[n], 2048), 2)

        def wb(n):
            return reg({0: 12288, 1: 6144, 2: 2048, 3: 6144, 4: 6144}[n], 1024)

        hTf = v3(reg(0, 4096), 8)
        xg = v3(reg(7168, 2048), 2)
        ysb = v3(reg(9216, 2048), 2)
        sg = v3(reg(11264, 512), 2)
        aact = v3(reg(11776, 512), 2)
        YP = reg(12288, 8192).rearrange("p (b j d) -> p b j d", b=4, j=2)

        def squares(n):
            return reg(7168 if n in (2, 4) else 18432, DM)
        ovWg = v3(reg(16384, 4096), 8)
        ovWd = v3(reg(20480, 2048), 2)

        SEM = {}

        def s_(name):
            if name not in SEM:
                SEM[name] = sem(name)
            return SEM[name]

        raw_loaded = [sem(f"raw_loaded{n}") for n in range(NRAW)]
        hi_done, lo_pool, lo_dve = sem("hi_done"), sem("lo_pool"), sem("lo_dve")
        piece_used, dense_ready = sem("piece_used"), sem("dense_ready")
        dense_read = {"act": sem("dense_read_act"), "dve": sem("dense_read_dve")}
        tile_ready = sem("tile_ready")
        tile_read = {"act": sem("tile_read_act"), "dve": sem("tile_read_dve")}

        def piece_src(i):
            for l in range(2):
                if MOE_PIECE[l] <= i < MOE_PIECE[l] + 6 * NE:
                    q = i - MOE_PIECE[l]
                    if q < 4:
                        return gate_up_src(l, 0, q)
                    if q >= 6 * NE - 2:
                        return down_src(l, NE - 1, q - (6 * NE - 2))
                    return moe_src(l, 0, *divmod(q - 4, 6))
            db = i // 4 if i < MOE_PIECE[0] else (i - 6 * NE) // 4
            kp = (i - first_piece(db)) % 4
            kind, which, c = BLOCKS[db]
            if kind.endswith("in"):
                w = a["even_w_in"][0] if kind == "even_in" else a["odd_w_in"][0]
                return w.rearrange("(p k) c -> p k c", k=KD)[:, 2 * kp:2 * kp + 2, c:c + 512]
            w = a["even_w_out"][0] if kind == "even_out" else a["odd_w_out"][0][DM * which:DM * which + DM]
            return w.rearrange("(k p) c -> p k c", p=P)[:, 2 * kp:2 * kp + 2, c:c + 512]

        def gate_up_src(l, e, j):
            w = a["moe_w_gate_up"][l].rearrange("e (p k) c -> p e k c", k=KD)
            return w[:, bass.ds(e, 1), 2 * j:2 * j + 2, :].squeeze(1) if not isinstance(e, int) else w[:, e, 2 * j:2 * j + 2, :]

        def down_src(l, e, hf):
            w = a["moe_w_down"][l].rearrange("e (k p) c -> p e k c", p=P)
            c = 512 * hf
            return w[:, bass.ds(e, 1), :, c:c + 512].squeeze(1) if not isinstance(e, int) else w[:, e, :, c:c + 512]

        def moe_src(l, e, par, q):
            return gate_up_src(l, e + (par + 1), q) if q < 4 else down_src(l, e + par, q - 4)

        def wait_lo(eng, i):
            eng.wait_ge(lo_dve if lo_by_dve(i) else lo_pool, lo_count(i))

        def wait_used(eng, i):
            db = i // 4 if i < MOE_PIECE[0] else (i - 6 * NE) // 4
            kp = i - first_piece(db)
            assert 0 <= kp < 4
            if kp == 3:
                eng.wait_ge(dense_ready, 4 * db + 4)
            else:
                eng.wait_ge(piece_used, 3 * db + kp + 1)

        def wait_spl_free(eng, i):
            j = i - NSPL
            for l, m in enumerate(MOE_PIECE):
                if m <= j < m + 6 * NE:
                    eng.wait_ge(s_("moe_used"), 6 * NE * l + j - m + 1)
                    return
            if j >= 0:
                wait_used(eng, j)

        def tile(name):
            return ps[:, 4 + SIDE_AT[name] % 4, :]

        def tile_is_ready(eng, name):
            eng.wait_ge(tile_ready, SIDE_AT[name] + 1)

        def tile_is_read(eng, name):
            eng.wait_ge(tile_read[SIDE[SIDE_AT[name]][1]], SIDE_READ[name])

        class Line:

            def __init__(self, eng, who):
                self.eng, self.who = eng, who
                self.own = s_(f"{who}_line")
                self.n = {}
                self.reads = 0

            def __call__(self, ins, on=None):
                sm = on if on is not None else self.own
                ins.then_inc(sm, 1)
                self.n[sm.name] = self.n.get(sm.name, 0) + 1
                self.eng.wait_ge(sm, self.n[sm.name])

            def read(self, ins, name):
                assert SIDE[SIDE_AT[name]][1] == self.who, name
                assert SIDE_READ[name] == self.reads + 1, (name, SIDE_READ[name], self.reads)
                self.reads += 1
                self(ins, tile_read[self.who])

        def bc_h(ap, n=P):
            return ap.unsqueeze(2).broadcast_to([ap.shape[0], 4, n])

        def bc_m(ap, n=4):
            return ap.unsqueeze(1).broadcast_to([ap.shape[0], n, ap.shape[1]])

        def cols(T, w=P):
            return slice(T * w, T * w + w)

        def mm3(dst, lh, ll, rh, rl, first, last):
            nc.tensor.matmul(dst, lh, rh, start=first, stop=False)
            nc.tensor.matmul(dst, lh, rl, start=False, stop=False)
            return nc.tensor.matmul(dst, ll, rh, start=False, stop=last)

        NORM_W = [a["norm_mix_w"][0], a["norm_ffn_w"][0], a["norm_mix_w"][1], a["norm_ffn_w"][1], a["final_norm_w"]]
        def x_ready(n, T):
            if n == 0:
                return s_(f"x_loaded{T}"), 16
            if n in (1, 3):
                return dense_read["dve"], evac_count({1: 9, 3: 25}[n], T)
            return s_(f"moe_added{n // 2 - 1}"), T + 1


        RO = 12288
        Lst = reg(RO, 128)
        ones = reg(RO + 128, 128)
        lg = v3(reg(RO + 256, 80), 4)
        g0 = reg(RO + 356, 4)
        r_a = v3(reg(RO + 384, 16), 4)
        r_b = v3(reg(RO + 400, 16), 4)
        gm = v3(reg(RO + 416, 16), 4)
        r_c = reg(RO + 432, 64).rearrange("p (T g e) -> p T g e", T=4, g=4)
        fs = v3(reg(RO + 496, 16), 4)
        m1 = v3(reg(RO + 512, 16), 4)
        m2 = v3(reg(RO + 528, 16), 4)
        mx = reg(RO + 544, 4)
        mx2 = reg(RO + 548, 4)
        gp = reg(RO + 552, 4)
        ed = reg(RO + 556, 4)
        oh = [v3(reg(RO + 560 + 64 * n, 64), 4) for n in range(2)]
        anyh = v3(reg(RO + 3344, 64), 4)
        any80 = reg(RO + 3344, 80)
        ahead = v3(reg(RO + 3424, 64), 4)
        ahead80 = reg(RO + 3424, 80)
        slotv = v3(reg(RO + 752, 64), 4)
        tmp64 = v3(reg(RO + 816, 64), 4)
        ncnt = reg(RO + 880, 16)
        ovc = reg(RO + 896, 16)
        ovi = reg(RO + 912, 16)
        ovt = reg(RO + 928, 16)
        slotf = reg(RO + 944, 8)
        slots_u = reg(RO + 952, 8).bitcast(U32)
        tokv = reg(RO + 960, 8)
        first4 = reg(RO + 968, 4)
        hotB = v3(reg(RO + 1440, 1024), 8)
        hotA = v3(reg(RO + 2464, 8 * SLOT_TILES), 8)
        iotas = reg(RO + 2656, 24 + SLOT_TILES + P)
        iota8, offs16 = iotas[:, 0:8], iotas[:, 8:24]
        iotaA, iotaB = iotas[:, 24:24 + SLOT_TILES], iotas[:, 24 + SLOT_TILES:24 + SLOT_TILES + P]
        lgT = ar[0:20, RO + 2832:RO + 2832 + SEQ]
        slotA = reg(RO + 3520, 8)
        slotB = reg(RO + 3528, 8)
        sA_i, sB_i = reg(RO + 3536, 8).bitcast(U32), reg(RO + 3544, 8).bitcast(U32)
        lgb = ar[0:20, RO + 3552:RO + 3553]
        eidf = reg(RO + 996, 8)
        cmp7 = reg(RO + 1004, 112)
        rw = v3(reg(RO + 1120, 160), 8)
        w12 = small[:, 404:412]
        onesrow = reg(RO + 1408, 16)
        zero16 = reg(RO + 1424, 16)

        def overflow_flag(eng, l):
            eng.wait_ge(s_("slots_known"), l + 1)
            return eng.value_load(eid[0:1, 7:8], min_val=0, max_val=7)

        def overflow_sp(sp, l):
            n = overflow_flag(sp, l)
            with sp.If(n > 0):
                with sp.Fori(0, 7) as j:
                    sp.wait_ge(s_(f"ov_stored{l}"), j + 1)
                    settle(sp)
                    e = sp.value_load(eid[0:1, bass.ds(j, 1)], min_val=0, max_val=NE - 1)
                    wg = a["moe_w_gate_up"][l].rearrange("e (p k) c -> p e (k c)", k=KD)[:, bass.ds(e, 1), :].squeeze(1)
                    wd = a["moe_w_down"][l].rearrange("e (k p) c -> p e k c", p=P)[:, bass.ds(e, 1), :, :].squeeze(1)
                    sp.dma_start(ovWg.rearrange("p k c -> p (k c)"), wg).then_inc(s_(f"ov_w{l}"), 16)
                    sp.dma_start(ovWd, wd).then_inc(s_(f"ov_w{l}"), 16)

        def settle(eng):
            eng.wait_ge(hi_done, 1)

        gate_cell = sb("gate_cell", [P, 1])
        block = ctx.enter_context(nc.Block())

        @block.sync
        def _(sp):
            for T in range(NT):
                sp.dma_start(X[:, T, :], a["x"][0].rearrange("(T p) d -> T p d", p=P)[T]).then_inc(s_(f"x_loaded{T}"), 16)

            def load(i):
                if i >= NRAW:
                    wait_lo(sp, i - NRAW)
                sp.dma_start(raw[:, i % NRAW, :, :], piece_src(i)).then_inc(raw_loaded[i % NRAW], 16)

            def moe_loads(l):
                m = MOE_PIECE[l]
                for i in range(m, m + 16):
                    load(i)
                with sp.Fori(1, NE // 2 - 1) as it:
                    for j in range(12):
                        n = m + 4 + j
                        sp.wait_ge(lo_dve, it * 12 + (lo_count(n + 12 - NRAW) - 12))
                        sp.dma_start(raw[:, n % NRAW, :, :], moe_src(l, it * 2, j // 6, j % 6)).then_inc(raw_loaded[n % NRAW], 16)
                for i in range(m + 88, m + 6 * NE):
                    load(i)

            for i in range(MOE_PIECE[0]):
                load(i)
            moe_loads(0)
            for i in range(MOE_PIECE[0] + 6 * NE, MOE_PIECE[1]):
                load(i)
                if i == MOE_PIECE[0] + 6 * NE + 3:
                    overflow_sp(sp, 0)
            moe_loads(1)
            for i in range(MOE_PIECE[1] + 6 * NE, NPIECE):
                load(i)
            overflow_sp(sp, 1)
            for T in range(NT):
                sp.wait_ge(s_("h_ready"), 4 * 4 + T + 1)
                sp.dma_start(out[0].rearrange("(T p) d -> T p d", p=P)[T], htok(4)[:, T % 2, :]).then_inc(s_(f"out_stored{T % 2}"), 16)
            sp.wait_ge(s_("out_stored0"), 32)
            sp.wait_ge(s_("out_stored1"), 32)

        @block.gpsimd
        def _(pool):
            L = Line(pool, "pool")

            def lo(i):
                if i >= NPIECE or lo_by_dve(i):
                    return
                pool.wait_ge(hi_done, i + 1)
                wait_spl_free(pool, i)
                pool.tensor_tensor(wl[:, i % NSPL, :, :], raw[:, i % NRAW, :, :], wh[:, i % NSPL, :, :].bitcast(F32),
                                   ALU.subtract).then_inc(lo_pool, 1)

            def rsqrt(dst, src, n, ready, count, on):
                pool.wait_ge(ready, count)
                pool.tensor_tensor(dst, src, mhalf[:, 0:n], ALU.pow).then_inc(on, 1)

            def carry():
                pool.tensor_tensor(gate_cell[:, :], mhalf[:, 0:1], mhalf[:, 0:1], ALU.add)

            def moe(l):
                last_row = pool.to_reg(SEQ - 1)
                last_pair_row = pool.to_reg(2 * SEQ - 1)
                pool.wait_ge(s_("rows_known"), l + 1)
                for q in range(2):
                    pool.wait_ge(s_(f"h_stored{q}"), 32 * (l + 1))
                pool.wait_ge(s_("xg_cleared"), l + 1)

                def gather(col, par):
                    L(pool.tensor_copy(cur[:, par:par + 1], idx[:, 0, col].bitcast(U32)))
                    pool.indirect_dma_start(out=xg[:, par, :], out_offset=None, in_=hs_dram[l],
                                            in_offset=bass.IndirectOffsetOnAxis(ap=cur[:, par:par + 1], axis=0),
                                            bounds_check=last_row, oob_is_err=False).then_inc(s_(f"xg_loaded{par}"), 16)

                gather(slice(0, 1), 0)
                gather(slice(1, 2), 1)
                G = s_("pool_moe")

                def gather_ahead(it, par):
                    pool.wait_ge(s_("xT_ready"), it * 4 + (32 * l + 2 * par + 2))
                    col = it * 2 + (2 + par)
                    col = slice(col, col + 1) if isinstance(col, int) else bass.ds(col, 1)
                    pool.tensor_copy(cur[:, par:par + 1], idx[:, 0, col].bitcast(U32)).then_inc(G, 1)

                def gather_now(it, par):
                    pool.indirect_dma_start(out=xg[:, par, :], out_offset=None, in_=hs_dram[l],
                                            in_offset=bass.IndirectOffsetOnAxis(ap=cur[:, par:par + 1], axis=0),
                                            bounds_check=last_row, oob_is_err=False).then_inc(s_(f"xg_loaded{par}"), 16)

                def scatter(it, par, g):
                    col = it * 2 + par
                    col = slice(col, col + 1) if isinstance(col, int) else bass.ds(col, 1)
                    pool.tensor_copy(cur[:, 2 + par:3 + par], idx[:, 1, col].bitcast(U32)).then_inc(G, 1)
                    pool.wait_ge(G, g)
                    pool.wait_ge(s_("y_read"), it * 4 + (32 * l + 2 * par + 4))
                    carry()
                    pool.indirect_dma_start(out=y2_dram[l], out_offset=bass.IndirectOffsetOnAxis(ap=cur[:, 2 + par:3 + par], axis=0),
                                            in_=ysb[:, par, :], in_offset=None,
                                            bounds_check=last_pair_row, oob_is_err=False).then_inc(s_("y_stored"), 16)
                    pool.wait_ge(s_("y_stored"), it * 32 + (256 * l + 16 * par + 16))
                    pool.nop().then_inc(s_("ysb_free"), 1)

                for par in range(2):
                    gather_ahead(0, par)
                    pool.wait_ge(G, 32 * l + par + 1)
                    gather_now(0, par)
                with pool.Fori(0, NE // 2 - 1) as it:
                    for par in range(2):
                        gather_ahead(it + 1, par)
                        pool.wait_ge(G, it * 4 + (32 * l + 2 * par + 3))
                        carry()
                        gather_now(it, par)
                        scatter(it, par, it * 4 + (32 * l + 2 * par + 4))
                for par in range(2):
                    scatter(NE // 2 - 1, par, 32 * l + 31 + par)
                for q in range(2):
                    pool.wait_ge(s_(f"xg_loaded{q}"), 144 * (l + 1))
                pool.nop().then_inc(s_(f"ov_stored{l}"), 1)
                n = overflow_flag(pool, l)
                with pool.If(n > 0):
                    with pool.Fori(0, 7) as j:
                        pool.tensor_copy(cur[:, 0:1], idx[:, 0, bass.ds(j + NE, 1)].bitcast(U32)).then_inc(s_(f"ov_cur{l}"), 1)
                        pool.wait_ge(s_(f"ov_cur{l}"), j * 2 + 1)
                        pool.wait_ge(s_(f"ov_stored{l}"), j + 1)
                        carry()
                        pool.indirect_dma_start(out=xg[:, 0, :], out_offset=None, in_=hs_dram[l],
                                                in_offset=bass.IndirectOffsetOnAxis(ap=cur[:, 0:1], axis=0),
                                                bounds_check=last_row, oob_is_err=False).then_inc(s_(f"ov_x{l}"), 16)
                        pool.tensor_copy(cur[:, 2:3], idx[:, 1, bass.ds(j + NE, 1)].bitcast(U32)).then_inc(s_(f"ov_cur{l}"), 1)
                        pool.wait_ge(s_(f"ov_cur{l}"), j * 2 + 2)
                        pool.wait_ge(s_(f"ov_y{l}"), j * 2 + 2)
                        carry()
                        pool.indirect_dma_start(out=y2_dram[l], out_offset=bass.IndirectOffsetOnAxis(ap=cur[:, 2:3], axis=0),
                                                in_=ysb[:, 0, :], in_offset=None,
                                                bounds_check=last_pair_row, oob_is_err=False).then_inc(s_(f"ov_ydma{l}"), 16)
                        pool.wait_ge(s_(f"ov_ydma{l}"), j * 16 + 16)
                        pool.nop().then_inc(s_(f"ov_stored{l}"), 1)
                pool.nop().then_inc(s_("y_all_stored"), 1)

            pool.memset(mhalf, -0.5).then_inc(L.own, 1)
            L.n[L.own.name] = 1
            pool.wait_ge(L.own, 1)
            for _ in range(2):
                pool.nop().then_inc(s_("ysb_free"), 1)
            for i in range(3):
                lo(i)
            for step in SCHEDULE:
                if step[0] == "piece":
                    lo(first_piece(step[1]) + step[2] + 3)
                elif step[0] == "norm":
                    for T in range(NT):
                        pool.wait_ge(s_("norm_ss"), 4 * step[1] + T + 1)
                        L(pool.tensor_scalar(ms[:, T:T + 1], ss[:, T:T + 1], EPS, None, ALU.add))
                        pool.tensor_tensor(rs[:, T:T + 1], ms[:, T:T + 1], mhalf[:, 0:1], ALU.pow).then_inc(s_("norm_r"), 1)
                elif step[0] == "l2":
                    rsqrt(rn, ssn, 32, s_("l2_ms"), 1, s_("l2_r"))
                elif step[0] == "onorm":
                    rsqrt(ors, oss, 16, s_("o_ms"), step[1] + 1, s_("o_r"))
                elif step[0] == "evac" and BLOCKS[step[1]][1] and isinstance(BLOCKS[step[1]][1], tuple) and BLOCKS[step[1]][1][0] == "rg":
                    h = BLOCKS[step[1]][1][1]
                    rsqrt(ors[:, 0:4], oss[:, 0:4], 4, s_("ro_ms"), h + 1, s_("ro_r"))
                elif step[0] == "moe":
                    lo(MOE_PIECE[step[1]] + 3)
                    moe(step[1])
                    for i in range(3):
                        lo(MOE_PIECE[step[1]] + 6 * NE + i)

        @block.scalar
        def _(act):
            A = Line(act, "act")
            dense_reads = [0]

            def hi(i):
                if i >= NPIECE:
                    return
                act.wait_ge(raw_loaded[i % NRAW], 16 * (i // NRAW + 1))
                wait_spl_free(act, i)
                act.activation(wh[:, i % NSPL, :, :], raw[:, i % NRAW, :, :], ACT.Copy).then_inc(hi_done, 1)

            def dense_tile(db, t):
                act.wait_ge(dense_ready, 4 * db + t + 1)
                return ps[:, t, :]

            def load_consts():
                act.dma_start(wb(0), NORM_W[0].rearrange("(a n) -> a n", a=1).broadcast_to([P, DM])).then_inc(s_("wb_loaded"), 16)
                ld = s_("consts_loaded")
                dm = [(ident[:, :], a["c_ident"]), (U[:, :], a["c_U"]), (m16[:, :], a["c_m16"]), (moff[:, :], a["c_moff"]),
                      (lv_raw, a["c_lv"]), (resetm[:, :], a["c_reset"]),
                      (raw_vec[0:48, :], a["gdn_conv_w"][0].rearrange("j (g p) -> (j g) p", p=P)),
                      (raw_vec[48:60, :], a["hgrn_lb_logits"].rearrange("r (h p) -> (r h) p", p=P)),
                      (dtb, a["gdn_dt_bias"].broadcast_to([P, 4])), (alog, a["gdn_a_log"].broadcast_to([P, 4])),
                      (gnw[:, :], a["gdn_norm_w"].broadcast_to([P, P])), (hnw[:, :], a["hgrn_norm_w"].broadcast_to([P, P])),
                      (wba_raw, a["even_w_in"][0].rearrange("(p k) c -> p k c", k=KD)[:, :, 2048:2056])]
                for dst, src in dm:
                    act.dma_start(dst, src).then_inc(ld, 16)

            def consts():
                act.wait_ge(s_("consts_loaded"), 16 * 13)
                A(act.activation(wba_h[:, :, :], wba_raw, ACT.Copy), s_("wba_hi"))
                act.wait_ge(s_("lb_args"), 1)
                A(act.activation(lbt[:, 0:12], lbt[:, 0:12], ACT.Exp), s_("lb_exp"))

            def norm(n):
                if n in (1, 3):
                    load_wb(n)
                for T in range(NT):
                    act.wait_ge(*x_ready(n, T))
                    A(act.activation(squares(n), X[:, T, :], ACT.Square, scale=DM ** -0.5, accum_out=ss[:, T:T + 1]), s_("norm_ss"))
                if n == 4:
                    return
                for T in range(NT):
                    if n in (1, 3):
                        act.wait_ge(s_("h_ready"), 4 * n + T + 1)
                        act.dma_start(hs_dram[n // 2].rearrange("(T p) d -> T p d", p=P)[T], htok(n)[:, T % 2, :])\
                            .then_inc(s_(f"h_stored{T % 2}"), 16)
                    for g in range(2):
                        name = ("hT", n, T, g)
                        tile_is_ready(act, name)
                        src = v3(tile(name), 4)
                        if n in (1, 3):
                            A.read(act.activation(hTf[:, 4 * g:4 * g + 4, cols(T)], src, ACT.Copy), name)
                        else:
                            A(act.activation(HTH[:, 4 * g:4 * g + 4, cols(T)], src, ACT.Copy), s_("hT_hi_made"))

            def load_wb(n):
                act.dma_start(wb(n), NORM_W[n].rearrange("(a n) -> a n", a=1).broadcast_to([P, DM])).then_inc(s_("wb_loaded"), 16)

            def yT(l, kh):
                act.wait_ge(dense_ready, 4 * {(0, 0): 8, (1, 0): 22, (1, 1): 24}[l, kh])
                for T in range(NT):
                    for g in range(2):
                        name = ("yT", l, kh, T, g)
                        tile_is_ready(act, name)
                        A(act.activation(HTH[:, 4 * g:4 * g + 4, cols(T)], v3(tile(name), 4), ACT.Copy), s_("hT_hi_made"))

            def gates_act():
                act.wait_ge(s_("z_ready"), 1)
                A(act.activation(esp, esp, ACT.Exp, scale=-1.0), s_("gate_exp"))
                A(act.activation(alog, alog, ACT.Exp), s_("gate_exp"))
                A(act.activation(beta, beta, ACT.Tanh, scale=0.5), s_("gate_exp"))
                act.wait_ge(s_("sp_ready"), 1)
                A(act.activation(spt, spt, ACT.Ln), s_("gate_exp"))
                tile_is_read(act, "gc")
                A(act.activation(egc, gc, ACT.Exp), s_("egc_ready"))

            def tok(nm, T):
                name = ("tok", nm, T)
                tile_is_ready(act, name)
                dst = {"q": Y0[:, T, 0:512], "k": KT[:, T, :], "v": VT[:, T, :]}[nm]
                if nm == "v":
                    A.read(act.activation(dst, tile(name), ACT.Copy), name)
                    return
                A(act.activation(dst, tile(name), ACT.Copy))
                n = (nm == "k") * 4 + T
                if n >= 2:
                    act.wait_ge(s_("sq_reduced"), n - 1)
                A.read(act.activation(sqt[:, n % 2, :], tile(name), ACT.Square), name)

            def l2():
                for T in range(NT):
                    tile_is_ready(act, ("qb", T))
                    A.read(act.activation(QF[:, :, cols(T)], v3(tile(("qb", T)), 4), ACT.Copy), ("qb", T))

            def gdn_chunks(pr):
                Ts = (2 * pr, 2 * pr + 1)
                for T in Ts:
                    q = T % 2
                    act.wait_ge(s_("g_args"), T + 1)
                    A.read(act.activation(PA[2][:, q, :], tile(("Gb", T)), ACT.Exp), ("Gb", T))
                    A(act.activation(PA[0][:, q, :], PA[0][:, q, :], ACT.Exp, scale=-1.0))
                    A(act.activation(PA[1][:, q, :], PA[1][:, q, :], ACT.Exp))
                    A(act.activation(kde[:, 4 * T:4 * T + 4], kde[:, 4 * T:4 * T + 4], ACT.Exp), s_("decays"))
                    tile_is_ready(act, ("DT", T))
                    A.read(act.activation(PA[4][:, q, :], tile(("DT", T)), ACT.Copy), ("DT", T))

                def copy(name, dst, after=None):
                    tile_is_ready(act, name)
                    if after is not None:
                        tile_is_ready(act, after)
                    A.read(act.activation(dst, tile(name), ACT.Copy), name)

                for T in Ts:
                    copy(("P2", T), PA[5][:, T % 2, :])
                    copy(("P2T", T), PA[6][:, T % 2, :])
                for r in (1, 2):
                    for T in Ts:
                        last = ("P", r, T) if r == 1 else ("PT", r, T)
                        copy(("PT", r, T), PA[6][:, T % 2, :], last)
                        if r == 1:
                            copy(("P", r, T), PA[5][:, T % 2, :])
                for T in Ts:
                    copy(("B", T), PA[5][:, T % 2, :])
                    copy(("BT", T), PA[6][:, T % 2, :])
                for T in Ts:
                    copy(("B2", T), PA[4][:, T % 2, :])
                for T in Ts:
                    copy(("IT", T), PA[8][:, T % 2, :])
                for T in Ts:
                    copy(("u", T), VT[:, T, :])
                    tile_is_ready(act, ("wT", T))
                    A.read(act.activation(KF[:, :, cols(T)], v3(tile(("wT", T)), 4), ACT.Copy), ("wT", T))

            def scan_out(nm, c, c0):
                T, r = c // 2, slice(64 * (c % 2), 64 * (c % 2) + 64)
                tile_is_ready(act, (nm, c))
                A.read(act.activation(Y0[r, T, c0:c0 + 512], tile((nm, c))[r, :], ACT.Copy, scale=DK ** -0.5), (nm, c))

            def onorm(w):
                act.wait_ge(s_("scan_done"), 1)
                for T in range(NT):
                    n = 8 + 4 * w + T
                    act.wait_ge(s_("sq_reduced"), n - 1)
                    A(act.activation(onsq[:, T % 2, :], Y0[:, T, 512 * w:512 * w + 512], ACT.Square), s_("o_sq"))

            def hgrn(step):
                if step[0] == "hdiag":
                    pass
                elif step[0] == "hlevel":
                    n = step[1]
                    act.wait_ge(s_("lv_args"), n + 1)
                    A(act.activation(LE, LE, ACT.Exp), s_("lv_exp"))
                elif step[0] == "hstate":
                    act.wait_ge(s_("lv_args"), len(LEVELS) + 1)
                    A(act.activation(LE, LE, ACT.Exp), s_("lv_exp"))
                    act.wait_ge(s_("hk_decayed"), 1)
                    A(act.activation(LE, HB.rearrange("p h t -> p (h t)"), ACT.Exp), s_("lv_exp"))
                    for T in range(NT):
                        tile_is_ready(act, ("kd", T))
                        A.read(act.activation(KDT[:, T, :], tile(("kd", T)), ACT.Copy), ("kd", T))

            def evac(db):
                kind, which, _c = BLOCKS[db]
                rd = dense_read["act"]
                if which in ("q", "k", "v"):
                    dst = {"q": QF, "k": KF, "v": VF}[which]
                    for t in range(5):
                        if t < 4:
                            n = 4 * db + t
                            src = dense_tile(db, t)
                            if n >= 2:
                                act.wait_ge(s_("conv_done"), n - 1)
                            A(act.activation(craw[:, t % 2, :], src, ACT.Copy), rd)
                        if t > 0:
                            act.wait_ge(s_("conv_done"), 4 * db + t)
                            A(act.activation(dst[:, t - 1, :], dst[:, t - 1, :], ACT.Silu), s_("conv_silu"))
                elif which == "hf":
                    for t in range(4):
                        src = dense_tile(db, t)
                        A(act.activation(HK[:, t, :], src, ACT.Tanh, scale=0.5), rd)
                    for t in range(4):
                        act.wait_ge(s_("f_ready"), t + 1)
                        A(act.activation(HQ[:, t, :], HB[:, t, :], ACT.Ln), s_("lf_ready"))
                elif which == "hq":
                    for t in range(4):
                        src = dense_tile(db, t)
                        act.wait_ge(s_("b_ready"), 4)
                        A(act.activation(HQ[:, t, :], src, ACT.Silu), rd)
                elif which == "hi":
                    for t in range(4):
                        src = dense_tile(db, t)
                        A(act.activation(HI[:, t, :], src, ACT.Copy), rd)
                elif which in ("z", "hg"):
                    for t in range(4):
                        src = dense_tile(db, t)
                        n = 4 * (which == "hg") + t
                        if n == 0:
                            act.wait_ge(s_("scan_done"), 1)
                        if n >= 2:
                            act.wait_ge(s_("z_used"), n - 1)
                        A(act.activation(zt[:, t % 2, :], src, ACT.Silu), rd)
                elif kind == "odd_in":
                    nm, h = which
                    if nm in ("rq", "rk"):
                        for t in range(4):
                            src = dense_tile(db, t)
                            n = rot_index(db) * 2 + t // 2
                            if n >= 1 and t % 2 == 0:
                                act.wait_ge(s_("rot_done"), n)
                            A(act.activation(rtmp[:, t % 2, :], src, ACT.Copy), rd)
                    elif nm == "rv":
                        for t in range(4):
                            src = dense_tile(db, t)
                            A(act.activation(RV[:, h % 2, t, :], src, ACT.Copy), rd)
                    else:
                        for t in range(4):
                            src = dense_tile(db, t)
                            n = 4 * h + t
                            if n >= 2:
                                act.wait_ge(s_("g_used"), n - 1)
                            A(act.activation(gt[:, t % 2, :], src, ACT.Silu), rd)

            def ro(h):
                for T in range(NT):
                    name = ("ro", h, T)
                    tile_is_ready(act, name)
                    A(act.activation(Y1[:, T, h * RDV:(h + 1) * RDV], tile(name), ACT.Copy))
                    if T == 0 and h > 0:
                        act.wait_ge(s_("ro_r"), h)
                    A.read(act.activation(rjunk, tile(name), ACT.Square, accum_out=oss[:, T:T + 1]), name)

            def moe(l):
                m = MOE_PIECE[l]
                act.wait_ge(s_("r_cexp"), l + 1)
                A(act.activation(r_a, r_a, ACT.Exp), s_("r_exp"))
                act.wait_ge(s_("r_eexp"), l + 1)
                A(act.activation(ed, ed, ACT.Exp), s_("r_exp"))
                used = s_("moe_used")

                def silu(E, par, count):
                    act.wait_ge(used, count)
                    act.activation(sg[:, par, :], ps[:, par, 0:FE], ACT.Silu).then_inc(s_("silu_done"), 1)

                xT_hi(l, 0, 0)
                hi(m + 4)
                hi(m + 5)
                xT_hi(l, 1, 1)
                hi(m + 6)
                silu(16 * l, 0, 6 * NE * l + 4)

                def expert(it, par):
                    E = it * 2 + (16 * l + par)
                    b = m + 4 + 6 * par
                    last = isinstance(it, int)

                    def hi_in(j):
                        n = b + j
                        act.wait_ge(raw_loaded[n % NRAW], it * 32 + 16 * (n // NRAW + 1))
                        act.wait_ge(used, it * 12 + (6 * NE * l + n - m - NSPL + 1))
                        act.activation(wh[:, n % NSPL, :, :], raw[:, n % NRAW, :, :], ACT.Copy).then_inc(hi_done, 1)

                    act.wait_ge(s_("aT_ready"), E + 1)
                    act.activation(HTH[:, 4 + par, 0:256], ps[:, 6, 0:256], ACT.Copy).then_inc(s_("aT_hi"), 1)
                    n0 = 0
                    if not last or par == 0:
                        n0 = 4
                        for j in (3, 4, 5, 6):
                            hi_in(j)
                        silu(E + 1, 1 - par, it * 12 + (6 * NE * l + 6 * par + 8))
                        hi_in(7)
                        if not last:
                            xT_hi(l, it * 2 + (par + 2), par)
                    act.wait_ge(s_("ysb_free"), E + 1)
                    for hf in range(2):
                        act.wait_ge(used, it * 12 + (6 * NE * l + 6 * par + 4 + n0 + hf + 1))
                        act.activation(ysb[:, par, 512 * hf:512 * hf + 512], ps[:, 2 + hf, :], ACT.Copy).then_inc(s_("y_read"), 1)
                        if hf == 0 and not last:
                            hi_in(8)

                with act.Fori(0, NE // 2 - 1) as it:
                    for par in range(2):
                        expert(it, par)
                for par in range(2):
                    expert(NE // 2 - 1, par)
                n = overflow_flag(act, l)
                with act.If(n > 0):
                    with act.Fori(0, 7) as j:
                        for g in range(2):
                            act.wait_ge(s_(f"ov_xT{l}"), j * 2 + (g + 1))
                            act.activation(hTf[:, 4 * g:4 * g + 4, 0:P], v3(ps[:, 4 + g, :], 4), ACT.Copy).then_inc(s_(f"ov_xTr{l}"), 1)
                        act.wait_ge(s_(f"ov_gu{l}"), j + 1)
                        act.activation(sg[:, 0, :], ps[:, 0, 0:FE], ACT.Silu).then_inc(s_(f"ov_silu{l}"), 1)
                        act.wait_ge(s_(f"ov_aT{l}"), j + 1)
                        act.activation(hTf[:, 0:2, P:2 * P], ps[:, 6, 0:256].rearrange("p (k n) -> p k n", k=2), ACT.Copy).then_inc(s_(f"ov_aTr{l}"), 1)
                        for hf in range(2):
                            act.wait_ge(s_(f"ov_yp{l}"), j * 2 + (hf + 1))
                            act.activation(ysb[:, 0, 512 * hf:512 * hf + 512], ps[:, 2 + hf, :], ACT.Copy).then_inc(s_(f"ov_y{l}"), 1)
                load_wb(2 * l + 2)
                act.wait_ge(s_("y_all_stored"), l + 1)
                src = y2_dram[l].rearrange("(T p j) d -> T p j d", p=P, j=2)
                for T in range(NT):
                    act.dma_start(YP[:, T, :, :], src[T]).then_inc(s_(f"yp_loaded{T}"), 16)

            def xT_hi(l, e, par):
                for g in range(2):
                    act.wait_ge(s_("xT_ready"), e * 2 + (32 * l + g + 1))
                    act.activation(HTH[:, 2 * par + g, :], ps[:, 4 + g, :], ACT.Copy).then_inc(s_("xT_hi"), 1)

            for _ in range(2):
                act.nop().then_inc(s_("y_read"), 1)
            load_consts()
            for i in range(3):
                hi(i)
            for step in SCHEDULE:
                k = step[0]
                if k == "consts":
                    consts()
                elif k == "norm":
                    if step[1] in (1, 3):
                        l = step[1] // 2
                        for dst, src in ((Lst, a["c_Lst"]), (iotas, a["c_iota"]),
                                         (lgb[0:4, :], a["router_c_b"][l].rearrange("(a n) -> a n", n=1)),
                                         (lgb[4:20, :], a["router_f_b"][l].rearrange("(a n) -> a n", n=1)),
                                         (rw[:, :, 0:4], a["router_c_w"][l].rearrange("(p k) c -> p k c", k=KD)),
                                         (rw[:, :, 4:20], a["router_f_w"][l].rearrange("(p k) c -> p k c", k=KD)),
                                         (tokv, a["c_tok"]), (first4, a["c_first"])):
                            act.dma_start(dst, src).then_inc(s_("router_loaded"), 16)
                    norm(step[1])
                    if step[1] == 2:
                        for n, (dst, src) in enumerate(((cos_t, a["c_cos"]), (sin_t, a["c_sin"]), (rnw, a["ret_norm_w"].broadcast_to([P, RDV])))):
                            act.dma_start(dst, src).then_inc(s_("ret_consts"), 16)
                elif k == "piece":
                    hi(first_piece(step[1]) + step[2] + 3)
                elif k == "ba":
                    pass
                elif k == "gates":
                    gates_act()
                elif k == "tok":
                    tok(step[1], step[2])
                elif k == "l2":
                    l2()
                elif k == "gdn_chunks":
                    gdn_chunks(step[1])
                elif k == "scan":
                    scan_out("so", step[1], 0)
                elif k == "hscan":
                    scan_out("ho", step[1], 512)
                elif k == "onorm":
                    onorm(step[1])
                elif k in ("hdiag", "hlevel", "hstate"):
                    hgrn(step)
                elif k == "evac":
                    if evac_engine(step[1]) == "act":
                        evac(step[1])
                elif k == "yT":
                    yT(step[1], step[2])
                elif k == "score":
                    h = step[1]
                    if h > 0:
                        act.wait_ge(tile_read["dve"], SIDE_READ[("sc", h - 1, NT - 1)])
                    act.dma_start(DH, a["c_decay"][h]).then_inc(s_("dh_loaded"), 16)
                elif k == "ro":
                    ro(step[1])
                elif k == "moe":
                    hi(MOE_PIECE[step[1]] + 3)
                    moe(step[1])
                    for i in range(3):
                        hi(MOE_PIECE[step[1]] + 6 * NE + i)

        @block.vector
        def _(dve):
            D = Line(dve, "dve")
            tt, ts, stt = dve.tensor_tensor, dve.tensor_scalar, dve.scalar_tensor_tensor

            def consts():
                D(dve.memset(S[:, :], 0.0))
                tile_is_ready(dve, "vec")
                D.read(dve.tensor_copy(vec[:, :], tile("vec")[:, 0:60]), "vec")
                D(dve.tensor_copy(lvmask[:, :, :], lv_raw))
                lb3 = vec[:, 48:60]
                D(tt(lbs[:, 0:4], lb3[:, 0:4], lb3[:, 4:8], ALU.max))
                D(tt(lbs[:, 0:4], lbs[:, 0:4], lb3[:, 8:12], ALU.max))
                D(tt(v3(lbt[:, 0:12], 3), v3(lb3, 3), bc_m(lbs[:, 0:4], 3), ALU.subtract), s_("lb_args"))
                dve.wait_ge(s_("lb_exp"), 1)
                D(tt(lbs[:, 4:8], lbt[:, 0:4], lbt[:, 4:8], ALU.add))
                D(tt(lbs[:, 4:8], lbs[:, 4:8], lbt[:, 8:12], ALU.add))
                D(dve.reciprocal(lbs[:, 4:8], lbs[:, 4:8]))
                D(tt(lbs[:, 8:12], lbt[:, 0:4], lbs[:, 4:8], ALU.mult))
                D(ts(c1, lbs[:, 8:12], -0.5, 0.5, ALU.mult, ALU.add))
                D(tt(c2, lbs[:, 8:12], c1, ALU.add))
                dve.wait_ge(s_("wba_hi"), 1)
                D(tt(wba_l[:, :, :], wba_raw, wba_h[:, :, :].bitcast(F32), ALU.subtract), s_("wba_lo"))

            def combine(l, T):
                dve.wait_ge(s_(f"yp_loaded{T}"), 16 * (l + 1))
                D(stt(X[:, T, :], YP[:, T, 0, :], w12[:, 2 * T:2 * T + 1], X[:, T, :], ALU.mult, ALU.add))
                D(stt(X[:, T, :], YP[:, T, 1, :], w12[:, 2 * T + 1:2 * T + 2], X[:, T, :], ALU.mult, ALU.add), s_(f"moe_added{l}"))

            def norm(n):
                moe_l = n // 2 - 1 if n in (2, 4) else None
                if moe_l is not None:
                    combine(moe_l, 0)
                    combine(moe_l, 1)
                dve.wait_ge(s_("wb_loaded"), 16 * (n + 1))
                for T in range(NT):
                    if T >= 2:
                        if n < 4:
                            tile_is_ready(dve, ("hT", n, T - 2, 1))
                        if n in (1, 3):
                            dve.wait_ge(s_(f"h_stored{T % 2}"), 32 * (n // 2) + 16)
                        if n == 4:
                            dve.wait_ge(s_(f"out_stored{T % 2}"), 16)
                    dve.wait_ge(s_("norm_r"), 4 * n + T + 1)
                    D(stt(htok(n)[:, T % 2, :], X[:, T, :], rs[:, T:T + 1], wb(n), ALU.mult, ALU.mult), s_("h_ready"))
                    if moe_l is not None and T + 2 < NT:
                        combine(moe_l, T + 2)
                    if n in (0, 2) and T >= 1:
                        lo_tiles(("hT", n, T - 1), T - 1)
                if n in (0, 2):
                    lo_tiles(("hT", n, 3), 3)

            his = [0]

            def lo_tiles(name, T):
                for g in range(2):
                    his[0] += 1
                    dve.wait_ge(s_("hT_hi_made"), his[0])
                    nm = name + (g,)
                    D.read(tt(HTL[:, 4 * g:4 * g + 4, cols(T)], v3(tile(nm), 4), HTH[:, 4 * g:4 * g + 4, cols(T)].bitcast(F32),
                              ALU.subtract), nm)

            def gate_inputs():
                tile_is_ready(dve, "ba_tok")
                D.read(dve.tensor_copy(ba, v3(tile("ba_tok")[:, 0:32], 4)), "ba_tok")
                D(tt(v3(zsp, 4), ba[:, :, 4:8], bc_m(dtb), ALU.add))
                D(ts(spt, zsp, -1.0, None, ALU.mult))
                D(tt(esp, zsp, spt, ALU.max))
                D(dve.tensor_copy(v3(beta, 4), ba[:, :, 0:4]), s_("z_ready"))

            def gates():
                dve.wait_ge(s_("gate_exp"), 3)
                D(ts(spt, esp, 1.0, None, ALU.add), s_("sp_ready"))
                D(ts(beta, beta, 0.5, 0.5, ALU.mult, ALU.add))
                dve.wait_ge(s_("gate_exp"), 4)
                D(stt(spt, zsp, 0.0, spt, ALU.max, ALU.add))
                D(stt(v3(gg, 4), v3(spt, 4), -1.0, bc_m(alog), ALU.mult, ALU.mult), s_("g_ready"))
                tile_is_ready(dve, "gc")
                D.read(dve.tensor_copy(gc, tile("gc")[:, 0:16]), "gc")
                dve.wait_ge(s_("egc_ready"), 1)
                D(tt(bege, beta, egc, ALU.mult))

            def tok(nm, T):
                if nm == "v":
                    return
                tile_is_read(dve, ("tok", nm, T))
                n = 4 * (nm == "k") + T
                D(dve.tensor_reduce(ssn[:, 4 * n:4 * n + 4], v3(sqt[:, n % 2, :], 4), AX.X, ALU.add), s_("sq_reduced"))

            def l2():
                D(ts(ssn, ssn, EPS, None, ALU.add), s_("l2_ms"))
                dve.wait_ge(s_("l2_r"), 1)
                for T in range(NT):
                    D(tt(v3(Y0[:, T, 0:512], 4), v3(Y0[:, T, 0:512], 4), bc_h(rn[:, 4 * T:4 * T + 4]), ALU.mult), s_("qk_normed"))
                    D(tt(v3(KT[:, T, :], 4), v3(KT[:, T, :], 4), bc_h(rn[:, 16 + 4 * T:20 + 4 * T]), ALU.mult), s_("qk_normed"))
                for T in range(NT):
                    tile_is_ready(dve, ("kb", T))
                    D.read(dve.tensor_copy(KF[:, :, cols(T)], v3(tile(("kb", T)), 4)), ("kb", T))

            def gdn_chunks(pr):
                Ts = (2 * pr, 2 * pr + 1)
                for T in Ts:
                    q = T % 2
                    h4 = slice(4 * T, 4 * T + 4)
                    gb = tile(("Gb", T))
                    tile_is_ready(dve, ("Gb", T))
                    for h in range(NH):
                        D(ts(PA[0][:, q, cols(h)], gb[:, cols(h)], gc[:, 4 * T + h:4 * T + h + 1], 0.0, ALU.subtract, ALU.max))
                        D(ts(PA[1][:, q, cols(h)], gb[:, cols(h)], gc[:, 4 * T + h:4 * T + h + 1], 0.0, ALU.subtract, ALU.min))
                    D(tt(kde[0:64, h4], v3(gb, 4)[0:64, :, 63], gc[0:64, h4], ALU.subtract))
                    D(tt(kde[64:128, h4], v3(gb, 4)[64:128, :, 127], gc[64:128, h4], ALU.subtract), s_("g_args"))
                    dve.wait_ge(s_("decays"), T + 1)
                    D(tt(v3(PA[0][:, q, :], 4), v3(PA[0][:, q, :], 4), bc_h(beta[:, h4]), ALU.mult))
                    D(tt(v3(PA[3][:, q, :], 4), v3(PA[0][:, q, :], 4), bc_m(moff[:, :]), ALU.mult))
                    D(tt(v3(PA[0][:, q, :], 4), v3(PA[0][:, q, :], 4), bc_m(m16[:, :]), ALU.mult))
                    D(tt(v3(PA[1][:, q, :], 4), v3(PA[1][:, q, :], 4), bc_m(U[:, :]), ALU.mult))
                    tile_is_ready(dve, ("KK", T))
                    D(tt(PA[3][:, q, :], tile(("KK", T)), PA[3][:, q, :], ALU.mult))
                    D.read(tt(PA[0][:, q, :], tile(("KK", T)), PA[0][:, q, :], ALU.mult), ("KK", T))
                    tile_is_ready(dve, ("KQ", T))
                    D.read(tt(AT0[:, T, :], tile(("KQ", T)), PA[1][:, q, :], ALU.mult), ("KQ", T))
                    for c in range(2):
                        D(dve.tensor_copy(egl[:, 2 * T + c, :], v3(PA[2][:, q, :], 4)[:, :, 64 * c + 63]))
                    D(tt(QF[:, :, cols(T)], QF[:, :, cols(T)], v3(PA[2][:, q, :], 4), ALU.mult))
                    D(tt(v3(PA[7][:, q, :], 4), bc_m(ident[:, :]), v3(PA[0][:, q, :], 4), ALU.subtract))
                    tile_is_read(dve, ("DT", T))
                    D(tt(v3(PA[8][:, q, :], 4), bc_m(ident[:, :]), v3(PA[4][:, q, :], 4), ALU.subtract), s_("x1_ready"))
                    D(tt(v3(PA[9][:, q, :], 4), v3(VT[:, T, :], 4), bc_h(beta[:, h4]), ALU.mult))
                    D(tt(v3(PA[10][:, q, :], 4), v3(KT[:, T, :], 4), bc_h(bege[:, h4]), ALU.mult))
                    D(tt(v3(KT[:, T, :], 4), v3(KT[:, T, :], 4), bc_h(kde[:, h4]), ALU.mult), s_("vk_ready"))
                for r in (1, 2, 3):
                    for T in Ts:
                        q = T % 2
                        tile_is_ready(dve, ("XT", r, T))
                        D.read(tt(PA[7][:, q, :], PA[7][:, q, :], tile(("X", r, T)), ALU.add), ("X", r, T))
                        D.read(tt(PA[8][:, q, :], PA[8][:, q, :], tile(("XT", r, T)), ALU.add), ("XT", r, T))
                for T in Ts:
                    tile_is_read(dve, ("BT", T))
                    D(tt(v3(PA[0][:, T % 2, :], 4), bc_m(ident[:, :]), v3(PA[6][:, T % 2, :], 4), ALU.subtract), s_("n1_ready"))
                for T in Ts:
                    tile_is_ready(dve, ("N2", T))
                    D.read(tt(PA[1][:, T % 2, :], PA[0][:, T % 2, :], tile(("N2", T)), ALU.add), ("N2", T))

            def scan(c):
                T, r = c // 2, slice(64 * (c % 2), 64 * (c % 2) + 64)
                tile_is_read(dve, ("u", T))
                tile_is_ready(dve, ("sv", c))
                D.read(tt(vnew[r, :], VT[r, T, :], tile(("sv", c))[r, :], ALU.subtract), ("sv", c))
                D(tt(v3(Stmp[:, :], 4), v3(S[:, :], 4), bc_h(egl[:, c, :]), ALU.mult))
                tile_is_ready(dve, ("ss", c))
                D.read(tt(S[:, :], Stmp[:, :], tile(("ss", c)), ALU.add), ("ss", c))
                if c == NC - 1:
                    D(dve.memset(S[:, :], 0.0), s_("scan_done"))

            def onorm(w):
                for T in range(NT):
                    dve.wait_ge(s_("o_sq"), 4 * w + T + 1)
                    D(dve.tensor_reduce(oss[:, 4 * T:4 * T + 4], v3(onsq[:, T % 2, :], 4), AX.X, ALU.add), s_("sq_reduced"))
                D(ts(oss, oss, 1.0 / DK, EPS, ALU.mult, ALU.add), s_("o_ms"))
                dve.wait_ge(s_("o_r"), w + 1)
                for T in range(NT):
                    y = v3(Y0[:, T, 512 * w:512 * w + 512], 4)
                    D(tt(y, y, bc_h(ors[:, 4 * T:4 * T + 4]), ALU.mult))

            HBf = HB.rearrange("p h t -> p (h t)")
            HQf = HQ.rearrange("p h t -> p (h t)")
            HKf = HK.rearrange("p h t -> p (h t)")

            def halves(ap, s):
                return ap.rearrange("p (b s) -> p b s", s=2 * s)

            def hgrn(step):
                if step[0] == "hdiag":
                    for T in range(NT):
                        tile_is_ready(dve, ("dg", T))
                        D.read(tt(v3(HAT[:, T, :], 4), v3(tile(("dg", T)), 4), bc_m(ident[:, :]), ALU.mult), ("dg", T))
                elif step[0] == "hlevel":
                    n = step[1]
                    s = LEVELS[n]
                    nb = 2048 // (2 * s)
                    b, e, p_ = halves(HBf, s), halves(LE, s), halves(LP, s)
                    ref = b[:, :, s - 1:s].broadcast_to([P, nb, s])
                    D(tt(e[:, :, 0:s], ref, b[:, :, 0:s], ALU.subtract))
                    D(tt(e[:, :, s:2 * s], b[:, :, s:2 * s], ref, ALU.subtract), s_("lv_args"))
                    dve.wait_ge(s_("lv_exp"), n + 1)
                    D(tt(p_[:, :, 0:s], halves(HKf, s)[:, :, 0:s], e[:, :, 0:s], ALU.mult))
                    D(tt(p_[:, :, s:2 * s], halves(HQf, s)[:, :, s:2 * s], e[:, :, s:2 * s], ALU.mult), s_("lp_ready"))
                    for T in range(NT):
                        tile_is_ready(dve, ("lv", n, T))
                        D.read(dve.copy_predicated(v3(HAT[:, T, :], 4), bc_m(lvmask[:, n, :]), v3(tile(("lv", n, T)), 4)), ("lv", n, T))
                elif step[0] == "hstate":
                    b = halves(HBf, CH // 2)
                    D(tt(halves(LE, CH // 2), b[:, :, CH - 1:CH].broadcast_to([P, 2048 // CH, CH]), b, ALU.subtract), s_("lv_args"))
                    dve.wait_ge(s_("lv_exp"), len(LEVELS) + 1)
                    D(tt(HKf, HKf, LE, ALU.mult), s_("hk_decayed"))
                    dve.wait_ge(s_("lv_exp"), len(LEVELS) + 2)
                    D(tt(HQf, HQf, LE, ALU.mult), s_("hq_decayed"))

            def hscan(c):
                D(tt(v3(Stmp[:, :], 4), v3(S[:, :], 4), bc_h(v3(LE, 4)[:, :, CH * c + CH - 1]), ALU.mult))
                tile_is_ready(dve, ("hs", c))
                D.read(tt(S[:, :], Stmp[:, :], tile(("hs", c)), ALU.add), ("hs", c))

            def dense_read_by_act(db, t):
                dve.wait_ge(dense_read["act"], evac_count(db, t))

            def evac(db):
                kind, which, c0 = BLOCKS[db]
                if which in ("q", "k", "v") :
                    dst = {"q": QF, "k": KF, "v": VF}[which]
                    for t in range(4):
                        g = 4 * db + t
                        w = [vec[:, 12 * j + g:12 * j + g + 1] for j in range(4)]
                        c, o = craw[:, t % 2, :], dst[:, t, :]
                        dense_read_by_act(db, t)
                        D(ts(o, c, w[3], None, ALU.mult))
                        for j in (2, 1):
                            d = 3 - j
                            D(stt(o[:, d:SEQ], c[:, 0:SEQ - d], w[j], o[:, d:SEQ], ALU.mult, ALU.add))
                        D(stt(o[:, 3:SEQ], c[:, 0:SEQ - 3], w[0], o[:, 3:SEQ], ALU.mult, ALU.add), s_("conv_done"))
                elif which == "hf":
                    for t in range(4):
                        dense_read_by_act(db, t)
                        D(ts(HB[:, t, :], HK[:, t, :], c1[:, t:t + 1], c2[:, t:t + 1], ALU.mult, ALU.add), s_("f_ready"))
                        D(ts(HK[:, t, :], HB[:, t, :], -1.0, 1.0, ALU.mult, ALU.add))
                    for t in range(4):
                        dve.wait_ge(s_("lf_ready"), t + 1)
                        D(dve.tensor_tensor_scan(HB[:, t, :], resetm[:, :], HQ[:, t, :], 0.0, ALU.mult, ALU.add), s_("b_ready"))
                elif which in ("z", "hg"):
                    wgt = gnw if which == "z" else hnw
                    w = int(which == "hg")
                    for t in range(4):
                        dense_read_by_act(db, t)
                        z = zt[:, t % 2, :]
                        y = Y0[:, t, 512 * w:512 * w + 512]
                        D(tt(v3(z, 4), v3(z, 4), bc_m(wgt[:, :]), ALU.mult))
                        D(tt(y, y, z, ALU.mult), s_("z_used"))
                elif kind == "odd_in" and which[0] in ("rq", "rk"):
                    dst = RQ if which[0] == "rq" else RK
                    dve.wait_ge(s_("ret_consts"), 48)
                    for hh in range(2):
                        dense_read_by_act(db, 2 * hh + 1)
                        D(tt(dst[:, hh, 0, :], rtmp[:, 0, :], cos_t, ALU.mult))
                        D(tt(rprod, rtmp[:, 1, :], sin_t, ALU.mult))
                        D(tt(dst[:, hh, 0, :], dst[:, hh, 0, :], rprod, ALU.subtract))
                        D(tt(dst[:, hh, 1, :], rtmp[:, 0, :], sin_t, ALU.mult))
                        D(tt(rprod, rtmp[:, 1, :], cos_t, ALU.mult), s_("rot_done"))
                        D(tt(dst[:, hh, 1, :], dst[:, hh, 1, :], rprod, ALU.add), s_("rot_ready"))
                elif kind == "odd_in" and which[0] == "rg":
                    h = which[1]
                    dve.wait_ge(s_("ro_r"), h + 1)
                    for t in range(4):
                        dense_read_by_act(db, t)
                        y = Y1[:, t, h * RDV:(h + 1) * RDV]
                        D(stt(y, y, ors[:, t:t + 1], gt[:, t % 2, :], ALU.mult, ALU.mult))
                        D(tt(y, y, rnw, ALU.mult), s_("g_used"))
                elif kind.endswith("out"):
                    for t in range(4):
                        dve.wait_ge(dense_ready, 4 * db + t + 1)
                        x = X[:, t, c0:c0 + 512]
                        D(tt(x, x, ps[:, t, :], ALU.add), dense_read["dve"])

            def score(h):
                dve.wait_ge(s_("dh_loaded"), 16 * (h + 1))
                if h > 0:
                    tile_is_ready(dve, ("ro", h - 1, NT - 1))
                for J in range(NT):
                    n = SEQ - P * J
                    tile_is_ready(dve, ("sc", h, J))
                    D.read(tt(RAT[:, J, 0:n], tile(("sc", h, J))[:, 0:n], DH[:, 0:n], ALU.mult), ("sc", h, J))

            def ro(h):
                tile_is_read(dve, ("ro", h, NT - 1))
                D(ts(oss[:, 0:4], oss[:, 0:4], 1.0 / RDV, EPS, ALU.mult, ALU.add), s_("ro_ms"))

            def pick_first(dst, eq):
                D(tt(eq, eq, bc_m(first4), ALU.mult))
                D(dve.tensor_reduce(mx2, eq, AX.X, ALU.max))
                D(tt(dst, eq, bc_h(mx2, 4), ALU.is_equal))

            def route(l):
                D(dve.memset(ar[:, 7168:9216], 0.0), s_("xg_cleared"))
                dve.wait_ge(s_("router_loaded"), 128 * (l + 1))
                D(dve.memset(ones, 1.0))
                D(dve.memset(ahead[:, 0, :], 0.0))
                D(dve.memset(onesrow, 1.0))
                D(dve.memset(any80[:, 64:80], 0.0))
                dve.wait_ge(s_("r_logits"), l + 1)
                D(ts(lgT, ps[0:20, 3, :], lgb, None, ALU.add), s_("r_lgT"))
                dve.wait_ge(s_("r_lg"), l + 1)
                D(dve.tensor_copy(lg, v3(ps[:, 7, 0:80], 4)))
                c, f = lg[:, :, 0:4], lg[:, :, 4:20]
                D(dve.tensor_reduce(mx, c, AX.X, ALU.max))
                D(tt(r_b, c, bc_h(mx, 4), ALU.is_equal))
                D(tt(r_a, c, bc_h(mx, 4), ALU.subtract), s_("r_cexp"))
                pick_first(gm, r_b)
                D(tt(r_c, f.rearrange("p T (g e) -> p T g e", g=4), gm.unsqueeze(3).broadcast_to([P, 4, 4, 4]), ALU.mult))
                D(dve.tensor_reduce(fs, r_c.rearrange("p T g e -> p T e g"), AX.X, ALU.add))
                D(dve.tensor_reduce(mx, fs, AX.X, ALU.max))
                D(tt(r_b, fs, bc_h(mx, 4), ALU.is_equal))
                pick_first(m1, r_b)
                D(stt(fs, m1, -1e30, fs, ALU.mult, ALU.add))
                D(dve.tensor_reduce(ed, fs, AX.X, ALU.max))
                D(tt(r_b, fs, bc_h(ed, 4), ALU.is_equal))
                pick_first(m2, r_b)
                D(tt(ed, ed, mx, ALU.subtract), s_("r_eexp"))
                for n, m in enumerate((m1, m2)):
                    D(tt(oh[n].rearrange("p T (g e) -> p T g e", g=4), gm.unsqueeze(3).broadcast_to([P, 4, 4, 4]),
                         m.unsqueeze(2).broadcast_to([P, 4, 4, 4]), ALU.mult))
                D(tt(anyh, oh[0], oh[1], ALU.add))
                D(dve.tensor_copy(ahead[:, 1, :], anyh[:, 0, :]))
                D(tt(ahead[:, 2, :], ahead[:, 1, :], anyh[:, 1, :], ALU.add))
                D(tt(ahead[:, 3, :], ahead[:, 2, :], anyh[:, 2, :], ALU.add))
                D(tt(ahead80[:, 64:80], ahead[:, 3, :], anyh[:, 3, :], ALU.add), s_("r_any"))
                dve.wait_ge(s_("r_exp"), 2 * l + 2)
                D(dve.tensor_reduce(gp, r_a, AX.X, ALU.add))
                D(ts(mx, ed, 1.0, None, ALU.add))
                D(tt(gp, gp, mx, ALU.mult))
                w = v3(w12, 4)
                D(dve.reciprocal(w[:, :, 0], gp))
                D(tt(w[:, :, 1], w[:, :, 0], ed, ALU.mult))
                dve.wait_ge(s_("r_pos"), l + 1)
                D(dve.tensor_copy(slotv, v3(ps[:, 7, 0:64], 4)))
                D(dve.tensor_copy(ncnt, ps[:, 7, 64:80]))
                D(ts(ovc, ncnt, 128.0, None, ALU.is_gt))
                D(stt(ovc, ncnt, 256.0, ovc, ALU.is_gt, ALU.add))
                D(stt(ovc, ncnt, 384.0, ovc, ALU.is_gt, ALU.add))
                D(dve.tensor_tensor_scan(ovi, onesrow, ovc, 0.0, ALU.mult, ALU.add))
                D(tt(ovt, ovi, ovc, ALU.subtract))
                D(ts(ovt, ovt, 128.0, 128.0 * NE - 128.0, ALU.mult, ALU.add))
                D(tt(ovt, ovt, offs16, ALU.subtract))
                D(ts(tmp64, slotv, 128.0, None, ALU.is_ge))
                D(tt(tmp64, tmp64, bc_m(ovt), ALU.mult))
                D(tt(slotv, slotv, tmp64, ALU.add))
                D(tt(slotv, slotv, bc_m(offs16), ALU.add))
                for n in range(2):
                    D(tt(tmp64, oh[n], slotv, ALU.mult))
                    D(dve.tensor_reduce(v3(slotf, 4)[:, :, n], tmp64, AX.X, ALU.add))
                D(dve.tensor_copy(slots_u, slotf))
                D(ts(sA_i, slots_u, 7, None, ALU.logical_shift_right))
                D(ts(sB_i, slots_u, P - 1, None, ALU.bitwise_and))
                D(dve.tensor_copy(slotA, sA_i))
                D(dve.tensor_copy(slotB, sB_i))
                D(tt(hotB, iotaB.unsqueeze(1).broadcast_to([P, 8, P]), slotB.unsqueeze(2).broadcast_to([P, 8, P]), ALU.is_equal))
                D(tt(hotA, iotaA.unsqueeze(1).broadcast_to([P, 8, SLOT_TILES]), slotA.unsqueeze(2).broadcast_to([P, 8, SLOT_TILES]), ALU.is_equal))
                D(tt(hotA, hotA, tokv.unsqueeze(2).broadcast_to([P, 8, SLOT_TILES]), ALU.mult), s_("r_hot"))
                D(tt(v3(cmp7, 7), bc_m(ovi, 7), iota8[:, 0:7].unsqueeze(2).broadcast_to([P, 7, 16]), ALU.is_le))
                D(dve.tensor_reduce(eidf[:, 0:7], v3(cmp7, 7), AX.X, ALU.add))
                D(ts(eidf[:, 0:7], eidf[:, 0:7], float(NE - 1), None, ALU.min))
                D(dve.tensor_copy(eidf[:, 7:8], ovi[:, 15:16]))
                D(dve.tensor_copy(eid[:, :], eidf[0:1, :]), s_("slots_known"))
                dve.wait_ge(s_("r_rows"), l + 1)
                D(ts(idx[:, 1, :], ps[:, 7, 0:SLOT_TILES], EMPTY, None, ALU.add))
                D(ts(idx[:, 0, :], idx[:, 1, :], 1, None, ALU.logical_shift_right), s_("rows_known"))

            def xT_lo(l, e, par):
                for g in range(2):
                    dve.wait_ge(s_("xT_hi"), e * 2 + (32 * l + g + 1))
                    tt(HTL[:, 2 * par + g, :], ps[:, 4 + g, :], HTH[:, 2 * par + g, :].bitcast(F32), ALU.subtract).then_inc(s_("xT_lo"), 1)

            def moe(l):
                m = MOE_PIECE[l]
                route(l)

                def lo_in(n, it=0):
                    dve.wait_ge(hi_done, it * 12 + (n + 1))
                    tt(wl[:, n % NSPL, :, :], raw[:, n % NRAW, :, :], wh[:, n % NSPL, :, :].bitcast(F32),
                       ALU.subtract).then_inc(lo_dve, 1)

                def gated(E, par):
                    dve.wait_ge(s_("silu_done"), E + 1)
                    tt(aact[:, par, :], sg[:, par, :], ps[:, par, FE:2 * FE], ALU.mult).then_inc(s_("act_done"), 1)

                xT_lo(l, 0, 0)
                lo_in(m + 4)
                lo_in(m + 5)
                xT_lo(l, 1, 1)
                lo_in(m + 6)
                gated(16 * l, 0)

                def expert(it, par):
                    E = it * 2 + (16 * l + par)
                    b = m + 4 + 6 * par
                    last = isinstance(it, int)
                    dve.wait_ge(s_("aT_hi"), E + 1)
                    tt(HTL[:, 4 + par, 0:256], ps[:, 6, 0:256], HTH[:, 4 + par, 0:256].bitcast(F32), ALU.subtract)\
                        .then_inc(s_("aT_lo"), 1)
                    if not last or par == 0:
                        for j in (3, 4, 5, 6):
                            lo_in(b + j, it)
                        gated(E + 1, 1 - par)
                        lo_in(b + 7, it)
                        if not last:
                            xT_lo(l, it * 2 + (par + 2), par)
                            lo_in(b + 8, it)

                with dve.Fori(0, NE // 2 - 1) as it:
                    for par in range(2):
                        expert(it, par)
                for par in range(2):
                    expert(NE // 2 - 1, par)
                n = overflow_flag(dve, l)
                with dve.If(n > 0):
                    with dve.Fori(0, 7) as j:
                        dve.wait_ge(s_(f"ov_silu{l}"), j + 1)
                        tt(aact[:, 0, :], sg[:, 0, :], ps[:, 0, FE:2 * FE], ALU.mult).then_inc(s_(f"ov_act{l}"), 1)
            for sm, n in ((s_("act_done"), 2), (s_("xT_lo"), 2), (s_("aT_lo"), 1), (lo_dve, 4)):
                for _ in range(n):
                    dve.nop().then_inc(sm, 1)
            for step in SCHEDULE:
                k = step[0]
                if k == "consts":
                    consts()
                elif k == "norm":
                    norm(step[1])
                elif k == "ba":
                    tile_is_ready(dve, "ba")
                    D.read(dve.tensor_copy(baT, tile("ba")[0:8, :]), "ba")
                elif k == "ba_tok":
                    gate_inputs()
                elif k == "gates":
                    gates()
                elif k == "tok":
                    tok(step[1], step[2])
                elif k == "l2":
                    l2()
                elif k == "gdn_chunks":
                    gdn_chunks(step[1])
                elif k == "scan":
                    scan(step[1])
                elif k == "onorm":
                    onorm(step[1])
                elif k in ("hdiag", "hlevel", "hstate"):
                    hgrn(step)
                elif k == "hscan":
                    hscan(step[1])
                elif k == "evac":
                    evac(step[1])
                elif k == "yT":
                    for T in range(NT):
                        lo_tiles(("yT", step[1], step[2], T), T)
                elif k == "score":
                    score(step[1])
                elif k == "ro":
                    ro(step[1])
                elif k == "moe":
                    moe(step[1])

        @block.tensor
        def _(pe):
            mm = nc.tensor.matmul
            tr = nc.tensor.transpose

            def open_tile(name):
                n = SIDE_AT[name]
                if n >= 4:
                    tile_is_read(pe, SIDE[n - 4][0])
                return tile(name)

            def done(ins):
                ins.then_inc(tile_ready, 1)

            def four(name, f):
                t = open_tile(name)
                for h in range(NH):
                    ins = f(t[:, cols(h)], h)
                done(ins)

            def norm(n):
                for T in range(NT):
                    pe.wait_ge(s_("h_ready"), 4 * n + T + 1)
                    for g in range(2):
                        t = open_tile(("hT", n, T, g))
                        for j in range(4):
                            k = 4 * g + j
                            ins = tr(t[:, cols(j)], htok(n)[:, T % 2, k:DM:KD], ident[:, :])
                        done(ins)
                    if n in (1, 3) and T % 2 == 1:
                        c = slice(P * (T - 1), P * (T + 1))
                        tile_is_read(pe, ("hT", n, T, 1))
                        if T == 1:
                            pe.wait_ge(s_("router_loaded"), 64 * (n + 1))
                            pe.wait_ge(*x_ready(n, NT - 1))
                        for k in range(KD):
                            ins = mm(ps[0:20, 3, c], rw[:, k, :], hTf[:, k, c], start=k == 0, stop=k == KD - 1)
                        if T == NT - 1:
                            ins.then_inc(s_("r_logits"), 1)

            def yT(l, kh):
                for T in range(NT):
                    if l == 0:
                        pe.wait_ge(s_("z_used"), 4 + T + 1)
                    else:
                        pe.wait_ge(s_("g_used"), 4 * (2 * kh + 1) + T + 1)
                    for g in range(2):
                        t = open_tile(("yT", l, kh, T, g))
                        for j in range(4):
                            c = (4 * g + j) * P
                            src = Y0[:, T, c:c + P] if l == 0 else Y1[:, T, kh * DM + c:kh * DM + c + P]
                            ins = tr(t[:, cols(j)], src, ident[:, :])
                        done(ins)

            def ba_product():
                tile_is_read(pe, ("hT", 0, NT - 1, 1))
                pe.wait_ge(s_("wba_lo"), 1)
                t = open_tile("ba")
                for k in range(KD):
                    ins = mm3(t[0:8, :], wba_h[:, k, :], wba_l[:, k, :], HTH[:, k, :], HTL[:, k, :], k == 0, k == KD - 1)
                done(ins)

            def ba_by_token():
                tile_is_read(pe, "ba")
                t = open_tile("ba_tok")
                for T in range(NT):
                    ins = tr(t[:, 8 * T:8 * T + 8], baT[:, cols(T)], ident[0:8, 0:8])
                done(ins)

            def hT_ready(db):
                last = {0: ("hT", 0), 8: ("yT", 0, 0), 10: ("hT", 2), 22: ("yT", 1, 0), 24: ("yT", 1, 1)}.get(db)
                if last:
                    tile_is_read(pe, last + (NT - 1, 1))

            def piece(db, kp):
                i = first_piece(db) + kp
                sl = i % NSPL
                kind, which, _c = BLOCKS[db]
                if kp == 0:
                    hT_ready(db)
                pe.wait_ge(hi_done, i + 1)
                wait_lo(pe, i)
                feature = which in ("q", "k", "v", "hf", "hq") or (kind == "odd_in" and which[0] in ("rq", "rk"))
                for t in range(NT):
                    if kp == 0 and db > 0:
                        pe.wait_ge(dense_read[evac_engine(db - 1)], evac_count(db - 1, t))
                    for k2 in range(2):
                        k = 2 * kp + k2
                        first, last = kp == 0 and k2 == 0, kp == 3 and k2 == 1
                        if feature:
                            c = cols(t) if kind == "even_in" else slice(256 * (t // 2) + t % 2, 256 * (t // 2 + 1), 2)
                            ins = mm3(ps[:, t, :], wh[:, sl, k2, c], wl[:, sl, k2, c], HTH[:, k, :], HTL[:, k, :], first, last)
                        else:
                            ins = mm3(ps[:, t, :], HTH[:, k, cols(t)], HTL[:, k, cols(t)], wh[:, sl, k2, :], wl[:, sl, k2, :], first, last)
                    if kp == 3:
                        ins.then_inc(dense_ready, 1)
                if kp < 3:
                    ins.then_inc(piece_used, 1)

            def tok(nm, T):
                src, n = {"q": (QF, 4), "k": (KF, 8), "v": (VF, 12)}[nm]
                pe.wait_ge(s_("conv_silu"), n)
                four(("tok", nm, T), lambda o, h: tr(o, src[:, h, cols(T)], ident[:, :]))

            def gates():
                pe.wait_ge(s_("g_ready"), 1)
                done(mm(open_tile("gc")[:, 0:16], U[:, :], gg, start=True, stop=True))

            def l2():
                for T in range(NT):
                    pe.wait_ge(s_("qk_normed"), 2 * T + 2)
                    four(("qb", T), lambda o, h: tr(o, Y0[:, T, cols(h)], ident[:, :]))
                    four(("kb", T), lambda o, h: tr(o, KT[:, T, cols(h)], ident[:, :]))

            def gdn_chunks(pr):
                Ts = (2 * pr, 2 * pr + 1)

                def prod(name, T, lh, rh):
                    q = T % 2
                    four(name, lambda o, h: mm(o, PA[lh][:, q, cols(h)], PA[rh][:, q, cols(h)], start=True, stop=True))

                for T in Ts:
                    tile_is_read(pe, ("qb", T))
                    tile_is_read(pe, ("kb", T))
                    four(("Gb", T), lambda o, h: mm(o, gg[:, 4 * T + h:4 * T + h + 1].broadcast_to([P, P]), U[:, :], start=True, stop=True))
                    four(("KK", T), lambda o, h: mm(o, KF[:, h, cols(T)], KF[:, h, cols(T)], start=True, stop=True))
                    four(("KQ", T), lambda o, h: mm(o, KF[:, h, cols(T)], QF[:, h, cols(T)], start=True, stop=True))
                    tile_is_read(pe, ("KK", T))
                    four(("DT", T), lambda o, h: tr(o, PA[0][:, T % 2, cols(h)], ident[:, :]))
                for T in Ts:
                    tile_is_read(pe, ("DT", T))
                    prod(("P2", T), T, 4, 0)
                    prod(("P2T", T), T, 0, 4)
                for r in (1, 2, 3):
                    for T in Ts:
                        if r == 1:
                            pe.wait_ge(s_("x1_ready"), T + 1)
                            tile_is_read(pe, ("P2T", T))
                        else:
                            tile_is_read(pe, ("XT", r - 1, T))
                            tile_is_read(pe, ("P", 1, T) if r == 2 else ("PT", 2, T))
                        prod(("X", r, T), T, 6, 7)
                        prod(("XT", r, T), T, 7, 6)
                        if r < 3:
                            prod(("PT", r, T), T, 5, 6)
                        if r == 1:
                            prod(("P", r, T), T, 6, 5)
                for T in Ts:
                    tile_is_read(pe, ("XT", 3, T))
                    prod(("B", T), T, 8, 3)
                    prod(("BT", T), T, 3, 8)
                for T in Ts:
                    tile_is_read(pe, ("BT", T))
                    prod(("B2", T), T, 6, 5)
                for T in Ts:
                    tile_is_read(pe, ("B2", T))
                    pe.wait_ge(s_("n1_ready"), T + 1)
                    prod(("N2", T), T, 4, 0)
                for T in Ts:
                    tile_is_read(pe, ("N2", T))
                    prod(("IT", T), T, 7, 1)
                for T in Ts:
                    tile_is_read(pe, ("IT", T))
                    pe.wait_ge(s_("vk_ready"), T + 1)
                    prod(("u", T), T, 8, 9)
                    prod(("wT", T), T, 10, 8)

            def scan(c):
                T, p0 = c // 2, 64 * (c % 2)
                r, tc = slice(p0, p0 + 64), slice(P * T + p0, P * T + p0 + 64)
                tile_is_read(pe, ("wT", T))
                pe.wait_ge(s_("vk_ready"), NT)
                if c > 0:
                    tile_is_read(pe, ("ss", c - 1))
                t = open_tile(("sv", c))
                for h in range(NH):
                    ins = mm(t[r, cols(h)], KF[:, h, tc], S[:, cols(h)], start=True, stop=True)
                done(ins)
                t = open_tile(("so", c))
                tile_is_read(pe, ("sv", c))
                for h in range(NH):
                    mm(t[r, cols(h)], QF[:, h, tc], S[:, cols(h)], start=True, stop=False)
                    ins = mm(t[r, cols(h)], AT0[r, T, P * h + p0:P * h + p0 + 64], vnew[r, cols(h)], start=False, stop=True)
                done(ins)
                t = open_tile(("ss", c))
                for h in range(NH):
                    ins = mm(t[:, cols(h)], KT[r, T, cols(h)], vnew[r, cols(h)], start=True, stop=True)
                done(ins)

            def hgrn(step):
                if step[0] == "hdiag":
                    pe.wait_ge(dense_read["act"], evac_count(4, 3))
                    pe.wait_ge(s_("b_ready"), 4)
                    for T in range(NT):
                        four(("dg", T), lambda o, h: mm(o, HK[:, h, cols(T)], HQ[:, h, cols(T)], start=True, stop=True))
                elif step[0] == "hlevel":
                    pe.wait_ge(s_("lp_ready"), step[1] + 1)
                    lp = v3(LP, 4)
                    for T in range(NT):
                        four(("lv", step[1], T), lambda o, h: mm(o, lp[:, h, cols(T)], lp[:, h, cols(T)], start=True, stop=True))
                elif step[0] == "hstate":
                    pe.wait_ge(s_("hk_decayed"), 1)
                    for T in range(NT):
                        four(("kd", T), lambda o, h: tr(o, HK[:, h, cols(T)], ident[:, :]))

            def hscan(c):
                T, p0 = c // 2, 64 * (c % 2)
                r, tc = slice(p0, p0 + 64), slice(P * T + p0, P * T + p0 + 64)
                pe.wait_ge(s_("hq_decayed"), 1)
                pe.wait_ge(s_("scan_done"), 1)
                tile_is_read(pe, ("kd", T))
                if c > 0:
                    tile_is_read(pe, ("hs", c - 1))
                t = open_tile(("ho", c))
                for h in range(NH):
                    mm(t[r, cols(h)], HQ[:, h, tc], S[:, cols(h)], start=True, stop=False)
                    ins = mm(t[r, cols(h)], HAT[r, T, P * h + p0:P * h + p0 + 64], HI[r, T, cols(h)], start=False, stop=True)
                done(ins)
                t = open_tile(("hs", c))
                for h in range(NH):
                    ins = mm(t[:, cols(h)], KDT[r, T, cols(h)], HI[r, T, cols(h)], start=True, stop=True)
                done(ins)

            def score(h):
                pe.wait_ge(s_("rot_ready"), 4 * (h // 2) + 3 + h % 2)
                for J in range(NT):
                    t = open_tile(("sc", h, J))
                    n = SEQ - P * J
                    mm(t[:, 0:n], RK[:, h % 2, 0, cols(J)], RQ[:, h % 2, 0, P * J:SEQ], start=True, stop=False)
                    done(mm(t[:, 0:n], RK[:, h % 2, 1, cols(J)], RQ[:, h % 2, 1, P * J:SEQ], start=False, stop=True))

            def ro(h):
                tile_is_read(pe, ("sc", h, NT - 1))
                pe.wait_ge(dense_read["act"], evac_count([b for b, x in enumerate(BLOCKS) if x[1] == ("rv", h)][0], 3))
                for T in range(NT):
                    t = open_tile(("ro", h, T))
                    for J in range(T + 1):
                        ins = mm(t, RAT[:, J, P * (T - J):P * (T - J) + P], RV[:, h % 2, J, :], start=J == 0, stop=J == T)
                    done(ins)

            def xT(l, e, par, loads):
                pe.wait_ge(s_(f"xg_loaded{par}"), loads)
                for g in range(2):
                    pe.wait_ge(s_("xT_lo"), e * 2 + (32 * l + g + 1))
                    for j in range(4):
                        ins = tr(ps[:, 4 + g, cols(j)], xg[:, par, 4 * g + j:DM:KD], ident[:, :])
                    ins.then_inc(s_("xT_ready"), 1)

            def moe(l):
                m = MOE_PIECE[l]
                for t in range(4):
                    tile_is_read(pe, SIDE[SIDE_AT[("hT", 2 * l + 1, NT - 1, 1)] - t][0])
                pe.wait_ge(s_("r_lgT"), l + 1)
                for T in range(NT):
                    ins = tr(ps[:, 7, 20 * T:20 * T + 20], lgT[:, cols(T)], ident[0:20, 0:20])
                ins.then_inc(s_("r_lg"), 1)
                pe.wait_ge(s_("r_any"), l + 1)
                mm(ps[:, 7, 0:80], Lst, any80, start=True, stop=False)
                ins = mm(ps[:, 7, 0:80], ones, ahead80, start=False, stop=True)
                ins.then_inc(s_("r_pos"), 1)
                pe.wait_ge(s_("r_hot"), l + 1)
                for n in range(8):
                    ins = mm(ps[:, 7, 0:SLOT_TILES], hotB[:, n, :], hotA[:, n, :], start=n == 0, stop=n == 7)
                ins.then_inc(s_("r_rows"), 1)

                def split_ready(n, it):
                    pe.wait_ge(hi_done, it * 12 + (n + 1))
                    if n < m + 4:
                        pe.wait_ge(lo_pool, lo_count(n))
                    else:
                        pe.wait_ge(lo_dve, it * 12 + lo_count(n))
                    return n % NSPL

                def gate_up(par, j, n, it=0):
                    sl = split_ready(n, it)
                    for k2 in range(2):
                        k = 2 * j + k2
                        a_ = 2 * par + k // 4
                        ins = mm3(ps[:, par, :], HTH[:, a_, cols(k % 4)], HTL[:, a_, cols(k % 4)], wh[:, sl, k2, :], wl[:, sl, k2, :],
                                  k == 0, k == KD - 1)
                    ins.then_inc(s_("moe_used"), 1)

                base = 144 * l + 16
                xT(l, 0, 0, base)
                pe.wait_ge(s_("act_done"), 16 * l + 1)
                pe.wait_ge(s_("xT_lo"), 32 * l + 4)
                gate_up(0, 0, m)
                gate_up(0, 1, m + 1)
                xT(l, 1, 1, base)
                gate_up(0, 2, m + 2)
                gate_up(0, 3, m + 3)

                def expert(it, par):
                    E = it * 2 + (16 * l + par)
                    b = m + 4 + 6 * par
                    last = isinstance(it, int)
                    pe.wait_ge(s_("act_done"), E + 3)
                    pe.wait_ge(s_("aT_lo"), E + 1)
                    for k in range(2):
                        ins = tr(ps[:, 6, cols(k)], aact[:, par, cols(k)], ident[:, :])
                    ins.then_inc(s_("aT_ready"), 1)
                    n0 = 0
                    if not last or par == 0:
                        n0 = 4
                        pe.wait_ge(s_("xT_lo"), it * 4 + (32 * l + 2 * par + 6))
                        for j in range(4):
                            gate_up(1 - par, j, b + j, it)
                        if not last:
                            xT(l, it * 2 + (par + 2), par, it * 16 + (base + 16))
                    pe.wait_ge(s_("aT_lo"), E + 2)
                    for hf in range(2):
                        sl = split_ready(b + n0 + hf, it)
                        pe.wait_ge(s_("y_read"), E * 2 + (hf + 1))
                        for k in range(2):
                            ins = mm3(ps[:, 2 + hf, :], HTH[:, 4 + par, cols(k)], HTL[:, 4 + par, cols(k)], wh[:, sl, k, :], wl[:, sl, k, :],
                                      k == 0, k == 1)
                        ins.then_inc(s_("moe_used"), 1)

                with pe.Fori(0, NE // 2 - 1) as it:
                    for par in range(2):
                        expert(it, par)
                for par in range(2):
                    expert(NE // 2 - 1, par)
                pe.wait_ge(s_("y_read"), 32 * (l + 1) + 2)
                n = overflow_flag(pe, l)
                with pe.If(n > 0):
                    pe.wait_ge(s_("xT_lo"), 32 * (l + 1) + 2)
                    with pe.Fori(0, 7) as j:
                        pe.wait_ge(s_(f"ov_x{l}"), j * 16 + 16)
                        pe.wait_ge(s_(f"ov_w{l}"), j * 32 + 32)
                        for g in range(2):
                            for q in range(4):
                                ins = tr(ps[:, 4 + g, cols(q)], xg[:, 0, 4 * g + q:DM:KD], ident[:, :])
                            ins.then_inc(s_(f"ov_xT{l}"), 1)
                        pe.wait_ge(s_(f"ov_xTr{l}"), j * 2 + 2)
                        for k in range(KD):
                            ins = mm(ps[:, 0, :], hTf[:, k, 0:P], ovWg[:, k, :], start=k == 0, stop=k == KD - 1)
                        ins.then_inc(s_(f"ov_gu{l}"), 1)
                        pe.wait_ge(s_(f"ov_act{l}"), j + 1)
                        for k in range(2):
                            ins = tr(ps[:, 6, cols(k)], aact[:, 0, cols(k)], ident[:, :])
                        ins.then_inc(s_(f"ov_aT{l}"), 1)
                        pe.wait_ge(s_(f"ov_aTr{l}"), j + 1)
                        for hf in range(2):
                            for k in range(2):
                                ins = mm(ps[:, 2 + hf, :], hTf[:, k, P:2 * P], ovWd[:, k, 512 * hf:512 * hf + 512], start=k == 0, stop=k == 1)
                            ins.then_inc(s_(f"ov_yp{l}"), 1)

            pe.wait_ge(s_("consts_loaded"), 16 * 13)
            for step in SCHEDULE:
                k = step[0]
                if k == "consts":
                    done(tr(open_tile("vec")[:, 0:60], raw_vec[0:60, :], ident[0:60, 0:60]))
                elif k == "norm" and step[1] < 4:
                    norm(step[1])
                elif k == "ba":
                    ba_product()
                elif k == "ba_tok":
                    ba_by_token()
                elif k == "piece":
                    piece(step[1], step[2])
                elif k == "tok":
                    tok(step[1], step[2])
                elif k == "gates":
                    gates()
                elif k == "l2":
                    l2()
                elif k == "gdn_chunks":
                    gdn_chunks(step[1])
                elif k == "scan":
                    scan(step[1])
                elif k in ("hdiag", "hlevel", "hstate"):
                    hgrn(step)
                elif k == "hscan":
                    hscan(step[1])
                elif k == "yT":
                    yT(step[1], step[2])
                elif k == "score":
                    score(step[1])
                elif k == "ro":
                    ro(step[1])
                elif k == "moe":
                    moe(step[1])


def shape_constants():
    i = np.arange(P)
    same = i[:, None] // CH == i[None, :] // CH
    c = {"c_ident": np.eye(P), "c_U": same & (i[:, None] <= i[None, :])}
    b16 = i[:, None] // 16 == i[None, :] // 16
    c["c_m16"] = b16 & (i[:, None] > i[None, :])
    c["c_moff"] = same & ~b16 & (i[:, None] > i[None, :])
    c["c_Lst"] = i[:, None] < i[None, :]
    c["c_reset"] = np.broadcast_to(np.arange(SEQ) % CH != 0, (P, SEQ))
    T, j = np.arange(NT), np.arange(2)
    c["c_tok"] = (2 * (P * T[None, :, None] + i[:, None, None]) + j[None, None, :]).reshape(P, 8) - EMPTY
    c["c_first"] = np.broadcast_to(np.array([4, 3, 2, 1]), (P, 4))
    c["c_iota"] = np.broadcast_to(np.concatenate([np.arange(8), P * np.arange(NE), np.arange(SLOT_TILES), i]), (P, 24 + SLOT_TILES + P))
    f = np.float32
    inv = f(1.0) / (f(10000.0) ** np.linspace(0.0, 1.0, RDK // 2, dtype=f))
    ang = (np.arange(SEQ, dtype=f)[None, :] * inv.astype(f)[:, None]).astype(f).astype(np.float64)
    c["c_cos"], c["c_sin"] = np.cos(ang), np.sin(ang)
    lg = np.log(1.0 - 2.0 ** (-5.0 - np.arange(NH)))
    rel = np.arange(SEQ)[None, :] - i[:, None]
    c["c_decay"] = np.where(rel >= 0, np.exp(np.maximum(rel, 0) * lg[:, None, None]), 0.0) * RDK ** -0.5
    c = {k: np.ascontiguousarray(v, dtype=np.float32) for k, v in c.items()}
    lv = [(i[:, None] // (2 * s) == i[None, :] // (2 * s)) & (i[:, None] % (2 * s) < s) & (i[None, :] % (2 * s) >= s) for s in LEVELS]
    c["c_lv"] = np.ascontiguousarray(np.stack(lv, 1), dtype=np.float32)
    return c


_INS = ['x', 'norm_mix_w', 'norm_ffn_w', 'even_w_in', 'gdn_conv_w', 'gdn_a_log', 'gdn_dt_bias', 'gdn_norm_w', 'hgrn_lb_logits',
        'hgrn_norm_w', 'even_w_out', 'odd_w_in', 'ret_norm_w', 'odd_w_out', 'router_c_w', 'router_c_b', 'router_f_w',
        'router_f_b', 'moe_w_gate_up', 'moe_w_down', 'final_norm_w']


def kernel(**inputs):
    import concourse.bacc as _bacc
    from concourse.bass_utils import run_bass_kernel_spmd as _run

    nc = _bacc.Bacc("TRN2", target_bir_lowering=False, num_devices=1)
    arrays, aps = {}, {}
    for name, v in [(n, inputs[n]) for n in _INS] + sorted(shape_constants().items()):
        v = np.ascontiguousarray(v)
        arrays[f"in_{name}_dram"] = v
        aps[name] = nc.dram_tensor(f"in_{name}_dram", v.shape, mybir.dt.from_np(v.dtype), kind="ExternalInput").ap()
    out = nc.dram_tensor("out_0_dram", (1, SEQ, DM), F32, kind="ExternalOutput").ap()
    build(nc, aps, out)
    r = _run(nc, [arrays], core_ids=[0])
    return r.results[0]["out_0_dram"]
```

```python
from contextlib import ExitStack

import concourse.bass as bass
from concourse import mybir
import numpy as np

F32 = mybir.dt.float32
F32R = mybir.dt.float32r
I32 = mybir.dt.int32
I8 = mybir.dt.int8
U32 = mybir.dt.uint32
ALU = mybir.AluOpType
ACT = mybir.ActivationFunctionType
AX = mybir.AxisListType

P = 128
SEQ = 512
DM = 1024
NT = SEQ // P
KD = DM // P
NH = 4
DK = 128
CH = 64
NC = SEQ // CH
RDV = 512
RDK = 256
NE = 16
NG = 4
EPG = 4
FE = 256
EPS = 1e-6
NRAW = 6
NRAW_MOE = 12
NRAW_ONCE = 6
NSPL = 4
SLOT_TILES = NE + 7
EMPTY = 4096.0
LEVELS = (32, 16, 8, 4, 2, 1)

EVEN_COL = {"q": 0, "k": 512, "v": 1024, "z": 1536, "hq": 2056, "hf": 2568, "hi": 3080, "hg": 3592}
BLOCKS = [("even_in", n, EVEN_COL[n]) for n in ("q", "k", "v", "hf", "hq", "hi", "z", "hg")]
BLOCKS += [("even_out", 0, 0), ("even_out", 0, 512)]
for pair in range(2):
    qk = [("odd_in", ("rq", pair), 512 * pair), ("odd_in", ("rk", pair), 1024 + 512 * pair)]
    v = [("odd_in", ("rv", 2 * pair + h), 2048 + 1024 * pair + 512 * h) for h in range(2)]
    BLOCKS += [v[0]] + qk + v[1:] if pair == 0 else qk + v
    BLOCKS += [("odd_in", ("rg", 2 * pair + h), 4096 + 1024 * pair + 512 * h) for h in range(2)]
BLOCKS += [("odd_out", kh, c) for kh in range(2) for c in (0, 512)]
MOE_AT = (10, 26)
MOE_PIECE = (4 * 10, 4 * 26 + 6 * NE)
NPIECE = 4 * len(BLOCKS) + 12 * NE


def first_piece(db):
    return 4 * db + (6 * NE if db >= MOE_AT[0] else 0)


def ahead_of_rows(db, t):
    i = first_piece(db)
    return {0: [i + 3] if db != MOE_AT[0] else [], NT - 1: [i + 4, i + 5, i + 6]}.get(t, [])


def raw_slot(i):
    for m in MOE_PIECE:
        if m <= i < m + 6 * NE:
            q = i - m
            if NRAW_MOE <= q < NRAW_MOE + NRAW_ONCE:
                return q
            r = (q if q < NRAW_MOE else q - NRAW_MOE - NRAW_ONCE) % NRAW_MOE
            return (m + r) % NRAW if r < NRAW else r
    return i % NRAW


RAW_SLOTS = [raw_slot(i) for i in range(NPIECE)]


def raw_before(i):
    return max((j for j in range(i) if RAW_SLOTS[j] == RAW_SLOTS[i]), default=None)


def raw_load(i):
    return sum(RAW_SLOTS[j] == RAW_SLOTS[i] for j in range(i + 1))


def rot_index(db):
    return [b for b, (_, w, _) in enumerate(BLOCKS) if isinstance(w, tuple) and w[0] in ("rq", "rk")].index(db)


def evac_engine(db):
    return "dve" if BLOCKS[db][0].endswith("out") else "act"


def evac_count(db, t):
    return 4 * sum(evac_engine(b) == evac_engine(db) for b in range(db)) + t + 1


def lo_by_dve(i):
    return any(m + 4 <= i < m + 6 * NE for m in MOE_PIECE)


def lo_count(i):
    return sum(lo_by_dve(j) == lo_by_dve(i) for j in range(i + 1)) + 4 * lo_by_dve(i)


def schedule():
    s = [("norm", 0), ("consts",)]

    def block(db, side=((), (), (), ())):
        for kp in range(4):
            s.append(("piece", db, kp))
            s.extend(side[kp])
        s.append(("evac", db))

    block(0)
    s.append(("ba",))
    block(1)
    s.append(("ba_tok",))
    block(2, ([("tok", "q", T) for T in range(NT)], (), [("gates",)] + [("tok", "k", T) for T in range(NT)], ()))
    s.extend(("tok", "v", T) for T in range(NT))
    s.append(("l2",))
    for T in range(NT):
        s += [("gdn_decay", T), ("piece", 3, T), ("gdn_x1", T)]
        if T % 2:
            s.append(("gdn_inverse", T // 2))
    for c in range(NC):
        s.append(("scan", c))
        if c == 0:
            s.append(("evac", 3))
        s.append(("piece", 4 + c // 4, c % 4))
        if c < 4:
            s.append(("fcum", c))
        if c == 3:
            s.append(("evac", 4))
    s += [("evac", 5), ("hdiag",), ("onorm", 0, (0, 1)), ("piece", 6, 0)]
    for n in range(len(LEVELS)):
        s.append(("hlevel", n))
        if n == 0:
            s.append(("onorm", 0, (2, 3)))
        if n < 2:
            s.append(("oscale", 0, (2 * n, 2 * n + 1)))
        if n == 2:
            s.append(("piece", 6, 3))
        if n in (2, 3):
            s += [("evac_gate", 6, 2 * n - 4), ("evac_gate", 6, 2 * n - 3)]
        if n < 2:
            s.append(("piece", 6, n + 1))
        if n > 2:
            s.append(("piece", 7, n - 3))
    s += [("hstate",), ("piece", 7, 3)]
    for T in range(NT + 1):
        if T < NT:
            s.append(("hscan", 2 * T))
        if T > 0:
            s.append(("onorm", 1, (T - 1,)))
        if T < NT:
            s.append(("hscan", 2 * T + 1))
        if T > 0:
            s += [("oscale", 1, (T - 1,)), ("evac_gate", 7, T - 1)]
        if T > 1:
            s.append(("yT", 0, 0, (T - 2,)))
        if T > 2:
            s.append(("rows", 8, T - 3))
    s += [("yT", 0, 0, (NT - 1,)), ("rows", 8, 2), ("rows", 8, 3), ("evac", 8)]
    block(9)
    s.append(("norm", 1))
    s.append(("moe", 0))
    s.append(("norm", 2))
    for pair in range(2):
        b = 10 + 6 * pair
        h0, h1 = 2 * pair, 2 * pair + 1
        if pair == 0:
            s += [("rows", b, t) for t in range(NT)] + [("evac", b)]
        else:
            block(b)
        block(b + 1)
        block(b + 2)
        block(b + 3, ((), [("score", h0)], [("ro", h0)], ()))
        block(b + 4, ((), [("score", h1)], (), ()))
        s.append(("ro", h1))
        block(b + 5)
    for kh in range(2):
        for T in range(NT):
            s.append(("yT", 1, kh, (T,)))
            if T > 0:
                s.append(("rows", 22 + 2 * kh, T - 1))
        s += [("rows", 22 + 2 * kh, NT - 1), ("evac", 22 + 2 * kh)]
        block(23 + 2 * kh)
    s.append(("norm", 3))
    s.append(("moe", 1))
    s.append(("norm", 4))
    return s


def side_tiles(step):
    k = step[0]
    if k == "consts":
        return [("vec", "dve")]
    if k == "norm" and step[1] < 4:
        who = "act" if step[1] in (1, 3) else "dve"
        return [(("hT", step[1], T, g), who) for T in range(NT) for g in range(2)]
    if k == "yT":
        return [(("yT", step[1], step[2], T, g), "dve") for T in step[3] for g in range(2)]
    if k == "ba":
        return [("ba", "dve")]
    if k == "ba_tok":
        return [("ba_tok", "dve")]
    if k == "tok":
        return [(("tok", step[1], step[2]), "act")]
    if k == "gates":
        return [("gc", "dve")]
    if k == "l2":
        return [((n, T), "act") for T in range(NT) for n in ("qb", "kb")]
    if k == "gdn_decay":
        T = step[1]
        return [(("Gb", T), "act"), (("KK", T), "dve"), (("KQ", T), "dve")]
    if k == "gdn_x1":
        return [(("DT", step[1]), "act")]
    if k == "gdn_inverse":
        Ts = (2 * step[1], 2 * step[1] + 1)
        out = []
        for T in Ts:
            out += [(("P2", T), "act"), (("P2T", T), "act")]
        for r in (1, 2):
            for T in Ts:
                out += [(("X", r, T), "dve"), (("XT", r, T), "dve"), (("PT", r, T), "act")]
                if r == 1:
                    out += [(("P", r, T), "act")]
        for T in Ts:
            out += [(("X", 3, T), "dve"), (("XT", 3, T), "dve")]
        for T in Ts:
            out += [(("B", T), "act"), (("BT", T), "act")]
        for T in Ts:
            out += [(("B2", T), "act")]
        for T in Ts:
            out += [(("N2", T), "dve")]
        for T in Ts:
            out += [(("IT", T), "act")]
        for T in Ts:
            out += [(("u", T), "act"), (("wT", T), "act")]
        return out
    if k == "scan":
        c = step[1]
        return [(("sv", c), "dve"), (("so", c), "act"), (("ss", c), "dve")]
    if k == "hdiag":
        return [(("dg", T), "dve") for T in range(NT)]
    if k == "hlevel":
        return [(("lv", step[1], T), "dve") for T in range(NT)]
    if k == "hstate":
        return [(("kd", T), "act") for T in range(NT)]
    if k == "hscan":
        return [(("ho", step[1]), "act"), (("hs", step[1]), "dve")]
    if k == "score":
        return [(("sc", step[1], J), "dve") for J in range(NT)]
    if k == "ro":
        return [(("ro", step[1], T), "act") for T in range(NT)]
    return []


SCHEDULE = schedule()


def onorm_count(w, Ts):
    return [st for st in SCHEDULE if st[0] == "onorm"].index(("onorm", w, Ts)) + 1


SIDE = [t for st in SCHEDULE for t in side_tiles(st)]
SIDE_AT = {name: n for n, (name, _) in enumerate(SIDE)}
SIDE_READ = {}
for _n, (_name, _who) in enumerate(SIDE):
    SIDE_READ[_name] = sum(w == _who for _, w in SIDE[:_n + 1])


def build(nc, a, out):
    ctx = ExitStack()
    with ctx:
        def sb(name, shape, dt=F32):
            return ctx.enter_context(nc.sbuf_tensor(name, shape, dt))

        def sem(name):
            return ctx.enter_context(nc.semaphore(name))

        hs_dram = [nc.dram_tensor(f"hs{l}", (SEQ, DM), F32, kind="Internal").ap() for l in range(2)]
        y2_dram = [nc.dram_tensor(f"y2{l}", (2 * SEQ, DM), F32, kind="Internal").ap() for l in range(2)]

        raw = sb("raw", [P, NRAW, 2, 512])
        wh = sb("wh", [P, NSPL, 2, 512], F32R)
        wl = sb("wl", [P, NSPL, 2, 512], F32R)
        X = sb("x", [P, NT, DM])
        HTH = sb("hT_hi", [P, KD, SEQ], F32R)
        HTL = sb("hT_lo", [P, KD, SEQ], F32R)
        ident = sb("ident", [P, P])
        U = sb("cum_upper", [P, P])
        m16 = sb("mask16", [P, P])
        moff = sb("mask_off", [P, P])
        lvmask = sb("level_masks", [P, len(LEVELS), P], I8)
        resetm = sb("reset", [P, SEQ])
        vec = sb("vec", [P, 60])
        small = sb("small", [P, 420])
        wba_h = sb("wba_hi", [P, KD, 8], F32R)
        wba_l = sb("wba_lo", [P, KD, 8], F32R)
        S = sb("state", [P, 512])
        Stmp = sb("state_decayed", [P, 512])
        vnew = sb("vnew", [P, 512])
        gnw = sb("gdn_w", [P, P])
        hnw = sb("hgrn_w", [P, P])
        ar = sb("arena", [P, 22528])
        idx = sb("slot_rows", [P, 2, SLOT_TILES], I32)
        cur = sb("cur_rows", [P, 4], U32)
        eid = sb("overflow_expert", [1, 8], I32)
        ps = ctx.enter_context(nc.psum_tensor("ps", [P, 8, 512], F32))

        def reg(off, n):
            return ar[:, off:off + n]

        def v3(ap, k):
            return ap.rearrange("p (k n) -> p k n", k=k)

        ss = small[:, 0:4]
        ms = small[:, 4:8]
        rs = small[:, 8:12]
        mhalf = small[:, 12:44]
        ba = v3(small[:, 44:76], 4)
        beta = small[:, 76:92]
        gg = small[:, 92:108]
        gc = small[:, 108:124]
        egc = small[:, 124:140]
        bege = small[:, 140:156]
        kde = small[:, 156:172]
        egl = v3(small[:, 172:204], 8)
        dtb = small[:, 204:208]
        alog = small[:, 208:212]
        ssn = small[:, 212:244]
        rn = small[:, 244:276]
        lbt = small[:, 276:300]
        c1 = small[:, 300:304]
        c2 = small[:, 304:308]
        zsp = small[:, 308:324]
        esp = small[:, 324:340]
        spt = small[:, 340:356]
        oss = small[:, 356:372]
        ors = small[:, 372:388]
        lbs = small[:, 388:404]

        QF, KF, VF = (v3(reg(2048 * n, 2048), 4) for n in range(3))
        KT, VT = (v3(reg(2048 * n, 2048), 4) for n in (3, 4))
        AT0 = v3(reg(4096, 2048), 4)
        Y0 = v3(reg(10240, 4096), 4)
        craw = v3(reg(14336, 1024), 2)
        sqt = v3(reg(15360, 1024), 2)
        HQ, HB, HK = (v3(reg(14336 + 2048 * n, 2048), 4) for n in range(3))
        HI = v3(reg(20480, 2048), 4)
        zt = v3(reg(6144, 1024), 2)
        PA = [v3(reg(14336 + 1024 * n, 1024), 2) for n in range(8)] + \
             [v3(reg(10240 + 1024 * n, 1024), 2) for n in range(4)]
        LE = reg(0, 2048)
        LP = [reg(2048, 2048), reg(8192, 2048)]
        HAT = v3(reg(4096, 2048), 4)
        KDT = v3(reg(8192, 2048), 4)
        onsq = v3(reg(7168, 1024), 2)
        raw_vec = reg(21000, 128)
        wba_raw = v3(reg(21200, 64), 8)
        lv_raw = v3(reg(21500, len(LEVELS) * P), len(LEVELS))
        baT = ar[0:8, 20480:20992]
        Y1 = v3(reg(0, 8192), 4)
        RQ = reg(8192, 2048).rearrange("p (h c t) -> p h c t", h=2, c=2)
        RK = reg(10240, 2048).rearrange("p (h c t) -> p h c t", h=2, c=2)
        RV = reg(12288, 4096).rearrange("p (h j n) -> p h j n", h=2, j=4)
        RAT = v3(reg(16384, 2048), 4)
        cos_t = reg(18432, 512)
        sin_t = reg(18944, 512)
        DH = reg(19456, 512)
        rtmp = v3(reg(19968, 1024), 2)
        gt = v3(reg(20992, 1024), 2)
        rprod = S[:, :]
        rnw = Stmp[:, :]
        rjunk = vnew[:, :]

        def htok(n):
            return v3(reg({0: 10240, 1: 4096, 2: 0, 3: 4096, 4: 4096}[n], 2048), 2)

        def wb(n):
            return reg(12288 if n == 0 else 6144, 1024)

        hTf = v3(reg(0, 4096), 8)
        xg = v3(reg(7168, 2048), 2)
        ysb = v3(reg(9216, 2048), 2)
        sg = v3(reg(11264, 512), 2)
        aact = v3(reg(11776, 512), 2)
        YP = reg(12288, 8192).rearrange("p (b j d) -> p b j d", b=4, j=2)

        def squares(n):
            return reg(7168, DM)
        ovWg = v3(reg(16384, 4096), 8)
        ovWd = v3(reg(20480, 2048), 2)

        SEM = {}

        def s_(name):
            if name not in SEM:
                SEM[name] = sem(name)
            return SEM[name]

        raw_loaded = [sem(f"raw_loaded{n}") for n in range(NRAW_MOE + NRAW_ONCE)]
        hi_done, lo_pool, lo_dve = sem("hi_done"), sem("lo_pool"), sem("lo_dve")
        piece_used, dense_ready = sem("piece_used"), sem("dense_ready")
        dense_read = {"act": sem("dense_read_act"), "dve": sem("dense_read_dve")}
        tile_ready = sem("tile_ready")
        tile_read = {"act": sem("tile_read_act"), "dve": sem("tile_read_dve")}

        def raw_at(i):
            n = RAW_SLOTS[i]
            if n < NRAW:
                return raw[:, n, :, :]
            return v3(reg(16384 + 1024 * (n - NRAW) if n < NRAW_MOE else 1024 * (n - NRAW_MOE), 1024), 2)

        def in_turn(n, it):
            return n + 12 * (it if isinstance(it, int) else 2)

        def raw_loaded_at(n, it):
            if isinstance(it, int):
                return 16 * raw_load(in_turn(n, it))
            return it * 16 + 16 * (raw_load(in_turn(n, it)) - 2)

        def piece_src(i):
            for l in range(2):
                if MOE_PIECE[l] <= i < MOE_PIECE[l] + 6 * NE:
                    q = i - MOE_PIECE[l]
                    if q < 4:
                        return gate_up_src(l, 0, q)
                    if q >= 6 * NE - 2:
                        return down_src(l, NE - 1, q - (6 * NE - 2))
                    return moe_src(l, 0, *divmod(q - 4, 6))
            db = i // 4 if i < MOE_PIECE[0] else (i - 6 * NE) // 4
            kp = (i - first_piece(db)) % 4
            kind, which, c = BLOCKS[db]
            if kind.endswith("in"):
                w = a["even_w_in"][0] if kind == "even_in" else a["odd_w_in"][0]
                return w.rearrange("(p k) c -> p k c", k=KD)[:, 2 * kp:2 * kp + 2, c:c + 512]
            w = a["even_w_out"][0] if kind == "even_out" else a["odd_w_out"][0][DM * which:DM * which + DM]
            return w.rearrange("(k p) c -> p k c", p=P)[:, 2 * kp:2 * kp + 2, c:c + 512]

        def gate_up_src(l, e, j):
            w = a["moe_w_gate_up"][l].rearrange("e (p k) c -> p e k c", k=KD)
            return w[:, bass.ds(e, 1), 2 * j:2 * j + 2, :].squeeze(1) if not isinstance(e, int) else w[:, e, 2 * j:2 * j + 2, :]

        def down_src(l, e, hf):
            w = a["moe_w_down"][l].rearrange("e (k p) c -> p e k c", p=P)
            c = 512 * hf
            return w[:, bass.ds(e, 1), :, c:c + 512].squeeze(1) if not isinstance(e, int) else w[:, e, :, c:c + 512]

        def moe_src(l, e, par, q):
            return gate_up_src(l, e + (par + 1), q) if q < 4 else down_src(l, e + par, q - 4)

        def wait_lo(eng, i):
            eng.wait_ge(lo_dve if lo_by_dve(i) else lo_pool, lo_count(i))

        def wait_used(eng, i):
            db = i // 4 if i < MOE_PIECE[0] else (i - 6 * NE) // 4
            kp = i - first_piece(db)
            assert 0 <= kp < 4
            if kp == 3:
                eng.wait_ge(dense_ready, 4 * db + 4)
            else:
                eng.wait_ge(piece_used, 3 * db + kp + 1)

        def wait_spl_free(eng, i):
            j = i - NSPL
            for l, m in enumerate(MOE_PIECE):
                if m <= j < m + 6 * NE:
                    eng.wait_ge(s_("moe_used"), 6 * NE * l + j - m + 1)
                    return
            if j >= 0:
                wait_used(eng, j)

        def tile(name):
            return ps[:, 4 + SIDE_AT[name] % 4, :]

        def tile_is_ready(eng, name):
            eng.wait_ge(tile_ready, SIDE_AT[name] + 1)

        def tile_is_read(eng, name):
            eng.wait_ge(tile_read[SIDE[SIDE_AT[name]][1]], SIDE_READ[name])

        def hT_hi_count(name):
            made = [n for n, _ in SIDE if n[0] == "yT" or (n[0] == "hT" and n[1] in (0, 2))]
            return made.index(name) + 1

        class Line:

            def __init__(self, eng, who):
                self.eng, self.who = eng, who
                self.own = s_(f"{who}_line")
                self.n = {}
                self.reads = 0

            def __call__(self, ins, on=None):
                sm = on if on is not None else self.own
                ins.then_inc(sm, 1)
                self.n[sm.name] = self.n.get(sm.name, 0) + 1
                self.eng.wait_ge(sm, self.n[sm.name])

            def read(self, ins, name):
                assert SIDE[SIDE_AT[name]][1] == self.who, name
                assert SIDE_READ[name] == self.reads + 1, (name, SIDE_READ[name], self.reads)
                self.reads += 1
                self(ins, tile_read[self.who])

        def bc_h(ap, n=P):
            return ap.unsqueeze(2).broadcast_to([ap.shape[0], 4, n])

        def bc_m(ap, n=4):
            return ap.unsqueeze(1).broadcast_to([ap.shape[0], n, ap.shape[1]])

        def cols(T, w=P):
            return slice(T * w, T * w + w)

        def mm3(dst, lh, ll, rh, rl, first, last):
            nc.tensor.matmul(dst, lh, rh, start=first, stop=False)
            nc.tensor.matmul(dst, lh, rl, start=False, stop=False)
            return nc.tensor.matmul(dst, ll, rh, start=False, stop=last)

        NORM_W = [a["norm_mix_w"][0], a["norm_ffn_w"][0], a["norm_mix_w"][1], a["norm_ffn_w"][1], a["final_norm_w"]]
        def x_ready(n, T):
            if n == 0:
                return s_(f"x_loaded{T}"), 16
            if n in (1, 3):
                return dense_read["dve"], evac_count({1: 9, 3: 25}[n], T)
            return s_(f"moe_added{n // 2 - 1}"), T + 1


        RO = 12288
        Lst = reg(RO, 128)
        ones = reg(RO + 128, 128)
        lg = v3(reg(RO + 256, 80), 4)
        g0 = reg(RO + 356, 4)
        r_a = v3(reg(RO + 384, 16), 4)
        r_b = v3(reg(RO + 400, 16), 4)
        gm = v3(reg(RO + 416, 16), 4)
        r_c = reg(RO + 432, 64).rearrange("p (T g e) -> p T g e", T=4, g=4)
        fs = v3(reg(RO + 496, 16), 4)
        m1 = v3(reg(RO + 512, 16), 4)
        m2 = v3(reg(RO + 528, 16), 4)
        mx = reg(RO + 544, 4)
        mx2 = reg(RO + 548, 4)
        gp = reg(RO + 552, 4)
        ed = reg(RO + 556, 4)
        oh = [v3(reg(RO + 560 + 64 * n, 64), 4) for n in range(2)]
        anyh = v3(reg(RO + 3344, 64), 4)
        any80 = reg(RO + 3344, 80)
        ahead = v3(reg(RO + 3424, 64), 4)
        ahead80 = reg(RO + 3424, 80)
        slotv = v3(reg(RO + 752, 64), 4)
        tmp64 = v3(reg(RO + 816, 64), 4)
        ncnt = reg(RO + 880, 16)
        ovc = reg(RO + 896, 16)
        ovi = reg(RO + 912, 16)
        ovt = reg(RO + 928, 16)
        slotf = reg(RO + 944, 8)
        slots_u = reg(RO + 952, 8).bitcast(U32)
        tokv = reg(RO + 960, 8)
        first4 = reg(RO + 968, 4)
        hotB = v3(reg(RO + 1440, 1024), 8)
        hotA = v3(reg(RO + 2464, 8 * SLOT_TILES), 8)
        iotas = reg(RO + 2656, 24 + SLOT_TILES + P)
        iota8, offs16 = iotas[:, 0:8], iotas[:, 8:24]
        iotaA, iotaB = iotas[:, 24:24 + SLOT_TILES], iotas[:, 24 + SLOT_TILES:24 + SLOT_TILES + P]
        lgT = ar[0:20, RO + 2832:RO + 2832 + SEQ]
        slotA = reg(RO + 3520, 8)
        slotB = reg(RO + 3528, 8)
        sA_i, sB_i = reg(RO + 3536, 8).bitcast(U32), reg(RO + 3544, 8).bitcast(U32)
        lgb = ar[0:20, RO + 3552:RO + 3553]
        eidf = reg(RO + 996, 8)
        cmp7 = reg(RO + 1004, 112)
        rw = v3(reg(RO + 1120, 160), 8)
        w12 = small[:, 404:412]
        onesrow = reg(RO + 1408, 16)
        zero16 = reg(RO + 1424, 16)

        def overflow_flag(eng, l):
            eng.wait_ge(s_("slots_known"), l + 1)
            return eng.value_load(eid[0:1, 7:8], min_val=0, max_val=7)

        def overflow_sp(sp, l):
            n = overflow_flag(sp, l)
            with sp.If(n > 0):
                with sp.Fori(0, 7) as j:
                    sp.wait_ge(s_(f"ov_stored{l}"), j + 1)
                    settle(sp)
                    e = sp.value_load(eid[0:1, bass.ds(j, 1)], min_val=0, max_val=NE - 1)
                    wg = a["moe_w_gate_up"][l].rearrange("e (p k) c -> p e (k c)", k=KD)[:, bass.ds(e, 1), :].squeeze(1)
                    wd = a["moe_w_down"][l].rearrange("e (k p) c -> p e k c", p=P)[:, bass.ds(e, 1), :, :].squeeze(1)
                    sp.dma_start(ovWg.rearrange("p k c -> p (k c)"), wg).then_inc(s_(f"ov_w{l}"), 16)
                    sp.dma_start(ovWd, wd).then_inc(s_(f"ov_w{l}"), 16)

        def settle(eng):
            eng.wait_ge(hi_done, 1)

        gate_cell = sb("gate_cell", [P, 1])
        block = ctx.enter_context(nc.Block())

        @block.sync
        def _(sp):
            def load_x(T):
                sp.dma_start(X[:, T, :], a["x"][0].rearrange("(T p) d -> T p d", p=P)[T]).then_inc(s_(f"x_loaded{T}"), 16)

            load_x(0)
            sp.dma_start(ident[:, :], a["c_ident"]).then_inc(s_("ident_loaded"), 16)
            sp.dma_start(wb(0), NORM_W[0].rearrange("(a n) -> a n", a=1).broadcast_to([P, DM])).then_inc(s_("wb0_loaded"), 16)
            for T in range(1, NT):
                load_x(T)
            small_ones = [(U[:, :], a["c_U"]), (m16[:, :], a["c_m16"]), (moff[:, :], a["c_moff"]),
                  (lv_raw, a["c_lv"]), (resetm[:, :], a["c_reset"]),
                  (raw_vec[0:48, :], a["gdn_conv_w"][0].rearrange("j (g p) -> (j g) p", p=P)),
                  (raw_vec[48:60, :], a["hgrn_lb_logits"].rearrange("r (h p) -> (r h) p", p=P)),
                  (dtb, a["gdn_dt_bias"].broadcast_to([P, 4])), (alog, a["gdn_a_log"].broadcast_to([P, 4])),
                  (gnw[:, :], a["gdn_norm_w"].broadcast_to([P, P])), (hnw[:, :], a["hgrn_norm_w"].broadcast_to([P, P])),
                  (wba_raw, a["even_w_in"][0].rearrange("(p k) c -> p k c", k=KD)[:, :, 2048:2056])]
            for dst, src in small_ones:
                sp.dma_start(dst, src).then_inc(s_("consts_loaded"), 16)
            sp.wait_ge(s_("consts_loaded"), 16 * 12)

            def load(i):
                before = raw_before(i)
                if before is not None:
                    wait_lo(sp, before)
                for l, m in enumerate(MOE_PIECE):
                    if i == m + NRAW:
                        sp.wait_ge(dense_ready, 4 * (MOE_AT[l] - 1))
                    if i == m + NRAW_MOE:
                        sp.wait_ge(s_("r_logits"), l + 1)
                        for q in range(2):
                            sp.wait_ge(s_(f"h_stored{q}"), 32 * (l + 1))
                sp.dma_start(raw_at(i), piece_src(i)).then_inc(raw_loaded[RAW_SLOTS[i]], 16)

            def moe_loads(l):
                m = MOE_PIECE[l]
                for i in range(m, m + 28):
                    load(i)
                with sp.Fori(2, NE // 2 - 1) as it:
                    for j in range(12):
                        n = m + 4 + j
                        sp.wait_ge(lo_dve, it * 12 + (lo_count(n) - 12))
                        sp.dma_start(raw_at(in_turn(n, it)), moe_src(l, it * 2, j // 6, j % 6))\
                            .then_inc(raw_loaded[RAW_SLOTS[in_turn(n, it)]], 16)
                for i in range(m + 88, m + 6 * NE):
                    load(i)

            for i in range(MOE_PIECE[0]):
                load(i)
            moe_loads(0)
            after = MOE_PIECE[0] + 6 * NE
            for i in range(after, after + 4):
                load(i)
            overflow_sp(sp, 0)
            sp.wait_ge(s_("yp_loaded3"), 16)
            for i in range(after + 4, MOE_PIECE[1]):
                load(i)
            moe_loads(1)
            for i in range(MOE_PIECE[1] + 6 * NE, NPIECE):
                load(i)
            overflow_sp(sp, 1)
            for T in range(NT):
                sp.wait_ge(s_("h_ready"), 4 * 4 + T + 1)
                sp.dma_start(out[0].rearrange("(T p) d -> T p d", p=P)[T], htok(4)[:, T % 2, :]).then_inc(s_(f"out_stored{T % 2}"), 16)
            sp.wait_ge(s_("out_stored0"), 32)
            sp.wait_ge(s_("out_stored1"), 32)

        @block.gpsimd
        def _(pool):
            L = Line(pool, "pool")

            def lo(i):
                if i >= NPIECE or lo_by_dve(i):
                    return
                pool.wait_ge(hi_done, i + 1)
                wait_spl_free(pool, i)
                pool.tensor_tensor(wl[:, i % NSPL, :, :], raw_at(i), wh[:, i % NSPL, :, :].bitcast(F32),
                                   ALU.subtract).then_inc(lo_pool, 1)

            def first_lo(n):
                if n == 0:
                    for i in range(3):
                        lo(i)

            def rsqrt(dst, src, n, ready, count, on):
                pool.wait_ge(ready, count)
                pool.tensor_tensor(dst, src, mhalf[:, 0:n], ALU.pow).then_inc(on, 1)

            def carry():
                pool.tensor_tensor(gate_cell[:, :], mhalf[:, 0:1], mhalf[:, 0:1], ALU.add)

            def moe(l):
                m = MOE_PIECE[l]
                last_row = pool.to_reg(SEQ - 1)
                last_pair_row = pool.to_reg(2 * SEQ - 1)
                pool.wait_ge(s_("rows_known"), l + 1)
                for q in range(2):
                    pool.wait_ge(s_(f"h_stored{q}"), 32 * (l + 1))
                pool.wait_ge(s_("xg_cleared"), l + 1)

                def gather(col, par):
                    L(pool.tensor_copy(cur[:, par:par + 1], idx[:, 0, col].bitcast(U32)))
                    pool.indirect_dma_start(out=xg[:, par, :], out_offset=None, in_=hs_dram[l],
                                            in_offset=bass.IndirectOffsetOnAxis(ap=cur[:, par:par + 1], axis=0),
                                            bounds_check=last_row, oob_is_err=False).then_inc(s_(f"xg_loaded{par}"), 16)

                gather(slice(0, 1), 0)
                gather(slice(1, 2), 1)
                G = s_("pool_moe")

                def gather_ahead(it, par):
                    pool.wait_ge(s_("xT_ready"), it * 4 + (32 * l + 2 * par + 2))
                    col = it * 2 + (2 + par)
                    col = slice(col, col + 1) if isinstance(col, int) else bass.ds(col, 1)
                    pool.tensor_copy(cur[:, par:par + 1], idx[:, 0, col].bitcast(U32)).then_inc(G, 1)

                def gather_now(it, par):
                    pool.indirect_dma_start(out=xg[:, par, :], out_offset=None, in_=hs_dram[l],
                                            in_offset=bass.IndirectOffsetOnAxis(ap=cur[:, par:par + 1], axis=0),
                                            bounds_check=last_row, oob_is_err=False).then_inc(s_(f"xg_loaded{par}"), 16)

                def scatter(it, par, g):
                    col = it * 2 + par
                    col = slice(col, col + 1) if isinstance(col, int) else bass.ds(col, 1)
                    pool.tensor_copy(cur[:, 2 + par:3 + par], idx[:, 1, col].bitcast(U32)).then_inc(G, 1)
                    pool.wait_ge(G, g)
                    pool.wait_ge(s_("y_read"), it * 4 + (32 * l + 2 * par + 4))
                    carry()
                    pool.indirect_dma_start(out=y2_dram[l], out_offset=bass.IndirectOffsetOnAxis(ap=cur[:, 2 + par:3 + par], axis=0),
                                            in_=ysb[:, par, :], in_offset=None,
                                            bounds_check=last_pair_row, oob_is_err=False).then_inc(s_(f"y_stored{par}"), 16)

                def free_last(it, par):
                    pool.wait_ge(s_(f"y_stored{1 - par}"), it * 16 + (128 * l + 16 * par))
                    pool.nop().then_inc(s_("ysb_free"), 1)

                for par in range(2):
                    gather_ahead(0, par)
                    pool.wait_ge(G, 32 * l + par + 1)
                    gather_now(0, par)
                def two_experts(it):
                    for par in range(2):
                        gather_ahead(it + 1, par)
                        pool.wait_ge(G, it * 4 + (32 * l + 2 * par + 3))
                        carry()
                        gather_now(it, par)
                        scatter(it, par, it * 4 + (32 * l + 2 * par + 4))
                        if par == 1 or not isinstance(it, int):
                            free_last(it, par)

                two_experts(0)
                with pool.Fori(1, NE // 2 - 1) as it:
                    two_experts(it)
                for par in range(2):
                    scatter(NE // 2 - 1, par, 32 * l + 31 + par)
                    free_last(NE // 2 - 1, par)
                for i in range(2):
                    lo(m + 6 * NE + i)
                free_last(NE // 2, 0)
                for q in range(2):
                    pool.wait_ge(s_(f"xg_loaded{q}"), 144 * (l + 1))
                pool.nop().then_inc(s_(f"ov_stored{l}"), 1)
                n = overflow_flag(pool, l)
                with pool.If(n > 0):
                    with pool.Fori(0, 7) as j:
                        pool.tensor_copy(cur[:, 0:1], idx[:, 0, bass.ds(j + NE, 1)].bitcast(U32)).then_inc(s_(f"ov_cur{l}"), 1)
                        pool.wait_ge(s_(f"ov_cur{l}"), j * 2 + 1)
                        pool.wait_ge(s_(f"ov_stored{l}"), j + 1)
                        carry()
                        pool.indirect_dma_start(out=xg[:, 0, :], out_offset=None, in_=hs_dram[l],
                                                in_offset=bass.IndirectOffsetOnAxis(ap=cur[:, 0:1], axis=0),
                                                bounds_check=last_row, oob_is_err=False).then_inc(s_(f"ov_x{l}"), 16)
                        pool.tensor_copy(cur[:, 2:3], idx[:, 1, bass.ds(j + NE, 1)].bitcast(U32)).then_inc(s_(f"ov_cur{l}"), 1)
                        pool.wait_ge(s_(f"ov_cur{l}"), j * 2 + 2)
                        pool.wait_ge(s_(f"ov_y{l}"), j * 2 + 2)
                        carry()
                        pool.indirect_dma_start(out=y2_dram[l], out_offset=bass.IndirectOffsetOnAxis(ap=cur[:, 2:3], axis=0),
                                                in_=ysb[:, 0, :], in_offset=None,
                                                bounds_check=last_pair_row, oob_is_err=False).then_inc(s_(f"ov_ydma{l}"), 16)
                        pool.wait_ge(s_(f"ov_ydma{l}"), j * 16 + 16)
                        pool.nop().then_inc(s_(f"ov_stored{l}"), 1)
                pool.nop().then_inc(s_("y_all_stored"), 1)
                for i in range(2, 4):
                    lo(m + 6 * NE + i)

            pool.memset(mhalf, -0.5).then_inc(L.own, 1)
            L.n[L.own.name] = 1
            pool.wait_ge(L.own, 1)
            for _ in range(2):
                pool.nop().then_inc(s_("ysb_free"), 1)
            for step in SCHEDULE:
                if step[0] == "piece":
                    lo(first_piece(step[1]) + step[2] + 3)
                elif step[0] == "rows":
                    for i in ahead_of_rows(step[1], step[2]):
                        lo(i)
                elif step[0] == "norm":
                    for T in range(NT):
                        pool.wait_ge(s_("norm_ss"), 4 * step[1] + T + 1)
                        L(pool.tensor_scalar(ms[:, T:T + 1], ss[:, T:T + 1], EPS, None, ALU.add))
                        pool.tensor_tensor(rs[:, T:T + 1], ms[:, T:T + 1], mhalf[:, 0:1], ALU.pow).then_inc(s_("norm_r"), 1)
                    first_lo(step[1])
                elif step[0] == "tok" and step[1] != "v":
                    n = 4 * (step[1] == "k") + step[2]
                    c = slice(4 * n, 4 * n + 4)
                    pool.wait_ge(s_("sq_reduced"), n + 1)
                    L(pool.tensor_scalar(ssn[:, c], ssn[:, c], EPS, None, ALU.add))
                    pool.tensor_tensor(rn[:, c], ssn[:, c], mhalf[:, 0:4], ALU.pow).then_inc(s_("l2_r"), 1)
                elif step[0] == "l2":
                    pool.wait_ge(s_("l2_r"), 8)
                    for T in range(NT):
                        k = v3(KT[:, T, :], 4)
                        pool.tensor_tensor(k, k, bc_h(rn[:, 16 + 4 * T:20 + 4 * T]), ALU.mult).then_inc(s_("k_normed"), 1)
                elif step[0] == "onorm":
                    w, Ts = step[1:]
                    n = len(Ts)
                    rsqrt(ors[:, 4 * Ts[0]:4 * Ts[0] + 4 * n], oss[:, 4 * Ts[0]:4 * Ts[0] + 4 * n], 4 * n, s_("o_ms"),
                          onorm_count(w, Ts), s_("o_r"))
                elif step[0] == "evac" and BLOCKS[step[1]][1] and isinstance(BLOCKS[step[1]][1], tuple) and BLOCKS[step[1]][1][0] == "rg":
                    h = BLOCKS[step[1]][1][1]
                    rsqrt(ors[:, 0:4], oss[:, 0:4], 4, s_("ro_ms"), h + 1, s_("ro_r"))
                elif step[0] == "moe":
                    lo(MOE_PIECE[step[1]] + 3)
                    moe(step[1])

        @block.scalar
        def _(act):
            A = Line(act, "act")
            dense_reads = [0]

            def hi(i):
                if i >= NPIECE:
                    return
                act.wait_ge(raw_loaded[RAW_SLOTS[i]], 16 * raw_load(i))
                wait_spl_free(act, i)
                act.activation(wh[:, i % NSPL, :, :], raw_at(i), ACT.Copy).then_inc(hi_done, 1)

            def dense_tile(db, t):
                act.wait_ge(dense_ready, 4 * db + t + 1)
                return ps[:, t, :]

            def consts():
                act.wait_ge(s_("consts_loaded"), 16 * 12)
                A(act.activation(wba_h[:, :, :], wba_raw, ACT.Copy), s_("wba_hi"))
                act.wait_ge(s_("lb_args"), 1)
                A(act.activation(lbt[:, 0:12], lbt[:, 0:12], ACT.Exp), s_("lb_exp"))

            def norm(n):
                def square(T):
                    act.wait_ge(*x_ready(n, T))
                    A(act.activation(squares(n), X[:, T, :], ACT.Square, scale=DM ** -0.5, accum_out=ss[:, T:T + 1]), s_("norm_ss"))

                def transposed(T):
                    if n in (1, 3):
                        act.wait_ge(s_("h_ready"), 4 * n + T + 1)
                        act.dma_start(hs_dram[n // 2].rearrange("(T p) d -> T p d", p=P)[T], htok(n)[:, T % 2, :])\
                            .then_inc(s_(f"h_stored{T % 2}"), 16)
                    for g in range(2):
                        name = ("hT", n, T, g)
                        tile_is_ready(act, name)
                        src = v3(tile(name), 4)
                        if n in (1, 3):
                            A.read(act.activation(hTf[:, 4 * g:4 * g + 4, cols(T)], src, ACT.Copy), name)
                        else:
                            A(act.activation(HTH[:, 4 * g:4 * g + 4, cols(T)], src, ACT.Copy), s_("hT_hi_made"))

                for T in range(3):
                    square(T)
                if n == 2:
                    transposed(0)
                square(3)
                if n == 4:
                    return
                for T in range(int(n == 2), NT):
                    transposed(T)
                    if n == 0 and T == 2:
                        for i in range(3):
                            hi(i)

            def load_wb(n):
                act.dma_start(wb(n), NORM_W[n].rearrange("(a n) -> a n", a=1).broadcast_to([P, DM])).then_inc(s_("wb_loaded"), 16)

            def yT(l, kh, Ts):
                act.wait_ge(dense_ready, 4 * {(0, 0): 8, (1, 0): 22, (1, 1): 24}[l, kh])
                for T in Ts:
                    for g in range(2):
                        name = ("yT", l, kh, T, g)
                        tile_is_ready(act, name)
                        A(act.activation(HTH[:, 4 * g:4 * g + 4, cols(T)], v3(tile(name), 4), ACT.Copy), s_("hT_hi_made"))

            def gates_act():
                act.wait_ge(s_("z_ready"), 1)
                A(act.activation(esp, esp, ACT.Exp, scale=-1.0), s_("gate_exp"))
                A(act.activation(alog, alog, ACT.Exp), s_("gate_exp"))
                A(act.activation(beta, beta, ACT.Tanh, scale=0.5), s_("gate_exp"))
                act.wait_ge(s_("sp_ready"), 1)
                A(act.activation(spt, spt, ACT.Ln), s_("gate_exp"))
                tile_is_read(act, "gc")
                A(act.activation(egc, gc, ACT.Exp), s_("egc_ready"))

            def tok(nm, T):
                name = ("tok", nm, T)
                tile_is_ready(act, name)
                dst = {"q": Y0[:, T, 0:512], "k": KT[:, T, :], "v": VT[:, T, :]}[nm]
                if nm == "v":
                    A.read(act.activation(dst, tile(name), ACT.Copy), name)
                    return
                A(act.activation(dst, tile(name), ACT.Copy))
                n = (nm == "k") * 4 + T
                if n >= 2:
                    act.wait_ge(s_("sq_reduced"), n - 1)
                A.read(act.activation(sqt[:, n % 2, :], tile(name), ACT.Square), name)

            def l2():
                for T in range(NT):
                    tile_is_ready(act, ("qb", T))
                    A.read(act.activation(QF[:, :, cols(T)], v3(tile(("qb", T)), 4), ACT.Copy), ("qb", T))
                    tile_is_ready(act, ("kb", T))
                    A.read(act.activation(KF[:, :, cols(T)], v3(tile(("kb", T)), 4), ACT.Copy), ("kb", T))

            def gdn_decay(T):
                q = T % 2
                act.wait_ge(s_("g_args"), T + 1)
                A(act.activation(PA[0][:, q, :], PA[0][:, q, :], ACT.Exp, scale=-1.0), s_("decays"))
                A(act.activation(PA[1][:, q, :], PA[1][:, q, :], ACT.Exp))
                act.wait_ge(s_("kd_args"), T + 1)
                A.read(act.activation(PA[2][:, q, :], tile(("Gb", T)), ACT.Exp), ("Gb", T))
                A(act.activation(kde[:, 4 * T:4 * T + 4], kde[:, 4 * T:4 * T + 4], ACT.Exp), s_("more_decays"))

            def gdn_x1(T):
                tile_is_ready(act, ("DT", T))
                A.read(act.activation(PA[4][:, T % 2, :], tile(("DT", T)), ACT.Copy), ("DT", T))

            def gdn_inverse(pr):
                Ts = (2 * pr, 2 * pr + 1)

                def copy(name, dst, after=None):
                    tile_is_ready(act, name)
                    if after is not None:
                        tile_is_ready(act, after)
                    A.read(act.activation(dst, tile(name), ACT.Copy), name)

                for T in Ts:
                    copy(("P2", T), PA[5][:, T % 2, :])
                    copy(("P2T", T), PA[6][:, T % 2, :])
                for r in (1, 2):
                    for T in Ts:
                        last = ("P", r, T) if r == 1 else ("PT", r, T)
                        copy(("PT", r, T), PA[6][:, T % 2, :], last)
                        if r == 1:
                            copy(("P", r, T), PA[5][:, T % 2, :])
                for T in Ts:
                    copy(("B", T), PA[5][:, T % 2, :])
                    copy(("BT", T), PA[6][:, T % 2, :])
                for T in Ts:
                    copy(("B2", T), PA[4][:, T % 2, :])
                for T in Ts:
                    copy(("IT", T), PA[8][:, T % 2, :])
                for T in Ts:
                    copy(("u", T), VT[:, T, :])
                    tile_is_ready(act, ("wT", T))
                    A.read(act.activation(KF[:, :, cols(T)], v3(tile(("wT", T)), 4), ACT.Copy), ("wT", T))

            def scan_out(nm, c, c0):
                T, r = c // 2, slice(64 * (c % 2), 64 * (c % 2) + 64)
                tile_is_ready(act, (nm, c))
                A.read(act.activation(Y0[r, T, c0:c0 + 512], tile((nm, c))[r, :], ACT.Copy, scale=DK ** -0.5), (nm, c))

            def onorm(w, Ts):
                act.wait_ge(s_("scan_done"), 1)
                for T in Ts:
                    n = 8 + 4 * w + T
                    act.wait_ge(s_("sq_reduced"), n - 1)
                    A(act.activation(onsq[:, T % 2, :], Y0[:, T, 512 * w:512 * w + 512], ACT.Square), s_("o_sq"))

            def hgrn(step):
                n = {"hdiag": 0, "hlevel": step[1] + 1 if len(step) > 1 else 0}.get(step[0])
                if n is not None:
                    act.wait_ge(s_("lv_args"), n + 1)
                    A(act.activation(LE, LE, ACT.Exp), s_("lv_exp"))
                else:
                    act.wait_ge(s_("hk_decayed"), 1)
                    A(act.activation(LE, HB.rearrange("p h t -> p (h t)"), ACT.Exp), s_("lv_exp"))
                    for T in range(NT):
                        tile_is_ready(act, ("kd", T))
                        A.read(act.activation(KDT[:, T, :], tile(("kd", T)), ACT.Copy), ("kd", T))

            def fcum(t):
                act.wait_ge(s_("f_ready"), t + 1)
                A(act.activation(HQ[:, t, :], HB[:, t, :], ACT.Ln), s_("lf_ready"))

            def evac(db, ts_=tuple(range(4))):
                kind, which, _c = BLOCKS[db]
                rd = dense_read["act"]
                if which in ("q", "k", "v"):
                    dst = {"q": QF, "k": KF, "v": VF}[which]
                    for t in range(5):
                        if t < 4:
                            n = 4 * db + t
                            src = dense_tile(db, t)
                            if n >= 2:
                                act.wait_ge(s_("conv_done"), n - 1)
                            w3 = vec[:, 36 + n:37 + n]
                            A(act.activation(dst[:, t, :], src, ACT.Copy, scale=w3))
                            A(act.activation(craw[:, t % 2, :], src, ACT.Copy), rd)
                        if t > 0:
                            act.wait_ge(s_("conv_done"), 4 * db + t)
                            A(act.activation(dst[:, t - 1, :], dst[:, t - 1, :], ACT.Silu), s_("conv_silu"))
                elif which == "hf":
                    for t in range(4):
                        src = dense_tile(db, t)
                        A(act.activation(HK[:, t, :], src, ACT.Tanh, scale=0.5), rd)
                elif which == "hq":
                    for t in range(4):
                        src = dense_tile(db, t)
                        act.wait_ge(s_("b_ready"), 4)
                        A(act.activation(HQ[:, t, :], src, ACT.Silu), rd)
                elif which == "hi":
                    for t in range(4):
                        src = dense_tile(db, t)
                        A(act.activation(HI[:, t, :], src, ACT.Copy), rd)
                elif which in ("z", "hg"):
                    for t in ts_:
                        src = dense_tile(db, t)
                        n = 4 * (which == "hg") + t
                        if n == 0:
                            act.wait_ge(s_("scan_done"), 1)
                        if n >= 2:
                            act.wait_ge(s_("z_used"), n - 1)
                        A(act.activation(zt[:, t % 2, :], src, ACT.Silu), rd)
                elif kind == "odd_in":
                    nm, h = which
                    if nm in ("rq", "rk"):
                        for t in range(4):
                            src = dense_tile(db, t)
                            n = rot_index(db) * 2 + t // 2
                            if n >= 1 and t % 2 == 0:
                                act.wait_ge(s_("rot_done"), n)
                            A(act.activation(rtmp[:, t % 2, :], src, ACT.Copy), rd)
                    elif nm == "rv":
                        for t in range(4):
                            src = dense_tile(db, t)
                            A(act.activation(RV[:, h % 2, t, :], src, ACT.Copy), rd)
                    else:
                        for t in range(4):
                            src = dense_tile(db, t)
                            n = 4 * h + t
                            if n >= 2:
                                act.wait_ge(s_("g_used"), n - 1)
                            A(act.activation(gt[:, t % 2, :], src, ACT.Silu), rd)

            def ro(h):
                for T in range(NT):
                    name = ("ro", h, T)
                    tile_is_ready(act, name)
                    A(act.activation(Y1[:, T, h * RDV:(h + 1) * RDV], tile(name), ACT.Copy))
                    if T == 0 and h > 0:
                        act.wait_ge(s_("ro_r"), h)
                    A.read(act.activation(rjunk, tile(name), ACT.Square, accum_out=oss[:, T:T + 1]), name)

            def moe(l):
                m = MOE_PIECE[l]
                act.wait_ge(s_("r_cexp"), l + 1)
                A(act.activation(r_a, r_a, ACT.Exp), s_("r_exp"))
                act.wait_ge(s_("r_eexp"), l + 1)
                A(act.activation(ed, ed, ACT.Exp), s_("r_exp"))
                used = s_("moe_used")

                def silu(E, par, count):
                    act.wait_ge(used, count)
                    act.activation(sg[:, par, :], ps[:, par, 0:FE], ACT.Silu).then_inc(s_("silu_done"), 1)

                load_wb(2 * l + 2)
                xT_hi(l, 0, 0)
                hi(m + 4)
                hi(m + 5)
                xT_hi(l, 1, 1)
                hi(m + 6)
                silu(16 * l, 0, 6 * NE * l + 4)

                def expert(it, par):
                    E = it * 2 + (16 * l + par)
                    b = m + 4 + 6 * par
                    last = isinstance(it, int) and it == NE // 2 - 1

                    def hi_in(j):
                        n = b + j
                        act.wait_ge(raw_loaded[RAW_SLOTS[in_turn(n, it)]], raw_loaded_at(n, it))
                        act.wait_ge(used, it * 12 + (6 * NE * l + n - m - NSPL + 1))
                        act.activation(wh[:, n % NSPL, :, :], raw_at(in_turn(n, it)), ACT.Copy).then_inc(hi_done, 1)

                    act.wait_ge(s_("aT_ready"), E + 1)
                    act.activation(HTH[:, 4 + par, 0:256], ps[:, 6, 0:256], ACT.Copy).then_inc(s_("aT_hi"), 1)
                    n0 = 0
                    if not last or par == 0:
                        n0 = 4
                        for j in (3, 4, 5, 6):
                            hi_in(j)
                        silu(E + 1, 1 - par, it * 12 + (6 * NE * l + 6 * par + 8))
                        hi_in(7)
                        if not last:
                            xT_hi(l, it * 2 + (par + 2), par)
                    act.wait_ge(s_("ysb_free"), E + 1)
                    for hf in range(2):
                        act.wait_ge(used, it * 12 + (6 * NE * l + 6 * par + 4 + n0 + hf + 1))
                        act.activation(ysb[:, par, 512 * hf:512 * hf + 512], ps[:, 2 + hf, :], ACT.Copy).then_inc(s_("y_read"), 1)
                        if hf == 0 and not last:
                            hi_in(8)

                for n in range(4):
                    expert(*divmod(n, 2))
                with act.Fori(2, NE // 2 - 1) as it:
                    for par in range(2):
                        expert(it, par)
                for par in range(2):
                    expert(NE // 2 - 1, par)
                for i in range(4):
                    hi(m + 6 * NE + i)
                n = overflow_flag(act, l)
                with act.If(n > 0):
                    with act.Fori(0, 7) as j:
                        for g in range(2):
                            act.wait_ge(s_(f"ov_xT{l}"), j * 2 + (g + 1))
                            act.activation(hTf[:, 4 * g:4 * g + 4, 0:P], v3(ps[:, 4 + g, :], 4), ACT.Copy).then_inc(s_(f"ov_xTr{l}"), 1)
                        act.wait_ge(s_(f"ov_gu{l}"), j + 1)
                        act.activation(sg[:, 0, :], ps[:, 0, 0:FE], ACT.Silu).then_inc(s_(f"ov_silu{l}"), 1)
                        act.wait_ge(s_(f"ov_aT{l}"), j + 1)
                        act.activation(hTf[:, 0:2, P:2 * P], ps[:, 6, 0:256].rearrange("p (k n) -> p k n", k=2), ACT.Copy).then_inc(s_(f"ov_aTr{l}"), 1)
                        for hf in range(2):
                            act.wait_ge(s_(f"ov_yp{l}"), j * 2 + (hf + 1))
                            act.activation(ysb[:, 0, 512 * hf:512 * hf + 512], ps[:, 2 + hf, :], ACT.Copy).then_inc(s_(f"ov_y{l}"), 1)
                act.wait_ge(s_("y_all_stored"), l + 1)
                src = y2_dram[l].rearrange("(T p j) d -> T p j d", p=P, j=2)
                for T in range(NT):
                    act.dma_start(YP[:, T, :, :], src[T]).then_inc(s_(f"yp_loaded{T}"), 16)

            def xT_hi(l, e, par):
                for g in range(2):
                    act.wait_ge(s_("xT_ready"), e * 2 + (32 * l + g + 1))
                    act.activation(HTH[:, 2 * par + g, :], ps[:, 4 + g, :], ACT.Copy).then_inc(s_("xT_hi"), 1)

            for _ in range(2):
                act.nop().then_inc(s_("y_read"), 1)
            for step in SCHEDULE:
                k = step[0]
                if k == "consts":
                    consts()
                elif k == "norm":
                    norm(step[1])
                    if step[1] == 2:
                        for n, (dst, src) in enumerate(((cos_t, a["c_cos"]), (sin_t, a["c_sin"]), (rnw, a["ret_norm_w"].broadcast_to([P, RDV])))):
                            act.dma_start(dst, src).then_inc(s_("ret_consts"), 16)
                elif k == "rows":
                    for i in ahead_of_rows(step[1], step[2]):
                        hi(i)
                elif k == "piece":
                    hi(first_piece(step[1]) + step[2] + 3)
                elif k == "ba":
                    pass
                elif k == "gates":
                    gates_act()
                elif k == "tok":
                    tok(step[1], step[2])
                elif k == "l2":
                    l2()
                elif k == "gdn_decay":
                    gdn_decay(step[1])
                elif k == "gdn_x1":
                    gdn_x1(step[1])
                elif k == "gdn_inverse":
                    gdn_inverse(step[1])
                elif k == "fcum":
                    fcum(step[1])
                elif k == "evac_gate":
                    evac(step[1], (step[2],))
                elif k == "scan":
                    scan_out("so", step[1], 0)
                elif k == "hscan":
                    scan_out("ho", step[1], 512)
                elif k == "onorm":
                    onorm(*step[1:])
                elif k in ("hdiag", "hlevel", "hstate"):
                    hgrn(step)
                elif k == "evac":
                    if step[1] in (8, 24):
                        l = int(step[1] == 24)
                        load_wb(2 * l + 1)
                        for dst, src in ((Lst, a["c_Lst"]), (iotas, a["c_iota"]),
                                         (lgb[0:4, :], a["router_c_b"][l].rearrange("(a n) -> a n", n=1)),
                                         (lgb[4:20, :], a["router_f_b"][l].rearrange("(a n) -> a n", n=1)),
                                         (rw[:, :, 0:4], a["router_c_w"][l].rearrange("(p k) c -> p k c", k=KD)),
                                         (rw[:, :, 4:20], a["router_f_w"][l].rearrange("(p k) c -> p k c", k=KD)),
                                         (tokv, a["c_tok"]), (first4, a["c_first"])):
                            act.dma_start(dst, src).then_inc(s_("router_loaded"), 16)
                    if evac_engine(step[1]) == "act":
                        evac(step[1])
                elif k == "yT":
                    yT(*step[1:])
                elif k == "score":
                    h = step[1]
                    if h > 0:
                        act.wait_ge(tile_read["dve"], SIDE_READ[("sc", h - 1, NT - 1)])
                    act.dma_start(DH, a["c_decay"][h]).then_inc(s_("dh_loaded"), 16)
                elif k == "ro":
                    ro(step[1])
                elif k == "moe":
                    hi(MOE_PIECE[step[1]] + 3)
                    moe(step[1])

        @block.vector
        def _(dve):
            D = Line(dve, "dve")
            tt, ts, stt = dve.tensor_tensor, dve.tensor_scalar, dve.scalar_tensor_tensor

            def consts():
                D(dve.memset(S[:, :], 0.0))
                tile_is_ready(dve, "vec")
                D.read(dve.tensor_copy(vec[:, :], tile("vec")[:, 0:60]), "vec")
                D(dve.tensor_copy(lvmask[:, :, :], lv_raw))
                lb3 = vec[:, 48:60]
                D(tt(lbs[:, 0:4], lb3[:, 0:4], lb3[:, 4:8], ALU.max))
                D(tt(lbs[:, 0:4], lbs[:, 0:4], lb3[:, 8:12], ALU.max))
                D(tt(v3(lbt[:, 0:12], 3), v3(lb3, 3), bc_m(lbs[:, 0:4], 3), ALU.subtract), s_("lb_args"))
                dve.wait_ge(s_("lb_exp"), 1)
                D(tt(lbs[:, 4:8], lbt[:, 0:4], lbt[:, 4:8], ALU.add))
                D(tt(lbs[:, 4:8], lbs[:, 4:8], lbt[:, 8:12], ALU.add))
                D(dve.reciprocal(lbs[:, 4:8], lbs[:, 4:8]))
                D(tt(lbs[:, 8:12], lbt[:, 0:4], lbs[:, 4:8], ALU.mult))
                D(ts(c1, lbs[:, 8:12], -0.5, 0.5, ALU.mult, ALU.add))
                D(tt(c2, lbs[:, 8:12], c1, ALU.add))
                dve.wait_ge(s_("wba_hi"), 1)
                D(tt(wba_l[:, :, :], wba_raw, wba_h[:, :, :].bitcast(F32), ALU.subtract), s_("wba_lo"))

            def combine(l, T):
                dve.wait_ge(s_(f"yp_loaded{T}"), 16 * (l + 1))
                D(stt(X[:, T, :], YP[:, T, 0, :], w12[:, 2 * T:2 * T + 1], X[:, T, :], ALU.mult, ALU.add))
                D(stt(X[:, T, :], YP[:, T, 1, :], w12[:, 2 * T + 1:2 * T + 2], X[:, T, :], ALU.mult, ALU.add), s_(f"moe_added{l}"))

            def norm(n):
                moe_l = n // 2 - 1 if n in (2, 4) else None
                if moe_l is not None:
                    combine(moe_l, 0)
                    combine(moe_l, 1)
                if n == 0:
                    dve.wait_ge(s_("wb0_loaded"), 16)
                else:
                    dve.wait_ge(s_("wb_loaded"), 16 * n)
                for T in range(NT):
                    if T >= 2:
                        if n < 4:
                            tile_is_ready(dve, ("hT", n, T - 2, 1))
                        if n in (1, 3):
                            dve.wait_ge(s_(f"h_stored{T % 2}"), 32 * (n // 2) + 16)
                        if n == 4:
                            dve.wait_ge(s_(f"out_stored{T % 2}"), 16)
                    dve.wait_ge(s_("norm_r"), 4 * n + T + 1)
                    D(stt(htok(n)[:, T % 2, :], X[:, T, :], rs[:, T:T + 1], wb(n), ALU.mult, ALU.mult), s_("h_ready"))
                    if moe_l is not None and T + 2 < NT:
                        combine(moe_l, T + 2)
                    if n in (0, 2) and T >= 1:
                        lo_tiles(("hT", n, T - 1), T - 1)
                if n in (0, 2):
                    lo_tiles(("hT", n, 3), 3)

            def lo_tiles(name, T):
                for g in range(2):
                    nm = name + (g,)
                    dve.wait_ge(s_("hT_hi_made"), hT_hi_count(nm))
                    D.read(tt(HTL[:, 4 * g:4 * g + 4, cols(T)], v3(tile(nm), 4), HTH[:, 4 * g:4 * g + 4, cols(T)].bitcast(F32),
                              ALU.subtract), nm)

            def gate_inputs():
                tile_is_ready(dve, "ba_tok")
                D.read(dve.tensor_copy(ba, v3(tile("ba_tok")[:, 0:32], 4)), "ba_tok")
                D(tt(v3(zsp, 4), ba[:, :, 4:8], bc_m(dtb), ALU.add))
                D(ts(spt, zsp, -1.0, None, ALU.mult))
                D(tt(esp, zsp, spt, ALU.max))
                D(dve.tensor_copy(v3(beta, 4), ba[:, :, 0:4]), s_("z_ready"))

            def gates():
                dve.wait_ge(s_("gate_exp"), 3)
                D(ts(spt, esp, 1.0, None, ALU.add), s_("sp_ready"))
                D(ts(beta, beta, 0.5, 0.5, ALU.mult, ALU.add))
                dve.wait_ge(s_("gate_exp"), 4)
                D(stt(spt, zsp, 0.0, spt, ALU.max, ALU.add))
                D(stt(v3(gg, 4), v3(spt, 4), -1.0, bc_m(alog), ALU.mult, ALU.mult), s_("g_ready"))
                tile_is_ready(dve, "gc")
                D.read(dve.tensor_copy(gc, tile("gc")[:, 0:16]), "gc")
                dve.wait_ge(s_("egc_ready"), 1)
                D(tt(bege, beta, egc, ALU.mult))

            def tok(nm, T):
                if nm == "v":
                    return
                tile_is_read(dve, ("tok", nm, T))
                n = 4 * (nm == "k") + T
                D(dve.tensor_reduce(ssn[:, 4 * n:4 * n + 4], v3(sqt[:, n % 2, :], 4), AX.X, ALU.add), s_("sq_reduced"))

            def l2():
                for T in range(NT):
                    dve.wait_ge(s_("l2_r"), T + 1)
                    D(tt(v3(Y0[:, T, 0:512], 4), v3(Y0[:, T, 0:512], 4), bc_h(rn[:, 4 * T:4 * T + 4]), ALU.mult), s_("q_normed"))

            def gdn_decay(T):
                q = T % 2
                h4 = slice(4 * T, 4 * T + 4)
                gb = tile(("Gb", T))
                tile_is_ready(dve, ("Gb", T))
                D(tt(v3(PA[1][:, q, :], 4), v3(gb, 4), bc_h(gc[:, h4]), ALU.subtract))
                D(ts(PA[0][:, q, :], PA[1][:, q, :], 0.0, None, ALU.max))
                D(ts(PA[1][:, q, :], PA[1][:, q, :], 0.0, None, ALU.min), s_("g_args"))
                D(tt(kde[0:64, h4], v3(gb, 4)[0:64, :, 63], gc[0:64, h4], ALU.subtract))
                D(tt(kde[64:128, h4], v3(gb, 4)[64:128, :, 127], gc[64:128, h4], ALU.subtract), s_("kd_args"))
                dve.wait_ge(s_("decays"), T + 1)
                D(tt(v3(PA[0][:, q, :], 4), v3(PA[0][:, q, :], 4), bc_h(beta[:, h4]), ALU.mult))
                tile_is_ready(dve, ("KK", T))
                D.read(tt(PA[3][:, q, :], tile(("KK", T)), PA[0][:, q, :], ALU.mult), ("KK", T))
                D(tt(v3(PA[0][:, q, :], 4), v3(PA[3][:, q, :], 4), bc_m(m16[:, :]), ALU.mult), s_("m16_ready"))
                D(tt(v3(PA[3][:, q, :], 4), v3(PA[3][:, q, :], 4), bc_m(moff[:, :]), ALU.mult))
                dve.wait_ge(s_("more_decays"), T + 1)
                D(tt(v3(PA[1][:, q, :], 4), v3(PA[1][:, q, :], 4), bc_m(U[:, :]), ALU.mult))
                tile_is_ready(dve, ("KQ", T))
                D.read(tt(AT0[:, T, :], tile(("KQ", T)), PA[1][:, q, :], ALU.mult), ("KQ", T))
                for c in range(2):
                    D(dve.tensor_copy(egl[:, 2 * T + c, :], v3(PA[2][:, q, :], 4)[:, :, 64 * c + 63]))
                D(tt(QF[:, :, cols(T)], QF[:, :, cols(T)], v3(PA[2][:, q, :], 4), ALU.mult))
                D(tt(v3(PA[7][:, q, :], 4), bc_m(ident[:, :]), v3(PA[0][:, q, :], 4), ALU.subtract))

            def gdn_x1(T):
                q = T % 2
                h4 = slice(4 * T, 4 * T + 4)
                tile_is_read(dve, ("DT", T))
                D(tt(v3(PA[8][:, q, :], 4), bc_m(ident[:, :]), v3(PA[4][:, q, :], 4), ALU.subtract), s_("x1_ready"))
                D(tt(v3(PA[9][:, q, :], 4), v3(VT[:, T, :], 4), bc_h(beta[:, h4]), ALU.mult))
                D(tt(v3(PA[10][:, q, :], 4), v3(KT[:, T, :], 4), bc_h(bege[:, h4]), ALU.mult))
                D(tt(v3(KT[:, T, :], 4), v3(KT[:, T, :], 4), bc_h(kde[:, h4]), ALU.mult), s_("vk_ready"))

            def gdn_inverse(pr):
                Ts = (2 * pr, 2 * pr + 1)
                for r in (1, 2, 3):
                    for T in Ts:
                        q = T % 2
                        tile_is_ready(dve, ("XT", r, T))
                        D.read(tt(PA[7][:, q, :], PA[7][:, q, :], tile(("X", r, T)), ALU.add), ("X", r, T))
                        D.read(tt(PA[8][:, q, :], PA[8][:, q, :], tile(("XT", r, T)), ALU.add), ("XT", r, T))
                for T in Ts:
                    tile_is_read(dve, ("BT", T))
                    D(tt(v3(PA[0][:, T % 2, :], 4), bc_m(ident[:, :]), v3(PA[6][:, T % 2, :], 4), ALU.subtract), s_("n1_ready"))
                for T in Ts:
                    tile_is_ready(dve, ("N2", T))
                    D.read(tt(PA[1][:, T % 2, :], PA[0][:, T % 2, :], tile(("N2", T)), ALU.add), ("N2", T))

            def scan(c):
                T, r = c // 2, slice(64 * (c % 2), 64 * (c % 2) + 64)
                tile_is_read(dve, ("u", T))
                tile_is_ready(dve, ("sv", c))
                D.read(tt(vnew[r, :], VT[r, T, :], tile(("sv", c))[r, :], ALU.subtract), ("sv", c))
                D(tt(v3(Stmp[:, :], 4), v3(S[:, :], 4), bc_h(egl[:, c, :]), ALU.mult))
                tile_is_ready(dve, ("ss", c))
                D.read(tt(S[:, :], Stmp[:, :], tile(("ss", c)), ALU.add), ("ss", c))
                if c == NC - 1:
                    D(dve.memset(S[:, :], 0.0), s_("scan_done"))

            def onorm(w, Ts):
                for T in Ts:
                    dve.wait_ge(s_("o_sq"), 4 * w + T + 1)
                    D(dve.tensor_reduce(oss[:, 4 * T:4 * T + 4], v3(onsq[:, T % 2, :], 4), AX.X, ALU.add), s_("sq_reduced"))
                a_, b_ = 4 * Ts[0], 4 * Ts[-1] + 4
                D(ts(oss[:, a_:b_], oss[:, a_:b_], 1.0 / DK, EPS, ALU.mult, ALU.add), s_("o_ms"))

            def oscale(w, Ts):
                dve.wait_ge(s_("o_r"), onorm_count(w, Ts))
                for T in Ts:
                    y = v3(Y0[:, T, 512 * w:512 * w + 512], 4)
                    D(tt(y, y, bc_h(ors[:, 4 * T:4 * T + 4]), ALU.mult))

            HBf = HB.rearrange("p h t -> p (h t)")
            HQf = HQ.rearrange("p h t -> p (h t)")
            HKf = HK.rearrange("p h t -> p (h t)")

            def halves(ap, s):
                return ap.rearrange("p (b s) -> p b s", s=2 * s)

            def level_args(n):
                if n == len(LEVELS):
                    b = halves(HBf, CH // 2)
                    D(tt(halves(LE, CH // 2), b[:, :, CH - 1:CH].broadcast_to([P, 2048 // CH, CH]), b, ALU.subtract), s_("lv_args"))
                    return
                s = LEVELS[n]
                b, e = halves(HBf, s), halves(LE, s)
                ref = b[:, :, s - 1:s].broadcast_to([P, 2048 // (2 * s), s])
                D(tt(e[:, :, 0:s], ref, b[:, :, 0:s], ALU.subtract))
                D(tt(e[:, :, s:2 * s], b[:, :, s:2 * s], ref, ALU.subtract), s_("lv_args"))

            def hgrn(step):
                if step[0] == "hdiag":
                    level_args(0)
                    for T in range(NT):
                        tile_is_ready(dve, ("dg", T))
                        D.read(tt(v3(HAT[:, T, :], 4), v3(tile(("dg", T)), 4), bc_m(ident[:, :]), ALU.mult), ("dg", T))
                elif step[0] == "hlevel":
                    n = step[1]
                    s = LEVELS[n]
                    e, p_ = halves(LE, s), halves(LP[n % 2], s)
                    dve.wait_ge(s_("lv_exp"), n + 1)
                    D(tt(p_[:, :, 0:s], halves(HKf, s)[:, :, 0:s], e[:, :, 0:s], ALU.mult))
                    D(tt(p_[:, :, s:2 * s], halves(HQf, s)[:, :, s:2 * s], e[:, :, s:2 * s], ALU.mult), s_("lp_ready"))
                    level_args(n + 1)
                    for T in range(NT):
                        tile_is_ready(dve, ("lv", n, T))
                        D.read(dve.copy_predicated(v3(HAT[:, T, :], 4), bc_m(lvmask[:, n, :]), v3(tile(("lv", n, T)), 4)), ("lv", n, T))
                elif step[0] == "hstate":
                    dve.wait_ge(s_("lv_exp"), len(LEVELS) + 1)
                    D(tt(HKf, HKf, LE, ALU.mult), s_("hk_decayed"))
                    dve.wait_ge(s_("lv_exp"), len(LEVELS) + 2)
                    D(tt(HQf, HQf, LE, ALU.mult), s_("hq_decayed"))

            def hscan(c):
                D(tt(v3(Stmp[:, :], 4), v3(S[:, :], 4), bc_h(v3(LE, 4)[:, :, CH * c + CH - 1]), ALU.mult))
                tile_is_ready(dve, ("hs", c))
                D.read(tt(S[:, :], Stmp[:, :], tile(("hs", c)), ALU.add), ("hs", c))

            def dense_read_by_act(db, t):
                dve.wait_ge(dense_read["act"], evac_count(db, t))

            def fcum(t):
                dve.wait_ge(s_("lf_ready"), t + 1)
                D(dve.tensor_tensor_scan(HB[:, t, :], resetm[:, :], HQ[:, t, :], 0.0, ALU.mult, ALU.add), s_("b_ready"))

            def evac(db, ts_=tuple(range(4))):
                kind, which, c0 = BLOCKS[db]
                if which in ("q", "k", "v") :
                    dst = {"q": QF, "k": KF, "v": VF}[which]
                    for t in range(4):
                        g = 4 * db + t
                        w = [vec[:, 12 * j + g:12 * j + g + 1] for j in range(4)]
                        c, o = craw[:, t % 2, :], dst[:, t, :]
                        dense_read_by_act(db, t)
                        for j in (2, 1):
                            d = 3 - j
                            D(stt(o[:, d:SEQ], c[:, 0:SEQ - d], w[j], o[:, d:SEQ], ALU.mult, ALU.add))
                        D(stt(o[:, 3:SEQ], c[:, 0:SEQ - 3], w[0], o[:, 3:SEQ], ALU.mult, ALU.add), s_("conv_done"))
                elif which == "hf":
                    for t in range(4):
                        dense_read_by_act(db, t)
                        D(ts(HB[:, t, :], HK[:, t, :], c1[:, t:t + 1], c2[:, t:t + 1], ALU.mult, ALU.add), s_("f_ready"))
                        D(ts(HK[:, t, :], HB[:, t, :], -1.0, 1.0, ALU.mult, ALU.add))
                elif which in ("z", "hg"):
                    wgt = gnw if which == "z" else hnw
                    w = int(which == "hg")
                    for t in ts_:
                        dense_read_by_act(db, t)
                        z = zt[:, t % 2, :]
                        y = Y0[:, t, 512 * w:512 * w + 512]
                        D(tt(v3(z, 4), v3(z, 4), bc_m(wgt[:, :]), ALU.mult))
                        D(tt(y, y, z, ALU.mult), s_("z_used"))
                elif kind == "odd_in" and which[0] in ("rq", "rk"):
                    dst = RQ if which[0] == "rq" else RK
                    dve.wait_ge(s_("ret_consts"), 48)
                    for hh in range(2):
                        dense_read_by_act(db, 2 * hh + 1)
                        D(tt(dst[:, hh, 0, :], rtmp[:, 0, :], cos_t, ALU.mult))
                        D(tt(rprod, rtmp[:, 1, :], sin_t, ALU.mult))
                        D(tt(dst[:, hh, 0, :], dst[:, hh, 0, :], rprod, ALU.subtract))
                        D(tt(dst[:, hh, 1, :], rtmp[:, 0, :], sin_t, ALU.mult))
                        D(tt(rprod, rtmp[:, 1, :], cos_t, ALU.mult), s_("rot_done"))
                        D(tt(dst[:, hh, 1, :], dst[:, hh, 1, :], rprod, ALU.add), s_("rot_ready"))
                elif kind == "odd_in" and which[0] == "rg":
                    h = which[1]
                    dve.wait_ge(s_("ro_r"), h + 1)
                    for t in range(4):
                        dense_read_by_act(db, t)
                        y = Y1[:, t, h * RDV:(h + 1) * RDV]
                        D(stt(y, y, ors[:, t:t + 1], gt[:, t % 2, :], ALU.mult, ALU.mult))
                        D(tt(y, y, rnw, ALU.mult), s_("g_used"))
                elif kind.endswith("out"):
                    for t in range(4):
                        dve.wait_ge(dense_ready, 4 * db + t + 1)
                        x = X[:, t, c0:c0 + 512]
                        D(tt(x, x, ps[:, t, :], ALU.add), dense_read["dve"])

            def score(h):
                dve.wait_ge(s_("dh_loaded"), 16 * (h + 1))
                if h > 0:
                    tile_is_ready(dve, ("ro", h - 1, NT - 1))
                for J in range(NT):
                    n = SEQ - P * J
                    tile_is_ready(dve, ("sc", h, J))
                    D.read(tt(RAT[:, J, 0:n], tile(("sc", h, J))[:, 0:n], DH[:, 0:n], ALU.mult), ("sc", h, J))

            def ro(h):
                tile_is_read(dve, ("ro", h, NT - 1))
                D(ts(oss[:, 0:4], oss[:, 0:4], 1.0 / RDV, EPS, ALU.mult, ALU.add), s_("ro_ms"))

            def pick_first(dst, eq):
                D(tt(eq, eq, bc_m(first4), ALU.mult))
                D(dve.tensor_reduce(mx2, eq, AX.X, ALU.max))
                D(tt(dst, eq, bc_h(mx2, 4), ALU.is_equal))

            def route(l):
                D(dve.memset(ar[:, 7168:9216], 0.0), s_("xg_cleared"))
                dve.wait_ge(s_("router_loaded"), 128 * (l + 1))
                D(dve.memset(ones, 1.0))
                D(dve.memset(ahead[:, 0, :], 0.0))
                D(dve.memset(onesrow, 1.0))
                D(dve.memset(any80[:, 64:80], 0.0))
                dve.wait_ge(s_("r_logits"), l + 1)
                D(ts(lgT, ps[0:20, 3, :], lgb, None, ALU.add), s_("r_lgT"))
                dve.wait_ge(s_("r_lg"), l + 1)
                D(dve.tensor_copy(lg, v3(ps[:, 7, 0:80], 4)))
                c, f = lg[:, :, 0:4], lg[:, :, 4:20]
                D(dve.tensor_reduce(mx, c, AX.X, ALU.max))
                D(tt(r_b, c, bc_h(mx, 4), ALU.is_equal))
                D(tt(r_a, c, bc_h(mx, 4), ALU.subtract), s_("r_cexp"))
                pick_first(gm, r_b)
                D(tt(r_c, f.rearrange("p T (g e) -> p T g e", g=4), gm.unsqueeze(3).broadcast_to([P, 4, 4, 4]), ALU.mult))
                D(dve.tensor_reduce(fs, r_c.rearrange("p T g e -> p T e g"), AX.X, ALU.add))
                D(dve.tensor_reduce(mx, fs, AX.X, ALU.max))
                D(tt(r_b, fs, bc_h(mx, 4), ALU.is_equal))
                pick_first(m1, r_b)
                D(stt(fs, m1, -1e30, fs, ALU.mult, ALU.add))
                D(dve.tensor_reduce(ed, fs, AX.X, ALU.max))
                D(tt(r_b, fs, bc_h(ed, 4), ALU.is_equal))
                pick_first(m2, r_b)
                D(tt(ed, ed, mx, ALU.subtract), s_("r_eexp"))
                for n, m in enumerate((m1, m2)):
                    D(tt(oh[n].rearrange("p T (g e) -> p T g e", g=4), gm.unsqueeze(3).broadcast_to([P, 4, 4, 4]),
                         m.unsqueeze(2).broadcast_to([P, 4, 4, 4]), ALU.mult))
                D(tt(anyh, oh[0], oh[1], ALU.add))
                D(dve.tensor_copy(ahead[:, 1, :], anyh[:, 0, :]))
                D(tt(ahead[:, 2, :], ahead[:, 1, :], anyh[:, 1, :], ALU.add))
                D(tt(ahead[:, 3, :], ahead[:, 2, :], anyh[:, 2, :], ALU.add))
                D(tt(ahead80[:, 64:80], ahead[:, 3, :], anyh[:, 3, :], ALU.add), s_("r_any"))
                dve.wait_ge(s_("r_exp"), 2 * l + 2)
                D(dve.tensor_reduce(gp, r_a, AX.X, ALU.add))
                D(ts(mx, ed, 1.0, None, ALU.add))
                D(tt(gp, gp, mx, ALU.mult))
                w = v3(w12, 4)
                D(dve.reciprocal(w[:, :, 0], gp))
                D(tt(w[:, :, 1], w[:, :, 0], ed, ALU.mult))
                dve.wait_ge(s_("r_pos"), l + 1)
                D(dve.tensor_copy(slotv, v3(ps[:, 7, 0:64], 4)))
                D(dve.tensor_copy(ncnt, ps[:, 7, 64:80]))
                D(ts(ovc, ncnt, 128.0, None, ALU.is_gt))
                D(stt(ovc, ncnt, 256.0, ovc, ALU.is_gt, ALU.add))
                D(stt(ovc, ncnt, 384.0, ovc, ALU.is_gt, ALU.add))
                D(dve.tensor_tensor_scan(ovi, onesrow, ovc, 0.0, ALU.mult, ALU.add))
                D(tt(ovt, ovi, ovc, ALU.subtract))
                D(ts(ovt, ovt, 128.0, 128.0 * NE - 128.0, ALU.mult, ALU.add))
                D(tt(ovt, ovt, offs16, ALU.subtract))
                D(ts(tmp64, slotv, 128.0, None, ALU.is_ge))
                D(tt(tmp64, tmp64, bc_m(ovt), ALU.mult))
                D(tt(slotv, slotv, tmp64, ALU.add))
                D(tt(slotv, slotv, bc_m(offs16), ALU.add))
                for n in range(2):
                    D(tt(tmp64, oh[n], slotv, ALU.mult))
                    D(dve.tensor_reduce(v3(slotf, 4)[:, :, n], tmp64, AX.X, ALU.add))
                D(dve.tensor_copy(slots_u, slotf))
                D(ts(sA_i, slots_u, 7, None, ALU.logical_shift_right))
                D(ts(sB_i, slots_u, P - 1, None, ALU.bitwise_and))
                D(dve.tensor_copy(slotA, sA_i))
                D(dve.tensor_copy(slotB, sB_i))
                D(tt(hotB, iotaB.unsqueeze(1).broadcast_to([P, 8, P]), slotB.unsqueeze(2).broadcast_to([P, 8, P]), ALU.is_equal))
                D(tt(hotA, iotaA.unsqueeze(1).broadcast_to([P, 8, SLOT_TILES]), slotA.unsqueeze(2).broadcast_to([P, 8, SLOT_TILES]), ALU.is_equal))
                D(tt(hotA, hotA, tokv.unsqueeze(2).broadcast_to([P, 8, SLOT_TILES]), ALU.mult), s_("r_hot"))
                D(tt(v3(cmp7, 7), bc_m(ovi, 7), iota8[:, 0:7].unsqueeze(2).broadcast_to([P, 7, 16]), ALU.is_le))
                D(dve.tensor_reduce(eidf[:, 0:7], v3(cmp7, 7), AX.X, ALU.add))
                D(ts(eidf[:, 0:7], eidf[:, 0:7], float(NE - 1), None, ALU.min))
                D(dve.tensor_copy(eidf[:, 7:8], ovi[:, 15:16]))
                D(dve.tensor_copy(eid[:, :], eidf[0:1, :]), s_("slots_known"))
                dve.wait_ge(s_("r_rows"), l + 1)
                D(ts(idx[:, 1, :], ps[:, 7, 0:SLOT_TILES], EMPTY, None, ALU.add))
                D(ts(idx[:, 0, :], idx[:, 1, :], 1, None, ALU.logical_shift_right), s_("rows_known"))

            def xT_lo(l, e, par):
                for g in range(2):
                    dve.wait_ge(s_("xT_hi"), e * 2 + (32 * l + g + 1))
                    tt(HTL[:, 2 * par + g, :], ps[:, 4 + g, :], HTH[:, 2 * par + g, :].bitcast(F32), ALU.subtract).then_inc(s_("xT_lo"), 1)

            def moe(l):
                m = MOE_PIECE[l]
                route(l)

                def lo_in(n, it=0):
                    dve.wait_ge(hi_done, it * 12 + (n + 1))
                    tt(wl[:, n % NSPL, :, :], raw_at(in_turn(n, it)), wh[:, n % NSPL, :, :].bitcast(F32),
                       ALU.subtract).then_inc(lo_dve, 1)

                def gated(E, par):
                    dve.wait_ge(s_("silu_done"), E + 1)
                    tt(aact[:, par, :], sg[:, par, :], ps[:, par, FE:2 * FE], ALU.mult).then_inc(s_("act_done"), 1)

                xT_lo(l, 0, 0)
                lo_in(m + 4)
                lo_in(m + 5)
                xT_lo(l, 1, 1)
                lo_in(m + 6)
                gated(16 * l, 0)

                def expert(it, par):
                    E = it * 2 + (16 * l + par)
                    b = m + 4 + 6 * par
                    last = isinstance(it, int) and it == NE // 2 - 1
                    dve.wait_ge(s_("aT_hi"), E + 1)
                    tt(HTL[:, 4 + par, 0:256], ps[:, 6, 0:256], HTH[:, 4 + par, 0:256].bitcast(F32), ALU.subtract)\
                        .then_inc(s_("aT_lo"), 1)
                    if not last or par == 0:
                        for j in (3, 4, 5, 6):
                            lo_in(b + j, it)
                        gated(E + 1, 1 - par)
                        lo_in(b + 7, it)
                        if not last:
                            xT_lo(l, it * 2 + (par + 2), par)
                            lo_in(b + 8, it)

                for n in range(4):
                    expert(*divmod(n, 2))
                with dve.Fori(2, NE // 2 - 1) as it:
                    for par in range(2):
                        expert(it, par)
                for par in range(2):
                    expert(NE // 2 - 1, par)
                n = overflow_flag(dve, l)
                with dve.If(n > 0):
                    with dve.Fori(0, 7) as j:
                        dve.wait_ge(s_(f"ov_silu{l}"), j + 1)
                        tt(aact[:, 0, :], sg[:, 0, :], ps[:, 0, FE:2 * FE], ALU.mult).then_inc(s_(f"ov_act{l}"), 1)
            for sm, n in ((s_("act_done"), 2), (s_("xT_lo"), 2), (s_("aT_lo"), 1), (lo_dve, 4)):
                for _ in range(n):
                    dve.nop().then_inc(sm, 1)
            for step in SCHEDULE:
                k = step[0]
                if k == "consts":
                    consts()
                elif k == "norm":
                    norm(step[1])
                elif k == "ba":
                    tile_is_ready(dve, "ba")
                    D.read(dve.tensor_copy(baT, tile("ba")[0:8, :]), "ba")
                elif k == "ba_tok":
                    gate_inputs()
                elif k == "gates":
                    gates()
                elif k == "tok":
                    tok(step[1], step[2])
                elif k == "l2":
                    l2()
                elif k == "gdn_decay":
                    gdn_decay(step[1])
                elif k == "gdn_x1":
                    gdn_x1(step[1])
                elif k == "gdn_inverse":
                    gdn_inverse(step[1])
                elif k == "fcum":
                    fcum(step[1])
                elif k == "evac_gate":
                    evac(step[1], (step[2],))
                elif k == "scan":
                    scan(step[1])
                elif k == "onorm":
                    onorm(*step[1:])
                elif k == "oscale":
                    oscale(*step[1:])
                elif k in ("hdiag", "hlevel", "hstate"):
                    hgrn(step)
                elif k == "hscan":
                    hscan(step[1])
                elif k == "evac":
                    evac(step[1])
                elif k == "yT":
                    for T in step[3]:
                        lo_tiles(("yT", step[1], step[2], T), T)
                elif k == "score":
                    score(step[1])
                elif k == "ro":
                    ro(step[1])
                elif k == "moe":
                    moe(step[1])

        @block.tensor
        def _(pe):
            mm = nc.tensor.matmul
            tr = nc.tensor.transpose

            def open_tile(name):
                n = SIDE_AT[name]
                if n >= 4:
                    tile_is_read(pe, SIDE[n - 4][0])
                return tile(name)

            def done(ins):
                ins.then_inc(tile_ready, 1)

            def four(name, f):
                t = open_tile(name)
                for h in range(NH):
                    ins = f(t[:, cols(h)], h)
                done(ins)

            def norm(n):
                for T in range(NT):
                    if n == 2 and T >= 2:
                        rows(MOE_AT[0], T - 2)
                    pe.wait_ge(s_("h_ready"), 4 * n + T + 1)
                    for g in range(2):
                        t = open_tile(("hT", n, T, g))
                        for j in range(4):
                            k = 4 * g + j
                            ins = tr(t[:, cols(j)], htok(n)[:, T % 2, k:DM:KD], ident[:, :])
                        done(ins)
                    if n in (1, 3) and T % 2 == 1:
                        c = slice(P * (T - 1), P * (T + 1))
                        tile_is_read(pe, ("hT", n, T, 1))
                        if T == 1:
                            pe.wait_ge(s_("router_loaded"), 64 * (n + 1))
                            pe.wait_ge(*x_ready(n, NT - 1))
                        for k in range(KD):
                            ins = mm(ps[0:20, 3, c], rw[:, k, :], hTf[:, k, c], start=k == 0, stop=k == KD - 1)
                        if T == NT - 1:
                            ins.then_inc(s_("r_logits"), 1)

                if n == 2:
                    rows(MOE_AT[0], 2)
                    rows(MOE_AT[0], 3)

            def yT(l, kh, Ts):
                for T in Ts:
                    if l == 0:
                        pe.wait_ge(s_("z_used"), 4 + T + 1)
                    else:
                        pe.wait_ge(s_("g_used"), 4 * (2 * kh + 1) + T + 1)
                    for g in range(2):
                        t = open_tile(("yT", l, kh, T, g))
                        for j in range(4):
                            c = (4 * g + j) * P
                            src = Y0[:, T, c:c + P] if l == 0 else Y1[:, T, kh * DM + c:kh * DM + c + P]
                            ins = tr(t[:, cols(j)], src, ident[:, :])
                        done(ins)

            def ba_product():
                pe.wait_ge(s_("wba_lo"), 1)
                t = open_tile("ba")
                for k in range(KD):
                    ins = mm3(t[0:8, :], wba_h[:, k, :], wba_l[:, k, :], HTH[:, k, :], HTL[:, k, :], k == 0, k == KD - 1)
                done(ins)

            def ba_by_token():
                tile_is_read(pe, "ba")
                t = open_tile("ba_tok")
                for T in range(NT):
                    ins = tr(t[:, 8 * T:8 * T + 8], baT[:, cols(T)], ident[0:8, 0:8])
                done(ins)

            def hT_ready(db, t=NT - 1):
                last = {0: ("hT", 0), 8: ("yT", 0, 0), 10: ("hT", 2), 22: ("yT", 1, 0), 24: ("yT", 1, 1)}.get(db)
                if last:
                    tile_is_read(pe, last + (t, 1))

            def rows(db, t):
                hT_ready(db, t)
                pe.wait_ge(dense_read[evac_engine(db - 1)], evac_count(db - 1, t))
                for kp in range(4):
                    i = first_piece(db) + kp
                    if t == 0:
                        pe.wait_ge(hi_done, i + 1)
                        wait_lo(pe, i)
                    for k2 in range(2):
                        k = 2 * kp + k2
                        ins = mm3(ps[:, t, :], HTH[:, k, cols(t)], HTL[:, k, cols(t)], wh[:, i % NSPL, k2, :], wl[:, i % NSPL, k2, :],
                                  k == 0, k == KD - 1)
                    if t == NT - 1 and kp < 3:
                        ins.then_inc(piece_used, 1)
                ins.then_inc(dense_ready, 1)

            def piece(db, kp):
                i = first_piece(db) + kp
                sl = i % NSPL
                kind, which, _c = BLOCKS[db]
                if kp == 0:
                    hT_ready(db)
                pe.wait_ge(hi_done, i + 1)
                wait_lo(pe, i)
                feature = which in ("q", "k", "v", "hf", "hq") or (kind == "odd_in" and which[0] in ("rq", "rk"))
                for t in range(NT):
                    if kp == 0 and db > 0:
                        pe.wait_ge(dense_read[evac_engine(db - 1)], evac_count(db - 1, t))
                    for k2 in range(2):
                        k = 2 * kp + k2
                        first, last = kp == 0 and k2 == 0, kp == 3 and k2 == 1
                        if feature:
                            c = cols(t) if kind == "even_in" else slice(256 * (t // 2) + t % 2, 256 * (t // 2 + 1), 2)
                            ins = mm3(ps[:, t, :], wh[:, sl, k2, c], wl[:, sl, k2, c], HTH[:, k, :], HTL[:, k, :], first, last)
                        else:
                            ins = mm3(ps[:, t, :], HTH[:, k, cols(t)], HTL[:, k, cols(t)], wh[:, sl, k2, :], wl[:, sl, k2, :], first, last)
                    if kp == 3:
                        ins.then_inc(dense_ready, 1)
                if kp < 3:
                    ins.then_inc(piece_used, 1)

            def tok(nm, T):
                src, n = {"q": (QF, 4), "k": (KF, 8), "v": (VF, 12)}[nm]
                pe.wait_ge(s_("conv_silu"), n)
                four(("tok", nm, T), lambda o, h: tr(o, src[:, h, cols(T)], ident[:, :]))

            def gates():
                pe.wait_ge(s_("g_ready"), 1)
                done(mm(open_tile("gc")[:, 0:16], U[:, :], gg, start=True, stop=True))

            def l2():
                for T in range(NT):
                    pe.wait_ge(s_("q_normed"), T + 1)
                    four(("qb", T), lambda o, h: tr(o, Y0[:, T, cols(h)], ident[:, :]))
                    pe.wait_ge(s_("k_normed"), T + 1)
                    four(("kb", T), lambda o, h: tr(o, KT[:, T, cols(h)], ident[:, :]))

            def gdn_decay(T):
                tile_is_read(pe, ("qb", T))
                tile_is_read(pe, ("kb", T))
                four(("Gb", T), lambda o, h: mm(o, gg[:, 4 * T + h:4 * T + h + 1].broadcast_to([P, P]), U[:, :], start=True, stop=True))
                four(("KK", T), lambda o, h: mm(o, KF[:, h, cols(T)], KF[:, h, cols(T)], start=True, stop=True))
                four(("KQ", T), lambda o, h: mm(o, KF[:, h, cols(T)], QF[:, h, cols(T)], start=True, stop=True))

            def gdn_x1(T):
                pe.wait_ge(s_("m16_ready"), T + 1)
                four(("DT", T), lambda o, h: tr(o, PA[0][:, T % 2, cols(h)], ident[:, :]))

            def gdn_inverse(pr):
                Ts = (2 * pr, 2 * pr + 1)

                def prod(name, T, lh, rh):
                    q = T % 2
                    four(name, lambda o, h: mm(o, PA[lh][:, q, cols(h)], PA[rh][:, q, cols(h)], start=True, stop=True))

                for T in Ts:
                    tile_is_read(pe, ("DT", T))
                    prod(("P2", T), T, 4, 0)
                    prod(("P2T", T), T, 0, 4)
                for r in (1, 2, 3):
                    for T in Ts:
                        if r == 1:
                            pe.wait_ge(s_("x1_ready"), T + 1)
                            tile_is_read(pe, ("P2T", T))
                        else:
                            tile_is_read(pe, ("XT", r - 1, T))
                            tile_is_read(pe, ("P", 1, T) if r == 2 else ("PT", 2, T))
                        prod(("X", r, T), T, 6, 7)
                        prod(("XT", r, T), T, 7, 6)
                        if r < 3:
                            prod(("PT", r, T), T, 5, 6)
                        if r == 1:
                            prod(("P", r, T), T, 6, 5)
                for T in Ts:
                    tile_is_read(pe, ("XT", 3, T))
                    prod(("B", T), T, 8, 3)
                    prod(("BT", T), T, 3, 8)
                for T in Ts:
                    tile_is_read(pe, ("BT", T))
                    prod(("B2", T), T, 6, 5)
                for T in Ts:
                    tile_is_read(pe, ("B2", T))
                    pe.wait_ge(s_("n1_ready"), T + 1)
                    prod(("N2", T), T, 4, 0)
                for T in Ts:
                    tile_is_read(pe, ("N2", T))
                    prod(("IT", T), T, 7, 1)
                for T in Ts:
                    tile_is_read(pe, ("IT", T))
                    pe.wait_ge(s_("vk_ready"), T + 1)
                    prod(("u", T), T, 8, 9)
                    prod(("wT", T), T, 10, 8)

            def scan(c):
                T, p0 = c // 2, 64 * (c % 2)
                r, tc = slice(p0, p0 + 64), slice(P * T + p0, P * T + p0 + 64)
                tile_is_read(pe, ("wT", T))
                pe.wait_ge(s_("vk_ready"), NT)
                if c > 0:
                    tile_is_read(pe, ("ss", c - 1))
                t = open_tile(("sv", c))
                for h in range(NH):
                    ins = mm(t[r, cols(h)], KF[:, h, tc], S[:, cols(h)], start=True, stop=True)
                done(ins)
                t = open_tile(("so", c))
                for h in range(NH):
                    mm(t[r, cols(h)], QF[:, h, tc], S[:, cols(h)], start=h == 0, stop=False)
                tile_is_read(pe, ("sv", c))
                for h in range(NH):
                    ins = mm(t[r, cols(h)], AT0[r, T, P * h + p0:P * h + p0 + 64], vnew[r, cols(h)], start=False, stop=h == NH - 1)
                done(ins)
                t = open_tile(("ss", c))
                for h in range(NH):
                    ins = mm(t[:, cols(h)], KT[r, T, cols(h)], vnew[r, cols(h)], start=True, stop=True)
                done(ins)

            def hgrn(step):
                if step[0] == "hdiag":
                    pe.wait_ge(dense_read["act"], evac_count(4, 3))
                    pe.wait_ge(s_("b_ready"), 4)
                    for T in range(NT):
                        four(("dg", T), lambda o, h: mm(o, HK[:, h, cols(T)], HQ[:, h, cols(T)], start=True, stop=True))
                elif step[0] == "hlevel":
                    pe.wait_ge(s_("lp_ready"), step[1] + 1)
                    lp = v3(LP[step[1] % 2], 4)
                    for T in range(NT):
                        four(("lv", step[1], T), lambda o, h: mm(o, lp[:, h, cols(T)], lp[:, h, cols(T)], start=True, stop=True))
                elif step[0] == "hstate":
                    pe.wait_ge(s_("hk_decayed"), 1)
                    for T in range(NT):
                        four(("kd", T), lambda o, h: tr(o, HK[:, h, cols(T)], ident[:, :]))

            def hscan(c):
                T, p0 = c // 2, 64 * (c % 2)
                r, tc = slice(p0, p0 + 64), slice(P * T + p0, P * T + p0 + 64)
                pe.wait_ge(s_("hq_decayed"), 1)
                pe.wait_ge(s_("scan_done"), 1)
                tile_is_read(pe, ("kd", T))
                t = open_tile(("ho", c))
                for h in range(NH):
                    mm(t[r, cols(h)], HAT[r, T, P * h + p0:P * h + p0 + 64], HI[r, T, cols(h)], start=h == 0, stop=False)
                if c > 0:
                    tile_is_read(pe, ("hs", c - 1))
                for h in range(NH):
                    ins = mm(t[r, cols(h)], HQ[:, h, tc], S[:, cols(h)], start=False, stop=h == NH - 1)
                done(ins)
                t = open_tile(("hs", c))
                for h in range(NH):
                    ins = mm(t[:, cols(h)], KDT[r, T, cols(h)], HI[r, T, cols(h)], start=True, stop=True)
                done(ins)

            def score(h):
                pe.wait_ge(s_("rot_ready"), 4 * (h // 2) + 3 + h % 2)
                for J in range(NT):
                    t = open_tile(("sc", h, J))
                    n = SEQ - P * J
                    mm(t[:, 0:n], RK[:, h % 2, 0, cols(J)], RQ[:, h % 2, 0, P * J:SEQ], start=True, stop=False)
                    done(mm(t[:, 0:n], RK[:, h % 2, 1, cols(J)], RQ[:, h % 2, 1, P * J:SEQ], start=False, stop=True))

            def ro(h):
                tile_is_read(pe, ("sc", h, NT - 1))
                pe.wait_ge(dense_read["act"], evac_count([b for b, x in enumerate(BLOCKS) if x[1] == ("rv", h)][0], 3))
                for T in range(NT):
                    t = open_tile(("ro", h, T))
                    for J in range(T + 1):
                        ins = mm(t, RAT[:, J, P * (T - J):P * (T - J) + P], RV[:, h % 2, J, :], start=J == 0, stop=J == T)
                    done(ins)

            def xT(l, e, par, loads):
                pe.wait_ge(s_(f"xg_loaded{par}"), loads)
                for g in range(2):
                    pe.wait_ge(s_("xT_lo"), e * 2 + (32 * l + g + 1))
                    for j in range(4):
                        ins = tr(ps[:, 4 + g, cols(j)], xg[:, par, 4 * g + j:DM:KD], ident[:, :])
                    ins.then_inc(s_("xT_ready"), 1)

            def moe(l):
                m = MOE_PIECE[l]
                for t in range(4):
                    tile_is_read(pe, SIDE[SIDE_AT[("hT", 2 * l + 1, NT - 1, 1)] - t][0])
                pe.wait_ge(s_("r_lgT"), l + 1)
                for T in range(NT):
                    ins = tr(ps[:, 7, 20 * T:20 * T + 20], lgT[:, cols(T)], ident[0:20, 0:20])
                ins.then_inc(s_("r_lg"), 1)
                pe.wait_ge(s_("r_any"), l + 1)
                mm(ps[:, 7, 0:80], Lst, any80, start=True, stop=False)
                ins = mm(ps[:, 7, 0:80], ones, ahead80, start=False, stop=True)
                ins.then_inc(s_("r_pos"), 1)
                pe.wait_ge(s_("r_hot"), l + 1)
                for n in range(8):
                    ins = mm(ps[:, 7, 0:SLOT_TILES], hotB[:, n, :], hotA[:, n, :], start=n == 0, stop=n == 7)
                ins.then_inc(s_("r_rows"), 1)

                def split_ready(n, it):
                    pe.wait_ge(hi_done, it * 12 + (n + 1))
                    if n < m + 4:
                        pe.wait_ge(lo_pool, lo_count(n))
                    else:
                        pe.wait_ge(lo_dve, it * 12 + lo_count(n))
                    return n % NSPL

                def gate_up(par, j, n, it=0):
                    sl = split_ready(n, it)
                    for k2 in range(2):
                        k = 2 * j + k2
                        a_ = 2 * par + k // 4
                        ins = mm3(ps[:, par, :], HTH[:, a_, cols(k % 4)], HTL[:, a_, cols(k % 4)], wh[:, sl, k2, :], wl[:, sl, k2, :],
                                  k == 0, k == KD - 1)
                    ins.then_inc(s_("moe_used"), 1)

                base = 144 * l + 16
                xT(l, 0, 0, base)
                pe.wait_ge(s_("act_done"), 16 * l + 1)
                pe.wait_ge(s_("xT_lo"), 32 * l + 4)
                gate_up(0, 0, m)
                gate_up(0, 1, m + 1)
                xT(l, 1, 1, base)
                gate_up(0, 2, m + 2)
                gate_up(0, 3, m + 3)

                def expert(it, par):
                    E = it * 2 + (16 * l + par)
                    b = m + 4 + 6 * par
                    last = isinstance(it, int)
                    pe.wait_ge(s_("act_done"), E + 3)
                    pe.wait_ge(s_("aT_lo"), E + 1)
                    for k in range(2):
                        ins = tr(ps[:, 6, cols(k)], aact[:, par, cols(k)], ident[:, :])
                    ins.then_inc(s_("aT_ready"), 1)
                    n0 = 0
                    if not last or par == 0:
                        n0 = 4
                        pe.wait_ge(s_("xT_lo"), it * 4 + (32 * l + 2 * par + 6))
                        for j in range(4):
                            gate_up(1 - par, j, b + j, it)
                        if not last:
                            xT(l, it * 2 + (par + 2), par, it * 16 + (base + 16))
                    pe.wait_ge(s_("aT_lo"), E + 2)
                    for hf in range(2):
                        sl = split_ready(b + n0 + hf, it)
                        pe.wait_ge(s_("y_read"), E * 2 + (hf + 1))
                        for k in range(2):
                            ins = mm3(ps[:, 2 + hf, :], HTH[:, 4 + par, cols(k)], HTL[:, 4 + par, cols(k)], wh[:, sl, k, :], wl[:, sl, k, :],
                                      k == 0, k == 1)
                        ins.then_inc(s_("moe_used"), 1)

                with pe.Fori(0, NE // 2 - 1) as it:
                    for par in range(2):
                        expert(it, par)
                for par in range(2):
                    expert(NE // 2 - 1, par)
                pe.wait_ge(s_("y_read"), 32 * (l + 1) + 2)
                n = overflow_flag(pe, l)
                with pe.If(n > 0):
                    pe.wait_ge(s_("xT_lo"), 32 * (l + 1) + 2)
                    with pe.Fori(0, 7) as j:
                        pe.wait_ge(s_(f"ov_x{l}"), j * 16 + 16)
                        pe.wait_ge(s_(f"ov_w{l}"), j * 32 + 32)
                        for g in range(2):
                            for q in range(4):
                                ins = tr(ps[:, 4 + g, cols(q)], xg[:, 0, 4 * g + q:DM:KD], ident[:, :])
                            ins.then_inc(s_(f"ov_xT{l}"), 1)
                        pe.wait_ge(s_(f"ov_xTr{l}"), j * 2 + 2)
                        for k in range(KD):
                            ins = mm(ps[:, 0, :], hTf[:, k, 0:P], ovWg[:, k, :], start=k == 0, stop=k == KD - 1)
                        ins.then_inc(s_(f"ov_gu{l}"), 1)
                        pe.wait_ge(s_(f"ov_act{l}"), j + 1)
                        for k in range(2):
                            ins = tr(ps[:, 6, cols(k)], aact[:, 0, cols(k)], ident[:, :])
                        ins.then_inc(s_(f"ov_aT{l}"), 1)
                        pe.wait_ge(s_(f"ov_aTr{l}"), j + 1)
                        for hf in range(2):
                            for k in range(2):
                                ins = mm(ps[:, 2 + hf, :], hTf[:, k, P:2 * P], ovWd[:, k, 512 * hf:512 * hf + 512], start=k == 0, stop=k == 1)
                            ins.then_inc(s_(f"ov_yp{l}"), 1)

            pe.wait_ge(s_("ident_loaded"), 16)
            for step in SCHEDULE:
                k = step[0]
                if k == "consts":
                    pe.wait_ge(s_("consts_loaded"), 16 * 12)
                    done(tr(open_tile("vec")[:, 0:60], raw_vec[0:60, :], ident[0:60, 0:60]))
                elif k == "norm" and step[1] < 4:
                    norm(step[1])
                elif k == "ba":
                    ba_product()
                elif k == "ba_tok":
                    ba_by_token()
                elif k == "rows":
                    if step[1] != MOE_AT[0]:
                        rows(step[1], step[2])
                elif k == "piece":
                    piece(step[1], step[2])
                elif k == "tok":
                    tok(step[1], step[2])
                elif k == "gates":
                    gates()
                elif k == "l2":
                    l2()
                elif k == "gdn_decay":
                    gdn_decay(step[1])
                elif k == "gdn_x1":
                    gdn_x1(step[1])
                elif k == "gdn_inverse":
                    gdn_inverse(step[1])
                elif k == "scan":
                    scan(step[1])
                elif k in ("hdiag", "hlevel", "hstate"):
                    hgrn(step)
                elif k == "hscan":
                    hscan(step[1])
                elif k == "yT":
                    yT(*step[1:])
                elif k == "score":
                    score(step[1])
                elif k == "ro":
                    ro(step[1])
                elif k == "moe":
                    moe(step[1])


def shape_constants():
    i = np.arange(P)
    same = i[:, None] // CH == i[None, :] // CH
    c = {"c_ident": np.eye(P), "c_U": same & (i[:, None] <= i[None, :])}
    b16 = i[:, None] // 16 == i[None, :] // 16
    c["c_m16"] = b16 & (i[:, None] > i[None, :])
    c["c_moff"] = same & ~b16 & (i[:, None] > i[None, :])
    c["c_Lst"] = i[:, None] < i[None, :]
    c["c_reset"] = np.broadcast_to(np.arange(SEQ) % CH != 0, (P, SEQ))
    T, j = np.arange(NT), np.arange(2)
    c["c_tok"] = (2 * (P * T[None, :, None] + i[:, None, None]) + j[None, None, :]).reshape(P, 8) - EMPTY
    c["c_first"] = np.broadcast_to(np.array([4, 3, 2, 1]), (P, 4))
    c["c_iota"] = np.broadcast_to(np.concatenate([np.arange(8), P * np.arange(NE), np.arange(SLOT_TILES), i]), (P, 24 + SLOT_TILES + P))
    f = np.float32
    inv = f(1.0) / (f(10000.0) ** np.linspace(0.0, 1.0, RDK // 2, dtype=f))
    ang = (np.arange(SEQ, dtype=f)[None, :] * inv.astype(f)[:, None]).astype(f).astype(np.float64)
    c["c_cos"], c["c_sin"] = np.cos(ang), np.sin(ang)
    lg = np.log(1.0 - 2.0 ** (-5.0 - np.arange(NH)))
    rel = np.arange(SEQ)[None, :] - i[:, None]
    c["c_decay"] = np.where(rel >= 0, np.exp(np.maximum(rel, 0) * lg[:, None, None]), 0.0) * RDK ** -0.5
    c = {k: np.ascontiguousarray(v, dtype=np.float32) for k, v in c.items()}
    lv = [(i[:, None] // (2 * s) == i[None, :] // (2 * s)) & (i[:, None] % (2 * s) < s) & (i[None, :] % (2 * s) >= s) for s in LEVELS]
    c["c_lv"] = np.ascontiguousarray(np.stack(lv, 1), dtype=np.float32)
    return c


_INS = ['x', 'norm_mix_w', 'norm_ffn_w', 'even_w_in', 'gdn_conv_w', 'gdn_a_log', 'gdn_dt_bias', 'gdn_norm_w', 'hgrn_lb_logits',
        'hgrn_norm_w', 'even_w_out', 'odd_w_in', 'ret_norm_w', 'odd_w_out', 'router_c_w', 'router_c_b', 'router_f_w',
        'router_f_b', 'moe_w_gate_up', 'moe_w_down', 'final_norm_w']


def kernel(**inputs):
    import concourse.bacc as _bacc
    from concourse.bass_utils import run_bass_kernel_spmd as _run

    nc = _bacc.Bacc("TRN2", target_bir_lowering=False, num_devices=1)
    arrays, aps = {}, {}
    for name, v in [(n, inputs[n]) for n in _INS] + sorted(shape_constants().items()):
        v = np.ascontiguousarray(v)
        arrays[f"in_{name}_dram"] = v
        aps[name] = nc.dram_tensor(f"in_{name}_dram", v.shape, mybir.dt.from_np(v.dtype), kind="ExternalInput").ap()
    out = nc.dram_tensor("out_0_dram", (1, SEQ, DM), F32, kind="ExternalOutput").ap()
    build(nc, aps, out)
    r = _run(nc, [arrays], core_ids=[0])
    return r.results[0]["out_0_dram"]
```
